# Optimizing a Trainium2 kernel written in Bass

```python
import math
import jax, jax.numpy as jnp
from jax import lax
import numpy as np

D_MODEL = 1024
BATCH = 1
SEQ = 512
DEPTH = 1

N_META = 16
MLA_HEADS = 8
QK_NOPE_DIM = 128
QK_ROPE_DIM = 64
V_HEAD_DIM = 128
Q_LORA_RANK = 384
KV_LORA_RANK = 256
ROPE_THETA = 10000.0
Q_BLOCK = 128
SOFTMAX_SCALE = (QK_NOPE_DIM + QK_ROPE_DIM) ** -0.5
D_ATTN = MLA_HEADS * V_HEAD_DIM
SSM_HEADS = 16
SSM_HEAD_DIM = 64
SSM_GROUPS = 2
HEADS_PER_GROUP = SSM_HEADS // SSM_GROUPS
SSM_STATE = 128
SSM_CONV = 4
CHUNK = 128
D_SSM = SSM_HEADS * SSM_HEAD_DIM
D_XBC = D_SSM + 2 * SSM_GROUPS * SSM_STATE
D_MIX = D_ATTN + D_SSM
D_FF = 2816
FFN_CONV = 3
EPS = 1e-6
IN_SPLITS = (Q_LORA_RANK, KV_LORA_RANK, QK_ROPE_DIM, D_SSM, D_XBC, SSM_HEADS)
D_IN = sum(IN_SPLITS)

kernel_name = 'hymba_mla_ssd_convffn_layer'

def rms_norm(x, gain):
    xf = x.astype(jnp.float32)
    y = xf * lax.rsqrt(jnp.mean(xf * xf, axis=-1, keepdims=True) + EPS)
    return (y * gain.astype(jnp.float32)).astype(x.dtype)

def causal_dwconv(x, w, b):
    k = w.shape[0]
    y = lax.conv_general_dilated(x, w[:, None, :].astype(x.dtype), window_strides=(1,),
                                 padding=[(k - 1, 0)], dimension_numbers=('NWC', 'WIO', 'NWC'),
                                 feature_group_count=x.shape[-1])
    return y + b.astype(x.dtype)

def split_cols(t, sizes):
    idx = np.cumsum(sizes)[:-1].tolist()
    return jnp.split(t, idx, axis=-1)

def rope_tables(n):
    inv = ROPE_THETA ** (-jnp.arange(0, QK_ROPE_DIM, 2, dtype=jnp.float32) / QK_ROPE_DIM)
    ang = jnp.arange(n, dtype=jnp.float32)[:, None] * inv[None, :]
    return jnp.cos(ang), jnp.sin(ang)

def apply_rope(x, cos, sin):
    x1, x2 = jnp.split(x, 2, axis=-1)
    cos = cos.astype(x.dtype)
    sin = sin.astype(x.dtype)
    return jnp.concatenate([x1 * cos - x2 * sin, x1 * sin + x2 * cos], axis=-1)

def attend_block(q_nope, q_pe, q_pos, k_nope, k_pe, v, k_pos):
    s = jnp.einsum('bqhd,bkhd->bhqk', q_nope, k_nope) + jnp.einsum('bqhr,bkr->bhqk', q_pe, k_pe)
    s = s.astype(jnp.float32) * SOFTMAX_SCALE
    s = jnp.where(k_pos[None, :] <= q_pos[:, None], s, -jnp.inf)
    p = jax.nn.softmax(s, axis=-1).astype(v.dtype)
    return jnp.einsum('bhqk,bkhd->bqhd', p, v)

def mla_group(q_c, kv_c, k_pe_raw, q_a_norm, w_uq, kv_a_norm, w_ukv, cos, sin):
    bsz, L = q_c.shape[0], q_c.shape[1]
    S = L - N_META
    q = jnp.einsum('blr,rhd->blhd', rms_norm(q_c, q_a_norm), w_uq)
    q_nope = q[..., :QK_NOPE_DIM]
    q_pe = apply_rope(q[..., QK_NOPE_DIM:], cos[:, None, :], sin[:, None, :])
    kv = jnp.einsum('blc,chd->blhd', rms_norm(kv_c, kv_a_norm), w_ukv)
    k_nope, v = kv[..., :QK_NOPE_DIM], kv[..., QK_NOPE_DIM:]
    k_pe = apply_rope(k_pe_raw, cos, sin)
    pos = jnp.arange(L)
    o_meta = attend_block(q_nope[:, :N_META], q_pe[:, :N_META], pos[:N_META],
                          k_nope[:, :N_META], k_pe[:, :N_META], v[:, :N_META], pos[:N_META])
    nb = S // Q_BLOCK

    def to_blocks(t):
        t = t[:, N_META:].reshape((bsz, nb, Q_BLOCK) + t.shape[2:])
        return jnp.moveaxis(t, 1, 0)

    o_real = lax.map(lambda blk: attend_block(blk[0], blk[1], blk[2], k_nope, k_pe, v, pos),
                     (to_blocks(q_nope), to_blocks(q_pe), pos[N_META:].reshape(nb, Q_BLOCK)))
    o_real = jnp.moveaxis(o_real, 0, 1).reshape(bsz, S, MLA_HEADS, V_HEAD_DIM)
    o = jnp.concatenate([o_meta, o_real], axis=1)
    return o.reshape(bsz, L, D_ATTN)

def ssd_chunks(xs, dt, A, Bm, Cm, init):
    Acs = jnp.cumsum(dt * A, axis=2)
    Q = xs.shape[2]
    causal = jnp.tril(jnp.ones((Q, Q), dtype=bool))[:, :, None, None]
    seg = Acs[:, :, :, None] - Acs[:, :, None, :]
    decay_in = jnp.exp(jnp.where(causal, seg, -jnp.inf))
    xdt = xs * dt[..., None]
    cb = jnp.einsum('bclgn,bcsgn->bclsg', Cm, Bm)
    y_diag = jnp.einsum('bclsgh,bcsghp->bclghp', cb[..., None] * decay_in, xdt)
    decay_to_end = jnp.exp(Acs[:, :, -1:] - Acs)
    states = jnp.einsum('bcsgn,bcsghp->bcghpn', Bm, xdt * decay_to_end[..., None])
    chunk_decay = jnp.exp(Acs[:, :, -1])

    def step(carry, inp):
        st, dec = inp
        return carry * dec[..., None, None] + st, carry

    final, prev = lax.scan(step, init, (jnp.moveaxis(states, 1, 0), jnp.moveaxis(chunk_decay, 1, 0)))
    prev = jnp.moveaxis(prev, 0, 1)
    y_off = jnp.einsum('bclgn,bcghpn->bclghp', Cm, prev) * jnp.exp(Acs)[..., None]
    return y_diag + y_off, final

def ssd_group(z, xbc, dt_raw, conv_w, conv_b, dt_bias, A_log, D, norm_gain):
    bsz, L = z.shape[0], z.shape[1]
    S = L - N_META
    nc = S // CHUNK
    f32 = jnp.float32
    xbc = jax.nn.silu(causal_dwconv(xbc, conv_w, conv_b)).astype(f32)
    xs, Bm, Cm = split_cols(xbc, (D_SSM, SSM_GROUPS * SSM_STATE, SSM_GROUPS * SSM_STATE))
    xs = xs.reshape(bsz, L, SSM_GROUPS, HEADS_PER_GROUP, SSM_HEAD_DIM)
    Bm = Bm.reshape(bsz, L, SSM_GROUPS, SSM_STATE)
    Cm = Cm.reshape(bsz, L, SSM_GROUPS, SSM_STATE)
    dt = jax.nn.softplus(dt_raw.astype(f32) + dt_bias.astype(f32)).reshape(bsz, L, SSM_GROUPS, HEADS_PER_GROUP)
    A = -jnp.exp(A_log.astype(f32)).reshape(SSM_GROUPS, HEADS_PER_GROUP)

    def meta_part(t):
        return t[:, None, :N_META]

    def real_part(t):
        return t[:, N_META:].reshape((bsz, nc, CHUNK) + t.shape[2:])

    init = jnp.zeros((bsz, SSM_GROUPS, HEADS_PER_GROUP, SSM_HEAD_DIM, SSM_STATE), f32)
    y_meta, h_meta = ssd_chunks(meta_part(xs), meta_part(dt), A, meta_part(Bm), meta_part(Cm), init)
    y_real, _ = ssd_chunks(real_part(xs), real_part(dt), A, real_part(Bm), real_part(Cm), h_meta)
    y = jnp.concatenate([y_meta.reshape(bsz, N_META, SSM_GROUPS, HEADS_PER_GROUP, SSM_HEAD_DIM),
                         y_real.reshape(bsz, S, SSM_GROUPS, HEADS_PER_GROUP, SSM_HEAD_DIM)], axis=1)
    y = y + D.astype(f32).reshape(SSM_GROUPS, HEADS_PER_GROUP)[..., None] * xs
    gsz = HEADS_PER_GROUP * SSM_HEAD_DIM
    y = y.reshape(bsz, L, SSM_GROUPS, gsz) * jax.nn.silu(z.astype(f32)).reshape(bsz, L, SSM_GROUPS, gsz)
    y = y * lax.rsqrt(jnp.mean(y * y, axis=-1, keepdims=True) + EPS)
    return (y.reshape(bsz, L, D_SSM) * norm_gain.astype(f32)).astype(z.dtype)

def conv_ffn(h, w_up, conv_w, conv_b, w_down):
    u = causal_dwconv(h @ w_up, conv_w, conv_b)
    g, v = jnp.split(u, 2, axis=-1)
    return (jax.nn.silu(g) * v) @ w_down

def setup_inputs(seed: int = 0) -> dict:
    key = jax.random.key(seed)
    ks = jax.random.split(key, 26)
    f32 = jnp.float32

    def nrm(k, shape, scale):
        return scale * jax.random.normal(k, shape, f32)

    def gain(k, n):
        return 1.0 + 0.05 * jax.random.normal(k, (DEPTH, n), f32)

    dt0 = jnp.exp(jax.random.uniform(ks[17], (DEPTH, SSM_HEADS), f32, math.log(1e-3), math.log(1e-1)))
    return {
        'x': nrm(ks[0], (BATCH, SEQ, D_MODEL), 1.0),
        'meta_tokens': nrm(ks[1], (N_META, D_MODEL), 1.0),
        'norm_mix_pre': gain(ks[2], D_MODEL),
        'norm_mix_post': gain(ks[3], D_MODEL),
        'norm_ffn_pre': gain(ks[4], D_MODEL),
        'norm_ffn_post': gain(ks[5], D_MODEL),
        'w_in': nrm(ks[6], (DEPTH, D_MODEL, D_IN), D_MODEL ** -0.5),
        'q_a_norm': gain(ks[7], Q_LORA_RANK),
        'w_uq': nrm(ks[8], (DEPTH, Q_LORA_RANK, MLA_HEADS, QK_NOPE_DIM + QK_ROPE_DIM), Q_LORA_RANK ** -0.5),
        'kv_a_norm': gain(ks[9], KV_LORA_RANK),
        'w_ukv': nrm(ks[10], (DEPTH, KV_LORA_RANK, MLA_HEADS, QK_NOPE_DIM + V_HEAD_DIM), KV_LORA_RANK ** -0.5),
        'attn_out_norm': gain(ks[11], D_ATTN),
        'ssm_conv_w': nrm(ks[12], (DEPTH, SSM_CONV, D_XBC), SSM_CONV ** -0.5),
        'ssm_conv_b': nrm(ks[13], (DEPTH, D_XBC), 0.02),
        'ssm_dt_bias': dt0 + jnp.log(-jnp.expm1(-dt0)),
        'ssm_A_log': jnp.log(jax.random.uniform(ks[14], (DEPTH, SSM_HEADS), f32, 1.0, 16.0)),
        'ssm_D': 1.0 + 0.1 * jax.random.normal(ks[15], (DEPTH, SSM_HEADS), f32),
        'ssm_norm': gain(ks[16], D_SSM),
        'w_out': nrm(ks[18], (DEPTH, D_MIX, D_MODEL), D_MIX ** -0.5),
        'w_up': nrm(ks[19], (DEPTH, D_MODEL, 2 * D_FF), D_MODEL ** -0.5),
        'ffn_conv_w': nrm(ks[20], (DEPTH, FFN_CONV, 2 * D_FF), FFN_CONV ** -0.5),
        'ffn_conv_b': nrm(ks[21], (DEPTH, 2 * D_FF), 0.02),
        'w_down': nrm(ks[22], (DEPTH, D_FF, D_MODEL), D_FF ** -0.5),
    }

def reference(x, meta_tokens, norm_mix_pre, norm_mix_post, norm_ffn_pre, norm_ffn_post, w_in,
              q_a_norm, w_uq, kv_a_norm, w_ukv, attn_out_norm, ssm_conv_w, ssm_conv_b, ssm_dt_bias,
              ssm_A_log, ssm_D, ssm_norm, w_out, w_up, ffn_conv_w, ffn_conv_b, w_down):
    bsz = x.shape[0]
    L = N_META + x.shape[1]
    meta = jnp.broadcast_to(meta_tokens[None].astype(x.dtype), (bsz, N_META, D_MODEL))
    h = jnp.concatenate([meta, x], axis=1)
    cos, sin = rope_tables(L)
    for l in range(DEPTH):
        hn = rms_norm(h, norm_mix_pre[l])
        q_c, kv_c, k_pe, z, xbc, dt_raw = split_cols(hn @ w_in[l], IN_SPLITS)
        attn = mla_group(q_c, kv_c, k_pe, q_a_norm[l], w_uq[l], kv_a_norm[l], w_ukv[l], cos, sin)
        ssm = ssd_group(z, xbc, dt_raw, ssm_conv_w[l], ssm_conv_b[l], ssm_dt_bias[l], ssm_A_log[l],
                        ssm_D[l], ssm_norm[l])
        mix = jnp.concatenate([rms_norm(attn, attn_out_norm[l]), ssm], axis=-1) @ w_out[l]
        h = h + rms_norm(mix, norm_mix_post[l])
        hn = rms_norm(h, norm_ffn_pre[l])
        h = h + rms_norm(conv_ffn(hn, w_up[l], ffn_conv_w[l], ffn_conv_b[l], w_down[l]), norm_ffn_post[l])
    return h[:, N_META:]


_drawn_inputs = setup_inputs


def setup_inputs(seed=0):
    import zlib

    import numpy as np

    out = dict(_drawn_inputs(seed))
    spreads = {}
    factors = {'ssm_conv_b': 3.247, 'ffn_conv_b': 3.312}
    for name, (base, spread) in spreads.items():
        noise = np.random.default_rng([zlib.crc32(name.encode()), seed]).standard_normal(out[name].shape)
        drawn = base * np.exp(spread * noise) if base else spread * noise
        out[name] = __import__('jax').numpy.asarray(drawn.astype(out[name].dtype))
    for name, factor in factors.items():
        out[name] = (out[name] * factor).astype(out[name].dtype)
    return out
```

```python
from contextlib import ExitStack, contextmanager

import concourse.bass as bass
from concourse import mybir

F32 = mybir.dt.float32
F32R = mybir.dt.float32r
BF16 = mybir.dt.bfloat16
ALU = mybir.AluOpType
ACT = mybir.ActivationFunctionType
AX = mybir.AxisListType

P = 128
BANK = 512


class Chain:

    def __init__(self, engine, sem):
        self.engine, self.sem, self.base, self.steps = engine, sem, None, 0

    def add(self, ins):
        ins.then_inc(self.sem, 1)
        self.steps += 1
        return ins

    def wait(self):
        self.engine.wait_ge(self.sem, self.steps if self.base is None else self.base + self.steps)

    @contextmanager
    def loop(self, i, trips, per):
        before = self.steps
        self.base, self.steps = i * per, before
        yield
        assert self.steps - before == per, (self.steps - before, per)
        self.base, self.steps = None, before + per * trips


def hymba_layer(nc, x, meta_tokens, norm_mix_pre, norm_mix_post, norm_ffn_pre, norm_ffn_post, w_in,
                q_a_norm, w_uq, kv_a_norm, w_ukv, attn_out_norm, ssm_conv_w, ssm_conv_b, ssm_dt_bias,
                ssm_A_log, ssm_D, ssm_norm, w_out, w_up, ffn_conv_w, ffn_conv_b, w_down,
                rope_cos, rope_sin, out):
    SEQ, D = x.shape[1], x.shape[2]
    META = meta_tokens.shape[0]
    TOK = META + SEQ
    HALF = TOK // 2
    NT = SEQ // P
    KD = D // P
    D_IN = w_in.shape[2]
    R_Q, HEADS = w_uq.shape[1], w_uq.shape[2]
    R_KV = w_ukv.shape[1]
    KQ, KKV = R_Q // P, R_KV // P
    NOPE = 128
    ROPE = w_uq.shape[3] - NOPE
    DV = w_ukv.shape[3] - NOPE
    SCALE = float(NOPE + ROPE) ** -0.5
    SH = ssm_A_log.shape[1]
    D_SSM = ssm_norm.shape[1]
    SP = D_SSM // SH
    TAPS = ssm_conv_w.shape[1]
    D_XBC = ssm_conv_w.shape[2]
    STATE = 128
    GROUPS = (D_XBC - D_SSM) // 2 // STATE
    HG = SH // GROUPS
    GC = HG * SP
    CT = D_XBC // P
    XT = D_SSM // P
    D_FF = w_down.shape[1]
    KF = D_FF // P
    FTAPS = ffn_conv_w.shape[1]
    EPS = 1e-6
    NEG = -1e30
    assert (META, NT, KD, KQ, KKV, CT, KF, ROPE) == (16, 4, 8, 3, 2, 12, 22, 64)

    SLOT = 9 * P
    C_Z = 6
    C_XBC = C_Z + D_SSM // P
    C_ATT = C_XBC + CT
    PAIRS = HEADS // 2
    C_OUT = C_ATT + 2 * PAIRS
    C_UP = C_OUT + 2 * KD
    C_DOWN = C_UP + 2 * KF
    C_END = C_DOWN + KF

    def tcol(t):
        return slice(0, META) if t == 0 else slice(META + P * (t - 1), META + P * t)

    def rows(t):
        return META if t == 0 else P

    NF = SEQ + 4
    F0 = TOK - NF
    FH = (slice(F0, F0 + NF // 2), slice(F0 + NF // 2, TOK))
    WH = (slice(0, HALF), slice(HALF, TOK))

    wi = w_in[0].rearrange("(k p) n -> p k n", p=P)
    wq = w_uq[0].rearrange("(k p) h d -> p k h d", p=P)
    wkv = w_ukv[0].rearrange("(k p) h d -> p k h d", p=P)
    wo = w_out[0].rearrange("(k p) n -> p k n", p=P)
    wu = w_up[0].rearrange("(k p) n -> p k n", p=P)

    with ExitStack() as ctx:
        def sem(name):
            return ctx.enter_context(nc.semaphore(name))

        top = [(nc.sbuf_base + 63) // 64 * 64]

        def fixed(name, shape, dt):
            n = 4 if dt != BF16 else 2
            for s in shape[1:]:
                n *= s
            t = nc.alloc_sbuf_tensor_at(name, shape, dt, offset=top[0])
            top[0] += (n + 63) // 64 * 64
            return t

        wf = [fixed(f"weights_f32_{s}", [P, SLOT], F32) for s in range(2)]
        whi = [fixed(f"weights_hi_{s}", [P, SLOT], F32R) for s in range(2)]
        wlo = [fixed(f"weights_lo_{s}", [P, SLOT], F32R) for s in range(2)]
        h_tm = fixed("h_tm", [P, NT + 1, D], F32)
        ident = fixed("ident", [P, P], F32)
        ident_bf = fixed("ident_bf", [P, P], BF16)
        mask_bf = fixed("mask_bf", [P, P], BF16)
        swap = fixed("swap", [P, P], F32)
        dup = fixed("dup", [ROPE, P], F32)
        dupswap = fixed("dupswap", [ROPE, P], F32)
        ones = fixed("ones", [P, P], F32)
        PARTS3 = 96
        pick = fixed("pick", [PARTS3, SH], BF16)
        vec_rows = fixed("vec_rows", [P, 3, P], F32)
        vec = fixed("vec", [P, 3, 96], F32)
        gain_a = fixed("gain_a", [P, D], F32)
        gain_b = fixed("gain_b", [P, D], F32)
        skip_d = fixed("skip_d", [P, SH], F32)
        dt_small = fixed("dt_small", [SH, 4], F32)
        stat = fixed("stat", [P, 96], F32)
        xn = [fixed(f"normed_{i}", [P, D], F32) for i in range(2)]
        dt_ends = fixed("dt_ends", [SH, NT + 1], F32)
        dtw = fixed("dt_weights", [P, KD, SH], F32)
        sm = fixed("ssm_rows", [P, TOK], F32)
        pool = top[0]
        spare = nc.sbuf_usable_end - pool

        def at(name, shape, dt, off):
            n = 4 if dt != BF16 else 2
            for s in shape[1:]:
                n *= s
            assert off + n <= spare, (name, off + n, spare)
            return nc.alloc_sbuf_tensor_at(name, shape, dt, offset=pool + off)

        TB = 4 * TOK
        AB = 4 * (NT + 1) * D
        O_QKV = (XT + CT) * TB
        O_W = O_QKV + 10 * TB
        z_silu = at("z_silu", [P, XT, TOK], F32, 0)
        xbc = at("xbc", [P, CT, TOK], F32, XT * TB)
        qkv_hi = at("qkv_hi", [P, KQ + KKV, TOK], F32R, O_QKV)
        qkv_lo = at("qkv_lo", [P, KQ + KKV, TOK], F32R, O_QKV + 5 * TB)
        hn_hi = at("hn_hi", [P, KD, TOK], F32R, O_W)
        hn_lo = at("hn_lo", [P, KD, TOK], F32R, O_W + 8 * TB)
        qkvk = at("qkvk", [P, C_Z, TOK], F32, O_W + 16 * TB)
        squares = at("squares", [P, KQ + KKV, TOK], F32, O_W + 22 * TB)
        XPAD = TAPS - 1
        xpad = [at(f"xpad_{i}", [P, XPAD + TOK + 1], F32, O_W + 27 * TB + i * (TB + 32)) for i in range(2)]
        o = O_W + 29 * TB + 64
        conv = [at(f"conv_{i}", [P, TOK], F32, o + i * TB) for i in range(2)]
        rstd_f = at("rstd_f", [P, 2, TOK], F32, o + 2 * TB)
        attn = at("attn", [P, NT + 1, D], F32, O_W)
        o = O_W + AB
        O_MIXA = o
        PTB = 4 * (NT + 1) * P
        pt_hi = [at(f"pt_hi_{i}", [P, NT + 1, P], F32R, o + i * PTB) for i in range(2)]
        pt_lo = [at(f"pt_lo_{i}", [P, NT + 1, P], F32R, o + (2 + i) * PTB) for i in range(2)]
        o += 4 * PTB
        probs = [at(f"probs_{i}", [P, TOK], F32, o + i * TB) for i in range(2)]
        qn_hi = [at(f"qn_hi_{i}", [P, TOK], F32R, o + (2 + i) * TB) for i in range(2)]
        qn_lo = [at(f"qn_lo_{i}", [P, TOK], F32R, o + (4 + i) * TB) for i in range(2)]
        kn_hi = [at(f"kn_hi_{i}", [P, TOK], F32R, o + (6 + i) * TB) for i in range(2)]
        o += 8 * TB
        kpe_hi = at("kpe_hi", [P, TOK], F32R, o)
        kpe_lo = at("kpe_lo", [P, TOK], F32R, o + TB)
        kn_lo = [at(f"kn_lo_{i}", [P, TOK], F32R, o + (2 + i) * TB) for i in range(2)]
        qpe_hi = at("qpe_hi", [P, TOK], F32R, o + 4 * TB)
        qpe_lo = at("qpe_lo", [P, TOK], F32R, o + 5 * TB)
        o += 6 * TB
        v_parts = at("v_parts", [P, NT + 1, 2, 2, DV], F32R, o)
        o += 8 * (NT + 1) * 2 * DV
        cos_t = at("cos_t", [P, TOK], F32, o)
        sin_t = at("sin_t", [P, TOK], F32, o + TB)
        mixa_hi = at("mixa_hi", [P, KD, TOK], F32R, O_MIXA)
        mixa_lo = at("mixa_lo", [P, KD, TOK], F32R, O_MIXA + 8 * TB)
        gated = at("gated", [P, XT, TOK], F32, O_QKV)
        plan = [O_QKV + 8 * TB]

        def ssm(name, shape, dt=F32):
            n = 4
            for s in shape[1:]:
                n *= s
            if plan[0] < O_MIXA < plan[0] + n:
                plan[0] = O_MIXA + 16 * TB
            t = at(name, shape, dt, plan[0])
            plan[0] += (n + 31) // 32 * 32
            return t

        xbc_c = ssm("xbc_chunk", [P, CT, P])
        decay = ssm("decay", [P, SH, P])
        xdt = ssm("xdt", [P, D_SSM])
        xdte = ssm("xdte", [P, D_SSM])
        b_c = ssm("b_chunk", [P, GROUPS * STATE])
        y_tm = ssm("y_tm", [P, D_SSM])
        state = ssm("state", [P, D_SSM])
        smt = ssm("ssm_cols", [P, NT + 1, P])
        smt_c = ssm("smt_chunk", [P, P])
        minus_acs = ssm("minus_acs", [P, SH])
        acs_rest = [ssm(f"acs_rest_{j}", [SH, TOK]) for j in range(3)]
        acs3 = ssm("acs_parts", [P, TOK], BF16)
        ends = ssm("chunk_ends", [SH, NT + 1, SH])
        dec_b = ssm("chunk_decay", [P, NT + 1, SH])
        gsq = at("gated_squares", [P, XT, TOK], F32, O_MIXA + 16 * TB)
        mixs_hi = at("mixs_hi", [P, KD, TOK], F32R, 0)
        mixs_lo = at("mixs_lo", [P, KD, TOK], F32R, 8 * TB)
        rstd_g = at("rstd_g", [P, GROUPS, TOK], F32, 16 * TB)
        normed_g = [at(f"normed_g_{i}", [P, TOK], F32, (18 + i) * TB) for i in range(2)]
        post = [at(f"post_{i}", [P, D], F32, (16 + 2 * i) * TB) for i in range(2)]
        mixo = at("mixo", [P, KD, TOK], F32, 28 * TB)
        hn2_hi = at("hn2_hi", [P, KD, TOK], F32R, 40 * TB)
        hn2_lo = at("hn2_lo", [P, KD, TOK], F32R, 48 * TB)
        act = at("act", [P, KF, SEQ], F32, 0)
        o = 22 * TB
        u_gate = at("u_gate", [P, NF], F32, o)
        u_value = at("u_value", [P, NF], F32, o + TB)
        c_gate = at("conv_gate", [P, SEQ], F32, o + 2 * TB)
        c_value = at("conv_value", [P, SEQ], F32, o + 3 * TB)
        o = 30 * TB
        st_hi = [at(f"act_hi_{i}", [P, SEQ], F32R, o + i * TB) for i in range(2)]
        st_lo = [at(f"act_lo_{i}", [P, SEQ], F32R, o + (2 + i) * TB) for i in range(2)]
        junk = at("junk", [P, D], F32, 34 * TB)
        y_out = [at(f"y_out_{i}", [P, D], F32, (36 + 2 * i) * TB) for i in range(2)]

        ps = ctx.enter_context(nc.psum_tensor("ps", [P, 8, BANK], F32))

        s_x = [sem(f"x_landed_{t}") for t in range(NT + 1)]
        s_land = [sem(f"weights_landed_{s}") for s in range(2)]
        s_gain_pre, s_gain_att, s_gain_post, s_gain_ffn, s_gain_last = (
            sem(f"gain_{n}_landed") for n in ("pre", "attn", "post", "ffn", "last"))
        s_vec, s_small, s_rope_tab = sem("vectors_landed"), sem("small_landed"), sem("rope_landed")
        s_const = sem("constants_ready")
        s_act, s_dve, s_pool = sem("scalar_steps"), sem("vector_steps"), sem("pool_steps")
        s_whi, s_wlo, s_pe = sem("weights_hi_ready"), sem("weights_lo_ready"), sem("chunk_multiplied")
        s_vt, s_vec_ready = sem("vectors_transposed"), sem("vectors_ready")

        class Norm:

            def __init__(self, name):
                self.rstd, self.xn, self.turned, self.hi, self.lo = (
                    sem(f"{name}_{n}") for n in ("rstd", "scaled", "turned", "hi", "lo"))

        pre, att, ffn = Norm("pre"), Norm("attn_norm"), Norm("ffn_norm")
        s_evac, s_sq, s_sumsq, s_rstdf = sem("qkvk_copied"), sem("squares_ready"), sem("sums_ready"), sem("rstd_f_ready")
        s_qkvn, s_qkvhi, s_qkvlo = sem("qkv_normed"), sem("qkv_hi_ready"), sem("qkv_lo_ready")
        s_xpad, s_conv, s_xbc = sem("xpad_filled"), sem("conv_done"), sem("xbc_ready")
        s_dtr, s_dtx, s_dtl, s_acs, s_exps = (
            sem(n) for n in ("dt_copied", "dt_biased", "dt_log_ready", "acs_ready", "acs_exps_ready"))
        s_sm, s_negA = sem("ssm_rows_ready"), sem("exp_A_ready")
        s_kpe, s_kper, s_kpehi, s_kpelo = (
            sem(n) for n in ("kpe_turned", "kpe_roped", "kpe_hi_ready", "kpe_lo_ready"))
        s_proj, s_rawcp, s_rope = sem("projections_done"), sem("rope_raw_copied"), sem("qpe_roped")
        s_phi, s_plo = sem("projections_hi"), sem("projections_lo")
        s_S, s_max, s_exp, s_T = sem("scores_ready"), sem("negmax_ready"), sem("probs_ready"), sem("probs_turned")
        s_pthi, s_ptlo, s_pv, s_attn = (
            sem(n) for n in ("probs_t_hi", "probs_t_lo", "pv_ready", "attn_stored"))
        s_smt, s_ends, s_dec, s_smt_ready, s_acs_copied, s_acs3 = (
            sem(n) for n in ("ssm_cols_turned", "ends_ready", "decay_summed", "ssm_cols_ready", "acs_copied",
                             "acs_parts_ready"))
        s_stage, s_xt, s_cb, s_ab, s_off, s_yd, s_st, s_yt = (
            sem(n) for n in ("chunk_staged", "xs_turned", "cb_ready", "acs_spread", "y_from_state",
                             "y_inside_ready",
                             "chunk_state_ready", "y_turned"))
        s_smtc, s_xs, s_xdt, s_xdte, s_xskip, s_yoff, s_ex, s_M = (
            sem(n) for n in ("chunk_cols_ready", "xs_copied", "xdt_ready", "xdte_ready", "xskip_ready",
                             "y_from_state_copied", "decays_ready", "mix_ready"))
        s_acs3_zero = sem("acs_parts_zeroed")
        s_y, s_state, s_gate = sem("y_ready"), sem("state_ready"), sem("gated_ready")
        s_gsq, s_gsum, s_rg, s_ng, s_mshi, s_mslo = (
            sem(n) for n in ("gated_squares", "gated_sums", "rstd_g", "normed_g", "mixs_hi_ready", "mixs_lo_ready"))
        s_mixo, s_t1, s_rpost, s_u, s_h = (
            sem(n) for n in ("mix_out_copied", "mix_out_turned", "post_rstd", "post_scaled", "residual_ready"))
        s_ug, s_uv, s_cg, s_cv, s_silu, s_actr = (
            sem(n) for n in ("u_gate_copied", "u_value_copied", "conv_gate_done", "conv_value_done", "silu_ready",
                             "act_ready"))
        s_sthi, s_stlo, s_down, s_rlast, s_ylast, s_yout = (
            sem(n) for n in ("act_hi_ready", "act_lo_ready", "down_ready", "last_rstd", "last_scaled", "y_ready_out"))
        s_out = [sem(f"out_written_{i}") for i in range(2)]

        V_QA, V_KVA, V_SN, V_CW, V_CB = 0, KQ, KQ + KKV, KQ + KKV + XT, KQ + KKV + XT + TAPS * CT
        NV0 = V_CB + CT
        CF = 2 * KF
        ST_PRE, ST_ATT, ST_POST, ST_FFN, ST_LAST, ST_NM, ST_DEN, ST_RDEN, ST_EPS = 0, 10, 20, 30, 40, 50, 60, 70, 95
        R_DT, R_ACS, R_DTE, R_EXP = 0, 32, 64, 96
        UNITS = 2 * (NT + 1)
        eps = stat[:, ST_EPS:ST_EPS + 1]

        PARTS = 4

        def landed(turn):
            return turn * (16 * PARTS) + 16 * PARTS

        def turned(b, w):
            return ps[:, 2 * b:2 * b + 2, :].rearrange("p a (k w) -> p (a k) w", w=P)[:, :, 0:w]

        def pair(b, w=HALF):
            return ps[:, 2 * b:2 * b + 2, 0:w]

        def two(ap):
            return ap.rearrange("p (a b) -> p a b", a=2)

        def by_head(ap):
            return ap.rearrange("p (t h d) -> p t h d", h=2, d=DV)

        def dt_cols(t):
            return t[:, 0:KD * P].rearrange("p (k n) -> p k n", k=KD)[:, :, ROPE:ROPE + SH]

        def bcast(ap, shape):
            return ap.unsqueeze(2).broadcast_to(shape)

        def score_cols(u):
            t = u % (NT + 1)
            return META + P * t

        def score_view(u):
            n, r = score_cols(u), rows(u % (NT + 1))
            b = 2 * (u % 2)
            return ps[0:r, b, 0:n] if n <= BANK else ps[0:r, b:b + 2, 0:n // 2]

        def prob_view(u):
            n, r = score_cols(u), rows(u % (NT + 1))
            v = probs[u % 2][0:r, 0:n]
            return v if n <= BANK else v.rearrange("p (a b) -> p a b", a=2)

        block = ctx.enter_context(nc.Block())

        @block.sync
        def _(sp):
            def load(slot, dst, src, chunk, n=1):
                if chunk is not None:
                    sp.wait_ge(s_wlo, chunk - 1)
                sp.dma_start(dst, src).then_inc(s_land[slot], 16 * PARTS // n)

            def blocks(slot, k=KD, w=P):
                return wf[slot][:, 0:k * w].rearrange("p (k n) -> p k n", k=k)

            sp.dma_start(h_tm[0:META, 0, :], meta_tokens).then_inc(s_x[0], 16)
            for t in range(1, NT + 1):
                sp.dma_start(h_tm[:, t, :], x[0, P * (t - 1):P * t, :]).then_inc(s_x[t], 16)
            for c in range(2):
                load(c, blocks(c), wi[:, :, P * c:P * (c + 1)], None)
            with sp.Fori(1, C_Z // 2) as i:
                for b in range(2):
                    load(b, blocks(b), wi[:, :, bass.ds(i * (2 * P) + b * P, P)], i * 2 + b)
            with sp.Fori(C_Z // 2, C_ATT // 2) as i:
                for b in range(2):
                    load(b, blocks(b), wi[:, :, bass.ds(i * (2 * P) + (b * P - (P - ROPE)), P)], i * 2 + b)
            with sp.Fori(0, PAIRS) as i:
                c = C_ATT + i * 2
                for hh in range(2):
                    h = i * 2 + hh
                    load(0, wf[0][:, hh * KQ * P:(hh + 1) * KQ * P].rearrange("p (k n) -> p k n", k=KQ),
                         wq[:, :, h, 0:NOPE], c if hh == 0 else None, PARTS)
                    load(0, wf[0][:, 2 * KQ * P:3 * KQ * P].rearrange("p (k n) -> p k n", k=KQ)
                         [:, :, hh * ROPE:(hh + 1) * ROPE], wq[:, :, h, NOPE:NOPE + ROPE], None, PARTS)
                for hh in range(2):
                    h = i * 2 + hh
                    load(1, wf[1][:, hh * KKV * P:(hh + 1) * KKV * P].rearrange("p (k n) -> p k n", k=KKV),
                         wkv[:, :, h, 0:NOPE], c + 1 if hh == 0 else None, PARTS)
                    load(1, wf[1][:, 2 * KKV * P:4 * KKV * P].rearrange("p (k n) -> p k n", k=KKV)
                         [:, :, hh * DV:(hh + 1) * DV], wkv[:, :, h, NOPE:NOPE + DV], None, PARTS)
            with sp.Fori(0, KD) as m:
                for b in range(2):
                    load(b, blocks(b), wo[:, KD * b:KD * (b + 1), bass.ds(m * P, P)], C_OUT + m * 2 + b)
            with sp.Fori(0, KF) as j:
                for b in range(2):
                    load(b, blocks(b), wu[:, :, bass.ds(j * P + b * D_FF, P)], C_UP + j * 2 + b)
            with sp.Fori(0, KF // 2) as i:
                for b in range(2):
                    load(b, wf[b][:, 0:D], w_down[0, bass.ds(i * (2 * P) + b * P, P), :], C_DOWN + i * 2 + b)
            for t in range(NT):
                sp.wait_ge(s_yout, t + 1)
                sp.dma_start(out[0, P * t:P * (t + 1), :], y_out[t % 2][:, :]).then_inc(s_out[t % 2], 16)
            for b in range(2):
                sp.wait_ge(s_out[b], 16 * (NT // 2))

        @block.gpsimd
        def _(pool):
            steps = Chain(pool, s_pool)
            for s in range(2):
                steps.add(pool.memset(wf[s][:, KD * P:SLOT], 0.0))
            steps.add(pool.memset(ident[:, :], 0.0))
            for t in (ident_bf, mask_bf, sm, ones):
                steps.add(pool.memset(t[:, :], 1.0 if t is ones else 0.0))
            steps.add(pool.memset(stat[:, ST_EPS:ST_EPS + 1], EPS))
            steps.wait()
            for t in (ident, ident_bf):
                steps.add(pool.affine_select(out=t[:, :], in_=t[:, :], compare_op=ALU.not_equal, fill=1.0, base=0,
                                             pattern=[[-1, P]], channel_multiplier=1))
            steps.add(pool.affine_select(out=mask_bf[:, :], in_=mask_bf[:, :], compare_op=ALU.is_ge, fill=NEG, base=0,
                                         pattern=[[-1, P]], channel_multiplier=1))
            steps.wait()
            H2 = ROPE // 2
            for b in range(P // H2):
                steps.add(pool.tensor_copy(swap[:, b * H2:(b + 1) * H2], ident[:, (b ^ 1) * H2:((b ^ 1) + 1) * H2]))
            for b in range(2):
                steps.add(pool.tensor_copy(dup[:, b * ROPE:(b + 1) * ROPE], ident[0:ROPE, 0:ROPE]))
            steps.add(pool.tensor_tensor(pick[:, :], ident[0:PARTS3, 0:SH], ident[0:PARTS3, 32:32 + SH], ALU.add))
            steps.wait()
            steps.add(pool.tensor_tensor(pick[:, :], pick[:, :], ident[0:PARTS3, 64:64 + SH], ALU.add))
            for b in range(2):
                steps.add(pool.tensor_copy(dupswap[:, b * ROPE:(b + 1) * ROPE], swap[0:ROPE, 0:ROPE]))
            steps.wait()
            pool.memset(xpad[0][:, 0:XPAD], 0.0).then_inc(s_const, 1)
            pool.memset(xpad[1][:, 0:XPAD], 0.0).then_inc(s_const, 1)
            pool.wait_ge(pre.xn, NT + 1)
            pool.dma_start(gain_a[:, :], norm_mix_post[0:1, :].broadcast_to([P, D])).then_inc(s_gain_post, 16)
            pool.wait_ge(att.xn, NT + 1)
            pool.dma_start(gain_b[:, :], norm_ffn_pre[0:1, :].broadcast_to([P, D])).then_inc(s_gain_ffn, 16)

            def heads(ap, w=P):
                return ap.rearrange("p (h e) -> p h e", e=SP)

            def chunk(q, w):
                first = isinstance(q, int)
                pool.wait_ge(s_smtc, q + 1)
                pool.wait_ge(s_xs, q + 1)
                if not first:
                    pool.wait_ge(s_st, q)
                pool.tensor_tensor(heads(xdte[0:w, :], w), heads(xn[0][0:w, :], w),
                                   bcast(smt_c[0:w, R_DTE:R_DTE + SH], [w, SH, SP]), ALU.mult).then_inc(s_xdte, 1)
                if not first:
                    pool.wait_ge(s_y, q)
                pool.tensor_tensor(heads(xn[1][0:w, :], w), heads(xn[0][0:w, :], w),
                                   bcast(skip_d[0:w, :], [w, SH, SP]), ALU.mult).then_inc(s_xskip, 1)

            pool.wait_ge(s_small, 16 * 4)
            chunk(0, META)
            with pool.Fori(1, NT + 1) as q:
                chunk(q, P)
            pool.wait_ge(s_u, NT + 1)
            pool.dma_start(gain_a[:, :], norm_ffn_post[0:1, :].broadcast_to([P, D])).then_inc(s_gain_last, 16)
            pool.wait_ge(s_gain_last, 16)

        @block.scalar
        def _(act_e):
            sc = nc.scalar
            steps = Chain(act_e, s_act)

            def split_hi(slot, chunk, turn, width=KD * P):
                act_e.wait_ge(s_land[slot], landed(turn))
                if not (isinstance(chunk, int) and chunk < 2):
                    act_e.wait_ge(s_pe, chunk - 1)
                if isinstance(chunk, int) and chunk == 5:
                    steps.add(sc.activation(whi[slot][:, 0:width], wf[slot][:, 0:width], ACT.Copy))
                    act_e.wait_ge(s_small, 16 * 4)
                    steps.wait()
                    sc.activation(dt_cols(whi[slot]), dtw[:, :, :], ACT.Copy).then_inc(s_whi, 1)
                else:
                    sc.activation(whi[slot][:, 0:width], wf[slot][:, 0:width], ACT.Copy).then_inc(s_whi, 1)

            def rstd(src, n, col, done, scale, junk_out):
                steps.add(sc.activation(junk_out, src, ACT.Square, accum_out=stat[0:n, col:col + 1]))
                steps.wait()
                steps.add(sc.activation(stat[0:n, col:col + 1], stat[0:n, col:col + 1], ACT.Ln, scale=scale,
                                        bias=eps[0:n]))
                steps.wait()
                sc.activation(stat[0:n, col + 5:col + 6], stat[0:n, col:col + 1], ACT.Exp, scale=-0.5).then_inc(done, 1)

            def turned_hi(norm, t, dst):
                act_e.wait_ge(norm.turned, t + 1)
                w, b = rows(t), t % 2
                sc.activation(dst[:, :, tcol(t)], turned(b, w), ACT.Copy).then_inc(norm.hi, 1)

            for dst, src, s in ((gain_a, norm_mix_pre, s_gain_pre), (gain_b, attn_out_norm, s_gain_att)):
                act_e.dma_start(dst[:, :], src[0:1, :].broadcast_to([P, D])).then_inc(s, 16)

            def vector_rows(k, r0, src, n):
                act_e.dma_start(vec_rows[r0:r0 + n, k, :], src.rearrange("(n p) -> n p", p=P)).then_inc(s_vec, 16)

            vector_rows(0, V_QA, q_a_norm[0], KQ)
            vector_rows(0, V_KVA, kv_a_norm[0], KKV)
            vector_rows(0, V_SN, ssm_norm[0], XT)
            vector_rows(0, V_CB, ssm_conv_b[0], CT)
            for w in range(TAPS):
                vector_rows(0, V_CW + w * CT, ssm_conv_w[0, w], CT)
            for w in range(2):
                vector_rows(1, w * CF, ffn_conv_w[0, w], CF)
            vector_rows(2, 0, ffn_conv_w[0, 2], CF)
            vector_rows(2, CF, ffn_conv_b[0], CF)
            act_e.dma_start(dtw[:, :, :], wi[:, :, D_IN - SH:D_IN]).then_inc(s_small, 16)
            act_e.dma_start(dt_small[:, 0:1], ssm_dt_bias.rearrange("a h -> h a")).then_inc(s_small, 16)
            act_e.dma_start(dt_small[:, 1:2], ssm_A_log.rearrange("a h -> h a")).then_inc(s_small, 16)
            act_e.dma_start(skip_d[:, :], ssm_D[0:1, :].broadcast_to([P, SH])).then_inc(s_small, 16)
            act_e.dma_start(cos_t[:, :], rope_cos).then_inc(s_rope_tab, 16)
            act_e.dma_start(sin_t[:, :], rope_sin).then_inc(s_rope_tab, 16)

            sc.preload_act_table_set("natural_log_exp_and_others")
            act_e.wait_ge(s_const, 2)
            for t in range(NT + 1):
                act_e.wait_ge(s_x[t], 16)
                rstd(two(h_tm[0:rows(t), t, :]), rows(t), ST_PRE + t, pre.rstd, 1.0 / D, ps[0:rows(t), 6:8, :])
            split_hi(0, 0, 0)
            act_e.wait_ge(s_vt, 1)
            sc.activation(vec[:, 0, 0:NV0], ps[:, 4, 0:NV0], ACT.Copy).then_inc(s_vec_ready, 1)
            sc.activation(vec[:, 1:3, 0:2 * CF], ps[:, 4, 96:3 * 96].rearrange("p (a b) -> p a b", a=2)[:, :, 0:2 * CF],
                          ACT.Copy).then_inc(s_vec_ready, 1)
            for t in range(NT + 1):
                turned_hi(pre, t, hn_hi)
            split_hi(1, 1, 0)

            for c in range(C_Z):
                act_e.wait_ge(s_pe, c + 1)
                sc.activation(two(qkvk[:, c, :]), pair(c % 2), ACT.Copy).then_inc(s_evac, 1)
                split_hi(c % 2, c + 2, (c + 2) // 2)
                if c < KQ + KKV:
                    act_e.wait_ge(s_evac, c + 1)
                    sc.activation(squares[:, c, :], qkvk[:, c, :], ACT.Square).then_inc(s_sq, 1)
            act_e.wait_ge(s_evac, C_Z)
            sc.activation(xn[0][0:SH, 0:TOK], qkvk[ROPE:ROPE + SH, C_Z - 1, :], ACT.Copy).then_inc(s_dtr, 1)
            for g, (n, b) in enumerate(((R_Q, 2), (R_KV, 3))):
                act_e.wait_ge(s_sumsq, g + 1)
                steps.add(sc.activation(two(rstd_f[:, g, :]), pair(b), ACT.Ln, scale=1.0 / n, bias=eps))
                steps.wait()
                sc.activation(rstd_f[:, g, :], rstd_f[:, g, :], ACT.Exp, scale=-0.5).then_inc(s_rstdf, 1)
            act_e.wait_ge(s_dtx, 2)
            steps.add(sc.activation(xn[0][0:SH, 0:TOK], xn[1][0:SH, 0:TOK], ACT.Abs))
            steps.wait()
            steps.add(sc.activation(xn[0][0:SH, 0:TOK], xn[0][0:SH, 0:TOK], ACT.Exp, scale=-1.0))
            steps.wait()
            sc.activation(xn[0][0:SH, 0:TOK], xn[0][0:SH, 0:TOK], ACT.Ln, bias=1.0).then_inc(s_dtl, 1)
            sc.activation(dt_small[:, 2:3], dt_small[:, 1:2], ACT.Exp).then_inc(s_negA, 1)
            for j in range(KQ + KKV):
                act_e.wait_ge(s_qkvn, j + 1)
                sc.activation(qkv_hi[:, j, :], qkvk[:, j, :], ACT.Copy).then_inc(s_qkvhi, 1)
            act_e.wait_ge(s_acs, NT + 1)
            for t in range(NT + 1):
                c = tcol(t)
                steps.add(sc.activation(xn[1][0:SH, c], xn[0][0:SH, c], ACT.Exp, scale=-1.0,
                                        bias=xn[0][0:SH, c.stop - 1:c.stop]))
            sc.activation(sm[R_EXP:R_EXP + SH, :], xn[0][0:SH, 0:TOK], ACT.Exp).then_inc(s_exps, 1)

            sc.preload_act_table(ACT.Silu)
            with act_e.Fori(0, XT // 2) as i:
                for b in range(2):
                    c = i * 2 + (C_Z + b)
                    act_e.wait_ge(s_pe, c + 1)
                    sc.activation(two(z_silu[:, i * 2 + b, :]), pair(b), ACT.Silu)
                    split_hi(b, c + 2, i + (C_Z // 2 + 1))
            with act_e.Fori(0, CT // 2) as i:
                for b in range(2):
                    c = i * 2 + (C_XBC + b)
                    act_e.wait_ge(s_pe, c + 1)
                    sc.activation(two(xpad[b][:, XPAD:XPAD + TOK]), pair(b), ACT.Copy).then_inc(s_xpad, 1)
                    split_hi(b, c + 2, i + (C_XBC // 2 + 1), SLOT)
                    act_e.wait_ge(s_conv, i * 2 + (b + 1))
                    sc.activation(xbc[:, i * 2 + b, :], conv[b][:, :], ACT.Silu).then_inc(s_xbc, 1)

            sc.preload_act_table_set("natural_log_exp_and_others")
            act_e.wait_ge(s_kper, 1)
            sc.activation(kpe_hi[:, :], probs[0][:, :], ACT.Copy).then_inc(s_kpehi, 1)

            with act_e.Fori(0, PAIRS) as i:
                def hi(dst, src, n):
                    if n:
                        act_e.wait_ge(s_proj, i * 6 + n)
                    sc.activation(dst, src, ACT.Copy).then_inc(s_phi, 1)

                act_e.wait_ge(s_proj, i * 6 + 1)
                sc.activation(two(xn[0][:, 0:TOK]), pair(2), ACT.Copy).then_inc(s_rawcp, 1)
                hi(two(qn_hi[0][:, :]), pair(0), 2)
                hi(two(qn_hi[1][:, :]), pair(1), 3)
                hi(two(kn_hi[0][:, :]), pair(3), 4)
                act_e.wait_ge(s_rope, i + 1)
                hi(qpe_hi[:, :], probs[0][:, :], 0)
                hi(two(kn_hi[1][:, :]), pair(0), 6)
                act_e.wait_ge(s_pe, i * 2 + (C_ATT + 2))
                hi(v_parts[:, 0:2, :, 0, :], by_head(ps[:, 2, :]), 0)
                hi(v_parts[:, 2:4, :, 0, :], by_head(ps[:, 3, :]), 0)
                hi(v_parts[:, 4:5, :, 0, :], by_head(ps[:, 6, 0:2 * DV]), 0)
                for s in range(UNITS + 3):
                    if s in (4, 6):
                        b = (s - 4) // 2
                        split_hi(b, i * 2 + (C_ATT + 2 + b), i + (C_ATT // 2 + 1), SLOT)
                    if 2 <= s < UNITS + 2:
                        u = s - 2
                        t, r = u % (NT + 1), rows(u % (NT + 1))
                        act_e.wait_ge(s_T, i * UNITS + (u + 1))
                        ins = sc.activation(pt_hi[u % 2][0:META, 0, :], ps[0:META, 4, 0:P], ACT.Copy)
                        if t:
                            ins = sc.activation(pt_hi[u % 2][:, 1:t + 1, :], turned(2, P)[:, 1:t + 1, :], ACT.Copy)
                        ins.then_inc(s_pthi, 1)
                    if s < UNITS:
                        r = rows(s % (NT + 1))
                        act_e.wait_ge(s_max, i * UNITS + (s + 1))
                        sc.activation(prob_view(s), score_view(s), ACT.Exp, scale=SCALE,
                                      bias=stat[0:r, ST_NM + s:ST_NM + s + 1],
                                      accum_out=stat[0:r, ST_DEN + s:ST_DEN + s + 1]).then_inc(s_exp, 1)

            for t in range(NT + 1):
                act_e.wait_ge(s_attn, PAIRS * UNITS)
                rstd(two(attn[0:rows(t), t, :]), rows(t), ST_ATT + t, att.rstd, 1.0 / D, ps[0:rows(t), 6:8, :])
            for t in range(NT + 1):
                turned_hi(att, t, mixa_hi)

            act_e.wait_ge(s_smt, 1)
            sc.activation(smt[0:META, 0, :], ps[0:META, 4, 0:P], ACT.Copy)
            sc.activation(smt[:, 1:NT + 1, :], ps[:, 5, :].rearrange("p (a b) -> p a b", b=P), ACT.Copy)\
                .then_inc(s_smt_ready, 1)
            act_e.wait_ge(s_dec, 1)
            sc.activation(dec_b[:, :, :], ps[:, 6, 0:(NT + 1) * SH].rearrange("p (a b) -> p a b", b=SH), ACT.Copy)\
                .then_inc(s_smt_ready, 1)
            for j in range(3):
                if j:
                    act_e.wait_ge(s_acs3, j)
                else:
                    act_e.wait_ge(s_acs3_zero, 1)
                    steps.add(sc.activation(acs_rest[0][:, :], sm[R_ACS:R_ACS + SH, :], ACT.Copy))
                    steps.wait()
                sc.activation(acs3[32 * j:32 * j + SH, :], acs_rest[j][:, :], ACT.Copy).then_inc(s_acs_copied, 1)

            def stage(q, cols, w):
                sc.activation(xbc_c[:, :, 0:w], xbc[:, :, cols], ACT.Copy).then_inc(s_stage, 1)

            def chunk(q, w, following):
                first = isinstance(q, int) and q == 0
                act_e.wait_ge(s_xt, q + 1)
                if not first:
                    for s in (s_xdt, s_xdte, s_xskip):
                        act_e.wait_ge(s, q)
                sc.activation(two(xn[0][0:w, :]), ps[0:w, 0:2, :], ACT.Copy)
                sc.activation(b_c[0:w, :], ps[0:w, 2, 0:GROUPS * STATE], ACT.Copy).then_inc(s_xs, 1)
                act_e.wait_ge(s_smtc, q + 1)
                for h in range(SH):
                    if h % 4 == 0:
                        act_e.wait_ge(s_ab, q * 4 + (h // 4 + 1))
                    ins = sc.activation(decay[0:w, h, 0:w], ps[0:w, 4 + h // 4, (h % 4) * P:(h % 4) * P + w], ACT.Exp,
                                        bias=minus_acs[0:w, h:h + 1])
                    if h % 4 == 3:
                        ins.then_inc(s_ex, 1)
                if following is not None:
                    act_e.wait_ge(s_cb if first else s_off, 1 if first else q)
                    stage(q + 1, following, P)

            def after(q):
                return bass.ds(q * P + META, P) if not isinstance(q, int) else slice(q * P + META, (q + 1) * P + META)

            act_e.wait_ge(s_xbc, CT)
            stage(0, slice(0, META), META)
            chunk(0, META, after(0))
            with act_e.Fori(1, NT) as q:
                chunk(q, P, after(q))
            chunk(NT, P, None)

            act_e.wait_ge(s_gate, NT + 1)
            for k in range(XT):
                sc.activation(gsq[:, k, :], gated[:, k, :], ACT.Square).then_inc(s_gsq, 1)
            for g in range(GROUPS):
                act_e.wait_ge(s_gsum, g + 1)
                steps.add(sc.activation(two(rstd_g[:, g, :]), pair(2 + g), ACT.Ln, scale=1.0 / GC, bias=eps))
                steps.wait()
                sc.activation(rstd_g[:, g, :], rstd_g[:, g, :], ACT.Exp, scale=-0.5).then_inc(s_rg, 1)
            for k in range(XT):
                act_e.wait_ge(s_ng, k + 1)
                sc.activation(mixs_hi[:, k, :], normed_g[k % 2][:, :], ACT.Copy).then_inc(s_mshi, 1)

            with act_e.Fori(0, KD // 2) as i:
                for m in range(2):
                    c = i * 4 + (C_OUT + 2 * m)
                    split_hi(0, c + 2, i * 2 + (C_OUT // 2 + 1 + m))
                    act_e.wait_ge(s_pe, c + 2)
                    sc.activation(two(mixo[:, i * 2 + m, :]), pair(m), ACT.Copy).then_inc(s_mixo, 1)
                    split_hi(1, c + 3, i * 2 + (C_OUT // 2 + 1 + m))
            for t in range(NT + 1):
                n = rows(t)
                act_e.wait_ge(s_t1, t + 1)
                rstd(ps[0:n, 2 * (t % 2):2 * (t % 2) + 2, :], n, ST_POST + t, s_rpost, 1.0 / D, ps[0:n, 6:8, :])
            for t in range(NT + 1):
                act_e.wait_ge(s_h, t + 1)
                rstd(two(h_tm[0:rows(t), t, :]), rows(t), ST_FFN + t, ffn.rstd, 1.0 / D, ps[0:rows(t), 6:8, :])
            for t in range(NT + 1):
                turned_hi(ffn, t, hn2_hi)

            sc.preload_act_table(ACT.Silu)
            with act_e.Fori(0, KF) as j:
                for b, (u, done) in enumerate(((u_gate, s_ug), (u_value, s_uv))):
                    c = j * 2 + (C_UP + b)
                    act_e.wait_ge(s_pe, c + 1)
                    sc.activation(two(u[:, :]), pair(b, NF // 2), ACT.Copy).then_inc(done, 1)
                    split_hi(b, c + 2, j + (C_UP // 2 + 1))
                act_e.wait_ge(s_cg, j + 1)
                sc.activation(c_gate[:, :], c_gate[:, :], ACT.Silu).then_inc(s_silu, 1)

            def stage_hi(slot, k, first=False):
                if not first:
                    act_e.wait_ge(s_pe, k + (C_DOWN - 1))
                sc.activation(st_hi[slot][:, :], act[:, k, :], ACT.Copy).then_inc(s_sthi, 1)

            for k in range(2):
                act_e.wait_ge(s_actr, KF)
                stage_hi(k, k, True)
            with act_e.Fori(0, KF // 2 - 1) as i:
                for b in range(2):
                    stage_hi(b, i * 2 + (2 + b))
                    split_hi(b, i * 2 + (C_DOWN + 2 + b), i + (C_DOWN // 2 + 1))
            sc.preload_act_table_set("natural_log_exp_and_others")
            for t in range(NT):
                act_e.wait_ge(s_down, t + 1)
                rstd(ps[:, 2 * t:2 * t + 2, :], P, ST_LAST + t, s_rlast, 1.0 / D, two(junk[:, :]))

        @block.vector
        def _(dve):
            ve = nc.vector
            steps = Chain(dve, s_dve)

            def split_lo(slot, chunk, width=KD * P):
                dve.wait_ge(s_whi, chunk + 1)
                whole = slice(0, width)
                if isinstance(chunk, int) and chunk == 5:
                    steps.add(ve.tensor_tensor(wlo[slot][:, whole], wf[slot][:, whole],
                                               whi[slot][:, whole].bitcast(F32), ALU.subtract))
                    dve.wait_ge(s_small, 16 * 4)
                    steps.wait()
                    ve.tensor_tensor(dt_cols(wlo[slot]), dtw[:, :, :], dt_cols(whi[slot]).bitcast(F32),
                                     ALU.subtract).then_inc(s_wlo, 1)
                else:
                    ve.tensor_tensor(wlo[slot][:, whole], wf[slot][:, whole], whi[slot][:, whole].bitcast(F32),
                                     ALU.subtract).then_inc(s_wlo, 1)

            def scale_rows(norm, t, src, col, gain):
                n = rows(t)
                dve.wait_ge(norm.rstd, t + 1)
                if t >= 2:
                    dve.wait_ge(norm.turned, t - 1)
                ve.scalar_tensor_tensor(xn[t % 2][0:n, :], src, stat[0:n, col + 5 + t:col + 6 + t], gain[0:n, :],
                                        ALU.mult, ALU.mult).then_inc(norm.xn, 1)

            def turned_lo(norm, t, dst, upper):
                dve.wait_ge(norm.hi, t + 1)
                w, b = rows(t), t % 2
                ve.tensor_tensor(dst[:, :, tcol(t)], turned(b, w), upper[:, :, tcol(t)].bitcast(F32),
                                 ALU.subtract).then_inc(norm.lo, 1)

            def norm_rows(norm, src, col, gain, upper, lower):
                for t in range(NT + 2):
                    if t <= NT:
                        scale_rows(norm, t, src[0:rows(t), t, :], col, gain)
                    if t:
                        turned_lo(norm, t - 1, lower, upper)

            dve.wait_ge(s_gain_pre, 16)
            norm_rows(pre, h_tm, ST_PRE, gain_a, hn_hi, hn_lo)
            split_lo(0, 0)
            split_lo(1, 1)
            for c in range(C_Z):
                split_lo(c % 2, c + 2)

            dve.wait_ge(s_dtr, 1)
            ve.tensor_scalar(xn[1][0:SH, 0:TOK], xn[0][0:SH, 0:TOK], dt_small[:, 0:1], None, ALU.add).then_inc(s_dtx, 1)
            dve.wait_ge(s_dtx, 1)
            ve.tensor_scalar(sm[R_DT:R_DT + SH, :], xn[1][0:SH, 0:TOK], 0.0, None, ALU.max).then_inc(s_dtx, 1)
            dve.wait_ge(s_vec_ready, 2)
            for j in range(KQ + KKV):
                g = int(j >= KQ)
                dve.wait_ge(s_rstdf, g + 1)
                ve.scalar_tensor_tensor(qkvk[:, j, :], qkvk[:, j, :], vec[:, 0, V_QA + j:V_QA + j + 1],
                                        rstd_f[:, g, :], ALU.mult, ALU.mult).then_inc(s_qkvn, 1)
            dve.wait_ge(s_dtl, 1)
            steps.add(ve.tensor_tensor(sm[R_DT:R_DT + SH, :], sm[R_DT:R_DT + SH, :], xn[0][0:SH, 0:TOK], ALU.add))
            dve.wait_ge(s_negA, 1)
            steps.wait()
            steps.add(ve.tensor_scalar(xn[1][0:SH, 0:TOK], sm[R_DT:R_DT + SH, :], dt_small[:, 2:3], -1.0, ALU.mult,
                                       ALU.mult))
            steps.wait()
            for t in range(NT + 1):
                c = tcol(t)
                ve.tensor_tensor_scan(xn[0][0:SH, c], ones[0:SH, 0:rows(t)], xn[1][0:SH, c], 0.0, ALU.mult,
                                      ALU.add).then_inc(s_acs, 1)
            dve.wait_ge(s_acs, NT + 1)
            steps.add(ve.tensor_copy(sm[R_ACS:R_ACS + SH, :], xn[0][0:SH, 0:TOK]))
            for j in range(KQ + KKV):
                dve.wait_ge(s_qkvhi, j + 1)
                ve.tensor_tensor(qkv_lo[:, j, :], qkvk[:, j, :], qkv_hi[:, j, :].bitcast(F32),
                                 ALU.subtract).then_inc(s_qkvlo, 1)
            dve.wait_ge(s_exps, 1)
            ve.tensor_tensor(sm[R_DTE:R_DTE + SH, :], sm[R_DT:R_DT + SH, :], xn[1][0:SH, 0:TOK],
                             ALU.mult).then_inc(s_sm, 1)
            dve.wait_ge(s_sm, 1)
            steps.add(ve.tensor_copy(dt_ends[:, 0:1], sm[R_EXP:R_EXP + SH, META - 1:META]))
            steps.add(ve.tensor_copy(dt_ends[:, 1:NT + 1], sm[R_EXP:R_EXP + SH, META + P - 1:TOK:P]))

            with dve.Fori(0, XT // 2) as i:
                for b in range(2):
                    split_lo(b, i * 2 + (C_Z + 2 + b))

            with dve.Fori(0, CT // 2) as i, steps.loop(i, CT // 2, 2 * (TAPS - 1)):
                for b in range(2):
                    t = i * 2 + b
                    dve.wait_ge(s_xpad, t + 1)

                    def tap(w):
                        return vec[:, 0, bass.ds(t + (V_CW + w * CT), 1)]

                    steps.add(ve.tensor_scalar(conv[b][:, :], xpad[b][:, XPAD:XPAD + TOK], tap(XPAD),
                                               vec[:, 0, bass.ds(t + V_CB, 1)], ALU.mult, ALU.add))
                    for w in range(XPAD):
                        steps.wait()
                        ins = ve.scalar_tensor_tensor(conv[b][:, :], xpad[b][:, w:w + TOK], tap(w), conv[b][:, :],
                                                      ALU.mult, ALU.add)
                        if w < XPAD - 1:
                            steps.add(ins)
                        else:
                            ins.then_inc(s_conv, 1)
                    split_lo(b, t + (C_XBC + 2), SLOT)

            dve.wait_ge(s_kpe, 1)
            dve.wait_ge(s_rope_tab, 32)
            steps.add(ve.tensor_tensor(two(probs[0][:, :]), pair(2), two(cos_t[:, :]), ALU.mult))
            steps.add(ve.tensor_tensor(two(probs[1][:, :]), pair(3), two(sin_t[:, :]), ALU.mult))
            steps.wait()
            ve.tensor_tensor(probs[0][:, :], probs[0][:, :], probs[1][:, :], ALU.add).then_inc(s_kper, 1)
            dve.wait_ge(s_kpehi, 1)
            ve.tensor_tensor(kpe_lo[:, :], probs[0][:, :], kpe_hi[:, :].bitcast(F32), ALU.subtract).then_inc(s_kpelo, 1)

            with dve.Fori(0, PAIRS) as i, steps.loop(i, PAIRS, 2 + 3 * UNITS):
                def lo(dst, src, upper, n):
                    dve.wait_ge(s_phi, i * 8 + n)
                    ve.tensor_tensor(dst, src, upper.bitcast(F32), ALU.subtract).then_inc(s_plo, 1)

                lo(two(qn_lo[0][:, :]), pair(0), two(qn_hi[0][:, :]), 1)
                lo(two(qn_lo[1][:, :]), pair(1), two(qn_hi[1][:, :]), 2)
                lo(two(kn_lo[0][:, :]), pair(3), two(kn_hi[0][:, :]), 3)
                dve.wait_ge(s_proj, i * 6 + 5)
                steps.add(ve.tensor_tensor(two(probs[1][:, :]), pair(2), two(sin_t[:, :]), ALU.mult))
                steps.add(ve.tensor_tensor(probs[0][:, :], xn[0][:, 0:TOK], cos_t[:, :], ALU.mult))
                steps.wait()
                ve.tensor_tensor(probs[0][:, :], probs[0][:, :], probs[1][:, :], ALU.add).then_inc(s_rope, 1)
                lo(qpe_lo[:, :], probs[0][:, :], qpe_hi[:, :], 4)
                lo(two(kn_lo[1][:, :]), pair(0), two(kn_hi[1][:, :]), 5)
                for n, (t0, t1, b) in enumerate(((0, 2, 2), (2, 4, 3), (4, 5, 6))):
                    lo(v_parts[:, t0:t1, :, 1, :], by_head(ps[:, b, 0:(t1 - t0) * 2 * DV]), v_parts[:, t0:t1, :, 0, :],
                       6 + n)
                for s in range(UNITS + 3):
                    if s in (5, 7):
                        b = (s - 5) // 2
                        split_lo(b, i * 2 + (C_ATT + 2 + b), SLOT)
                    if s < UNITS:
                        r = rows(s % (NT + 1))
                        v = score_view(s)
                        dve.wait_ge(s_S, i * UNITS + (s + 1))
                        m = stat[0:r, ST_NM + s:ST_NM + s + 1]
                        steps.add(ve.tensor_reduce(m, v, AX.XY if len(v.shape) == 3 else AX.X, ALU.max))
                        steps.wait()
                        ve.tensor_scalar(m, m, -SCALE, None, ALU.mult).then_inc(s_max, 1)
                    if 2 <= s < UNITS + 2:
                        u = s - 2
                        t, r = u % (NT + 1), rows(u % (NT + 1))
                        dve.wait_ge(s_pthi, i * UNITS + (u + 1))
                        ins = ve.tensor_tensor(pt_lo[u % 2][0:META, 0, :], ps[0:META, 4, 0:P],
                                               pt_hi[u % 2][0:META, 0, :].bitcast(F32), ALU.subtract)
                        if t:
                            ins = ve.tensor_tensor(pt_lo[u % 2][:, 1:t + 1, :], turned(2, P)[:, 1:t + 1, :],
                                                   pt_hi[u % 2][:, 1:t + 1, :].bitcast(F32), ALU.subtract)
                        ins.then_inc(s_ptlo, 1)
                    if s >= 3:
                        u = s - 3
                        t, r = u % (NT + 1), rows(u % (NT + 1))
                        rd = stat[0:r, ST_RDEN + u:ST_RDEN + u + 1]
                        dve.wait_ge(s_exp, i * UNITS + (u + 1))
                        steps.add(ve.reciprocal(rd, stat[0:r, ST_DEN + u:ST_DEN + u + 1]))
                        steps.wait()
                        dve.wait_ge(s_pv, i * UNITS + (u + 1))
                        dst = attn[0:r, t, bass.ds(i * (2 * DV) + (u // (NT + 1)) * DV, DV)]
                        steps.add(ve.tensor_scalar(dst, ps[0:r, 6, DV:2 * DV], rd, None, ALU.mult))
                        steps.wait()
                        ve.scalar_tensor_tensor(dst, ps[0:r, 6, 0:DV], rd, dst, ALU.mult, ALU.add).then_inc(s_attn, 1)

            dve.wait_ge(s_gain_att, 16)
            norm_rows(att, attn, ST_ATT, gain_b, mixa_hi, mixa_lo)

            ve.tensor_tensor(ends[:, :, :], bcast(dt_ends[:, :], [SH, NT + 1, SH]),
                             ident[0:SH, 0:SH].unsqueeze(1).broadcast_to([SH, NT + 1, SH]),
                             ALU.mult).then_inc(s_ends, 1)
            ve.memset(acs3[:, :], 0.0).then_inc(s_acs3_zero, 1)
            for j in range(2):
                dve.wait_ge(s_acs_copied, j + 1)
                ve.tensor_tensor(acs_rest[j + 1][:, :], acs_rest[j][:, :], acs3[32 * j:32 * j + SH, :],
                                 ALU.subtract).then_inc(s_acs3, 1)

            def heads(ap):
                return ap.rearrange("p (h e) -> p h e", e=SP)

            def both(ap):
                return ap.rearrange("p a (h e) -> p (a h) e", e=SP)

            def chunk(q, cols, w):
                first = isinstance(q, int)
                if first:
                    dve.wait_ge(s_smt_ready, 2)
                else:
                    dve.wait_ge(s_xdte, q)
                    dve.wait_ge(s_ex, q * 4)
                ve.tensor_copy(smt_c[0:w, :], smt[0:w, q, :])
                ve.tensor_scalar(minus_acs[0:w, :], smt[0:w, q, R_ACS:R_ACS + SH], -1.0, None, ALU.mult)\
                    .then_inc(s_smtc, 1)
                dve.wait_ge(s_xs, q + 1)
                dve.wait_ge(s_smtc, q + 1)
                ve.tensor_tensor(heads(xdt[0:w, :]), heads(xn[0][0:w, :]),
                                 bcast(smt_c[0:w, R_DT:R_DT + SH], [w, SH, SP]), ALU.mult).then_inc(s_xdt, 1)
                if not first:
                    dve.wait_ge(s_off, q)
                    ve.tensor_tensor(heads(y_tm[:, :]), both(ps[:, 0:2, :]),
                                     bcast(smt_c[:, R_EXP:R_EXP + SH], [P, SH, SP]), ALU.mult).then_inc(s_yoff, 1)
                    steps.add(ve.tensor_tensor(heads(state[:, :]), heads(state[:, :]),
                                               bcast(dec_b[:, q, :], [P, SH, SP]), ALU.mult))
                dve.wait_ge(s_cb, q + 1)
                for j in range(4):
                    dve.wait_ge(s_ex, q * 4 + (j + 1))
                    d = decay[0:w, 4 * j:4 * j + 4, 0:w]
                    g = 4 * j // HG
                    ins = ve.tensor_tensor(d, d, ps[0:w, 3, g * P:g * P + w].unsqueeze(1).broadcast_to([w, 4, w]),
                                           ALU.mult)
                ins.then_inc(s_M, 1)
                dve.wait_ge(s_xskip, q + 1)
                if first:
                    dve.wait_ge(s_st, q + 1)
                    ve.tensor_copy(two(state[:, :]), ps[:, 6:8, :]).then_inc(s_state, 1)
                    dve.wait_ge(s_yd, q + 1)
                    ve.tensor_tensor(two(y_tm[0:w, :]), ps[0:w, 4:6, :], two(xn[1][0:w, :]), ALU.add).then_inc(s_y, 1)
                else:
                    dve.wait_ge(s_yoff, q)
                    steps.add(ve.tensor_tensor(y_tm[:, :], y_tm[:, :], xn[1][:, :], ALU.add))
                    dve.wait_ge(s_st, q + 1)
                    steps.wait()
                    ve.tensor_tensor(two(state[:, :]), ps[:, 6:8, :], two(state[:, :]), ALU.add).then_inc(s_state, 1)
                    dve.wait_ge(s_yd, q + 1)
                    ve.tensor_tensor(two(y_tm[:, :]), ps[:, 4:6, :], two(y_tm[:, :]), ALU.add).then_inc(s_y, 1)
                dve.wait_ge(s_yt, q + 1)
                ve.tensor_tensor(gated[:, :, cols], turned(3, w), z_silu[:, :, cols], ALU.mult).then_inc(s_gate, 1)

            chunk(0, slice(0, META), META)
            with dve.Fori(1, NT + 1) as q, steps.loop(q - 1, NT, 2):
                chunk(q, bass.ds(q * P - (P - META), P), P)

            for k in range(XT):
                dve.wait_ge(s_rg, k // (XT // GROUPS) + 1)
                if k >= 2:
                    dve.wait_ge(s_mshi, k - 1)
                ve.scalar_tensor_tensor(normed_g[k % 2][:, :], gated[:, k, :], vec[:, 0, V_SN + k:V_SN + k + 1],
                                        rstd_g[:, k // (XT // GROUPS), :], ALU.mult, ALU.mult).then_inc(s_ng, 1)
                dve.wait_ge(s_mshi, k + 1)
                ve.tensor_tensor(mixs_lo[:, k, :], normed_g[k % 2][:, :], mixs_hi[:, k, :].bitcast(F32),
                                 ALU.subtract).then_inc(s_mslo, 1)

            with dve.Fori(0, KD // 2) as i:
                for m in range(2):
                    for b in range(2):
                        split_lo(b, i * 4 + (C_OUT + 2 * m + 2 + b))
            dve.wait_ge(s_gain_post, 16)
            for t in range(NT + 1):
                n = rows(t)
                dve.wait_ge(s_rpost, t + 1)
                ve.scalar_tensor_tensor(two(post[t % 2][0:n, :]), ps[0:n, 2 * (t % 2):2 * (t % 2) + 2, :],
                                        stat[0:n, ST_POST + 5 + t:ST_POST + 6 + t], two(gain_a[0:n, :]),
                                        ALU.mult, ALU.mult).then_inc(s_u, 1)
                dve.wait_ge(s_u, t + 1)
                ve.tensor_tensor(h_tm[0:n, t, :], h_tm[0:n, t, :], post[t % 2][0:n, :], ALU.add).then_inc(s_h, 1)
            dve.wait_ge(s_gain_ffn, 16)
            norm_rows(ffn, h_tm, ST_FFN, gain_b, hn2_hi, hn2_lo)

            with dve.Fori(0, KF) as j, steps.loop(j, KF, 2 * (FTAPS - 1)):
                for b, (u, cv, ready, done) in enumerate(((u_gate, c_gate, s_ug, s_cg), (u_value, c_value, s_uv, s_cv))):
                    dve.wait_ge(ready, j + 1)
                    steps.add(ve.tensor_scalar(cv[:, :], u[:, NF - SEQ:NF],
                                               vec[:, 2, bass.ds(j + b * KF, 1)],
                                               vec[:, 2, bass.ds(j + (CF + b * KF), 1)], ALU.mult, ALU.add))
                    for w in range(FTAPS - 1):
                        o = NF - SEQ - (FTAPS - 1) + w
                        steps.wait()
                        ins = ve.scalar_tensor_tensor(cv[:, :], u[:, o:o + SEQ],
                                                      vec[:, 1, bass.ds(j + (w * CF + b * KF), 1)], cv[:, :],
                                                      ALU.mult, ALU.add)
                        if w < FTAPS - 2:
                            steps.add(ins)
                        else:
                            ins.then_inc(done, 1)
                    split_lo(b, j * 2 + (C_UP + 2 + b))
                dve.wait_ge(s_silu, j + 1)
                dve.wait_ge(s_cv, j + 1)
                ve.tensor_tensor(act[:, j, :], c_gate[:, :], c_value[:, :], ALU.mult).then_inc(s_actr, 1)
                dve.wait_ge(s_actr, j + 1)

            def stage_lo(slot, k):
                dve.wait_ge(s_sthi, k + 1)
                ve.tensor_tensor(st_lo[slot][:, :], act[:, k, :], st_hi[slot][:, :].bitcast(F32),
                                 ALU.subtract).then_inc(s_stlo, 1)

            for k in range(2):
                stage_lo(k, k)
            with dve.Fori(0, KF // 2 - 1) as i:
                for b in range(2):
                    stage_lo(b, i * 2 + (2 + b))
                    split_lo(b, i * 2 + (C_DOWN + 2 + b))
            dve.wait_ge(s_gain_last, 16)
            for t in range(NT):
                dve.wait_ge(s_rlast, t + 1)
                if t >= 2:
                    dve.wait_ge(s_out[t % 2], 16)
                ve.scalar_tensor_tensor(two(y_out[t % 2][:, :]), ps[:, 2 * t:2 * t + 2, :],
                                        stat[:, ST_LAST + 5 + t:ST_LAST + 6 + t], two(gain_a[:, :]),
                                        ALU.mult, ALU.mult).then_inc(s_ylast, 1)
                dve.wait_ge(s_ylast, t + 1)
                ve.tensor_tensor(y_out[t % 2][:, :], y_out[t % 2][:, :], h_tm[:, t + 1, :], ALU.add)\
                    .then_inc(s_yout, 1)

        @block.tensor
        def _(pe):
            mm = nc.tensor.matmul

            def three(out_ap, w_hi, w_lo, x_hi, x_lo, first, last):
                mm(out_ap, w_hi, x_hi, start=first, stop=False)
                mm(out_ap, w_hi, x_lo, start=False, stop=False)
                return mm(out_ap, w_lo, x_hi, start=False, stop=last)

            def chunk(slot, b, x_hi, x_lo, halves, k0=0, first=True, last=True):
                for h, cols in enumerate(halves):
                    w = cols.stop - cols.start
                    for k in range(KD):
                        ins = three(ps[:, 2 * b + h, 0:w], whi[slot][:, k * P:(k + 1) * P],
                                    wlo[slot][:, k * P:(k + 1) * P], x_hi[:, k, cols], x_lo[:, k, cols],
                                    first and k == 0, last and k == KD - 1)
                return ins

            def turn_rows(norm, t):
                w, b = rows(t), t % 2
                pe.wait_ge(norm.xn, t + 1)
                if t >= 2:
                    pe.wait_ge(norm.lo, t - 1)
                for k in range(KD):
                    ins = nc.tensor.transpose(turned(b, w)[:, k, :], xn[b][0:w, k * P:(k + 1) * P], ident[0:w, 0:w])
                ins.then_inc(norm.turned, 1)

            pe.wait_ge(s_const, 2)
            pe.wait_ge(s_vec, 16 * 12)
            for k, n in enumerate((NV0, 2 * CF, 2 * CF)):
                ins = nc.tensor.transpose(ps[:, 4, k * 96:k * 96 + n], vec_rows[0:n, k, :], ident[0:n, 0:n])
            ins.then_inc(s_vt, 1)
            for t in range(NT + 1):
                turn_rows(pre, t)
            pe.wait_ge(pre.lo, NT + 1)
            for c in range(C_Z):
                pe.wait_ge(s_wlo, c + 1)
                chunk(c % 2, c % 2, hn_hi, hn_lo, WH).then_inc(s_pe, 1)
            for g, (j0, j1) in enumerate(((0, KQ), (KQ, KQ + KKV))):
                pe.wait_ge(s_sq, j1)
                for h, cols in enumerate(WH):
                    for j in range(j0, j1):
                        ins = mm(ps[:, 4 + 2 * g + h, 0:HALF], ones[:, :], squares[:, j, cols], start=j == j0,
                                 stop=j == j1 - 1)
                ins.then_inc(s_sumsq, 1)
            with pe.Fori(C_Z // 2, C_ATT // 2) as i:
                for b in range(2):
                    pe.wait_ge(s_wlo, i * 2 + (b + 1))
                    chunk(b, b, hn_hi, hn_lo, WH).then_inc(s_pe, 1)
            pe.wait_ge(s_rstdf, 2)
            pe.wait_ge(s_evac, C_Z)
            for b, m in enumerate((dup, dupswap)):
                for h, cols in enumerate(WH):
                    ins = mm(ps[:, 4 + 2 * b + h, 0:HALF], m[:, :], qkvk[0:ROPE, C_Z - 1, cols], start=True, stop=True)
            ins.then_inc(s_kpe, 1)

            pe.wait_ge(s_qkvlo, KQ + KKV)
            pe.wait_ge(s_kpelo, 1)
            with pe.Fori(0, PAIRS) as i:
                def project(b, slot, col, K, j0, step=P):
                    for h, cols in enumerate(WH):
                        for k in range(K):
                            w = slice(col + k * step, col + k * step + P)
                            ins = three(ps[:, 2 * b + h, 0:HALF], whi[slot][:, w], wlo[slot][:, w],
                                        qkv_hi[:, j0 + k, cols], qkv_lo[:, j0 + k, cols], k == 0, k == K - 1)
                    return ins

                def values(t, dst):
                    cols = slice(0, P) if t == 0 else tcol(t)
                    for k in range(KKV):
                        w = slice(2 * KKV * P + k * 2 * DV, 2 * KKV * P + (k + 1) * 2 * DV)
                        ins = three(dst, qkv_hi[:, KQ + k, cols], qkv_lo[:, KQ + k, cols], whi[1][:, w], wlo[1][:, w],
                                    k == 0, k == KKV - 1)
                    return ins

                pe.wait_ge(s_wlo, i * 2 + (C_ATT + 1))
                project(2, 0, 2 * KQ * P, KQ, 0).then_inc(s_proj, 1)
                project(0, 0, 0, KQ, 0).then_inc(s_proj, 1)
                project(1, 0, KQ * P, KQ, 0).then_inc(s_proj, 1)
                pe.wait_ge(s_wlo, i * 2 + (C_ATT + 2))
                pe.wait_ge(s_plo, i * 8 + 1)
                project(3, 1, 0, KKV, KQ).then_inc(s_proj, 1)
                pe.wait_ge(s_rawcp, i + 1)
                mm(ps[:, 4, 0:HALF], swap[:, :], xn[0][:, WH[0]], start=True, stop=True).then_inc(s_pe, 1)
                mm(ps[:, 5, 0:HALF], swap[:, :], xn[0][:, WH[1]], start=True, stop=True).then_inc(s_proj, 1)
                project(0, 1, KKV * P, KKV, KQ).then_inc(s_proj, 1)
                pe.wait_ge(s_plo, i * 8 + 2)
                values(0, ps[:, 2, 0:2 * DV])
                values(1, ps[:, 2, 2 * DV:4 * DV])
                values(2, ps[:, 3, 0:2 * DV])
                values(3, ps[:, 3, 2 * DV:4 * DV])
                pe.wait_ge(s_plo, i * 8 + 3)
                values(4, ps[:, 6, 0:2 * DV]).then_inc(s_pe, 1)

                def scores(u):
                    hh, t = divmod(u, NT + 1)
                    n, b = score_cols(u), 2 * (u % 2)
                    qc = slice(0, P) if t == 0 else tcol(t)
                    pr = slice(hh * ROPE, (hh + 1) * ROPE)
                    parts = [(ps[:, b, 0:n], 0, n)] if n <= BANK else \
                        [(ps[:, b + h, 0:HALF], h * HALF, (h + 1) * HALF) for h in range(2)]
                    for dst, c0, c1 in parts:
                        ks = slice(c0, c1)
                        three(dst, qn_hi[hh][:, qc], qn_lo[hh][:, qc], kn_hi[hh][:, ks], kn_lo[hh][:, ks], True, False)
                        masked = c1 == n
                        ins = three(dst, qpe_hi[pr, qc], qpe_lo[pr, qc], kpe_hi[pr, ks], kpe_lo[pr, ks], False,
                                    not masked)
                    d = META if t == 0 else P
                    last = parts[-1]
                    w = last[2] - last[1]
                    return mm(ps[:, b + len(parts) - 1, w - d:w], ident_bf[:, :], mask_bf[:, 0:d], start=False, stop=True)

                for s in range(UNITS + 3):
                    if s < UNITS:
                        if s == 0:
                            pe.wait_ge(s_plo, i * 8 + 5)
                        elif s == 1:
                            pe.wait_ge(s_plo, i * 8 + 7)
                        else:
                            pe.wait_ge(s_exp, i * UNITS + (s - 1))
                        scores(s).then_inc(s_S, 1)
                    if 2 <= s < UNITS + 2:
                        u = s - 2
                        t = u % (NT + 1)
                        pe.wait_ge(s_exp, i * UNITS + (u + 1))
                        if s == 2:
                            pe.wait_ge(s_plo, i * 8 + 8)
                        else:
                            pe.wait_ge(s_ptlo, i * UNITS + u)
                        p = probs[u % 2]
                        ins = nc.tensor.transpose(ps[0:META, 4, 0:P], p[:, 0:META], ident[:, :])
                        for j in range(t):
                            ins = nc.tensor.transpose(turned(2, P)[:, 1 + j, :],
                                                      p[:, META + j * P:META + (j + 1) * P], ident[:, :])
                        ins.then_inc(s_T, 1)
                    if s >= 3:
                        u = s - 3
                        hh, t = divmod(u, NT + 1)
                        pe.wait_ge(s_ptlo, i * UNITS + (u + 1))
                        if u >= 1:
                            pe.wait_ge(s_attn, i * UNITS + u)
                        for j in range(t + 1):
                            kr = slice(0, META if j == 0 else P)
                            v = v_parts[kr, j, hh, :, :].rearrange("p a d -> p (a d)")
                            mm(ps[:, 6, 0:2 * DV], pt_hi[u % 2][kr, j, :], v, start=j == 0, stop=False)
                            ins = mm(ps[:, 6, 0:2 * DV], pt_lo[u % 2][kr, j, :], v, start=False, stop=j == t)
                        ins.then_inc(s_pv, 1)

            for t in range(NT + 1):
                turn_rows(att, t)

            pe.wait_ge(s_sm, 1)
            nc.tensor.transpose(ps[0:META, 4, 0:P], sm[:, tcol(0)], ident[:, :])
            for t in range(1, NT + 1):
                ins = nc.tensor.transpose(ps[:, 5, (t - 1) * P:t * P], sm[:, tcol(t)], ident[:, :])
            ins.then_inc(s_smt, 1)
            pe.wait_ge(s_ends, 1)
            mm(ps[:, 6, 0:(NT + 1) * SH], ones[0:SH, :], ends[:, :, :].rearrange("p a b -> p (a b)"), start=True,
               stop=True).then_inc(s_dec, 1)
            pe.wait_ge(att.lo, NT + 1)
            pe.wait_ge(s_smt_ready, 2)
            pe.wait_ge(s_acs_copied, 3)

            def turn_chunk(q, w):
                pe.wait_ge(s_stage, q + 1)
                for k in range(XT):
                    nc.tensor.transpose(ps[0:w, k // 4, (k % 4) * P:(k % 4 + 1) * P], xbc_c[:, k, 0:w], ident[:, :])
                for g in range(GROUPS):
                    ins = nc.tensor.transpose(ps[0:w, 2, g * P:(g + 1) * P], xbc_c[:, XT + g, 0:w], ident[:, :])
                ins.then_inc(s_xt, 1)
                for g in range(GROUPS):
                    ins = mm(ps[0:w, 3, g * P:g * P + w], xbc_c[:, XT + g, 0:w], xbc_c[:, XT + GROUPS + g, 0:w],
                             start=True, stop=True)
                ins.then_inc(s_cb, 1)

            def ssm_chunk(q, cols, w, last=False):
                first = isinstance(q, int) and q == 0
                for j in range(4):
                    if not first and j == 0:
                        pe.wait_ge(s_y, q)
                    if not first and j == 2:
                        pe.wait_ge(s_gate, q)
                    block4 = ps[0:w, 4 + j, :].rearrange("p (a b) -> p a b", b=P)[:, :, 0:w]
                    mm(block4, mask_bf[0:w, 0:w], ident_bf[0:w, 0:w].unsqueeze(1).broadcast_to([w, 4, w]), start=True,
                       stop=False)
                    for h in range(4 * j, 4 * j + 4):
                        ins = mm(ps[0:w, 4 + j, (h % 4) * P:(h % 4) * P + w],
                                 pick[:, h:h + 1].broadcast_to([PARTS3, w]), acs3[0:PARTS3, cols], start=False,
                                 stop=h % 4 == 3)
                    ins.then_inc(s_ab, 1)
                pe.wait_ge(s_xs, q + 1)
                if not first:
                    pe.wait_ge(s_state, q)
                    for g in range(GROUPS):
                        ins = mm(ps[:, g, :], xbc_c[:, XT + GROUPS + g, :], state[:, g * GC:(g + 1) * GC],
                                 start=True, stop=True)
                    ins.then_inc(s_off, 1)
                pe.wait_ge(s_ex, q * 4 + 4)
                pe.wait_ge(s_xdte, q + 1)
                for g in range(GROUPS):
                    ins = mm(ps[:, 6 + g, :], b_c[0:w, g * STATE:(g + 1) * STATE], xdte[0:w, g * GC:(g + 1) * GC],
                             start=True, stop=True)
                ins.then_inc(s_st, 1)
                pe.wait_ge(s_xdt, q + 1)
                pe.wait_ge(s_M, q + 1)
                for h in range(SH):
                    ins = mm(ps[0:w, 4 + h // HG, (h % HG) * SP:(h % HG + 1) * SP], decay[0:w, h, 0:w],
                             xdt[0:w, h * SP:(h + 1) * SP], start=True, stop=True)
                ins.then_inc(s_yd, 1)
                if not last:
                    if not first:
                        pe.wait_ge(s_yoff, q)
                    turn_chunk(q + 1, P)
                pe.wait_ge(s_y, q + 1)
                pe.wait_ge(s_state, q + 1)
                for k in range(XT):
                    ins = nc.tensor.transpose(turned(3, w)[:, k, :], y_tm[0:w, k * P:(k + 1) * P], ident[0:w, 0:w])
                ins.then_inc(s_yt, 1)

            turn_chunk(0, META)
            ssm_chunk(0, slice(0, META), META)
            with pe.Fori(1, NT) as q:
                ssm_chunk(q, bass.ds(q * P - (P - META), P), P)
            ssm_chunk(NT, tcol(NT), P, last=True)
            KG = XT // GROUPS
            pe.wait_ge(s_gate, NT + 1)
            for g in range(GROUPS):
                pe.wait_ge(s_gsq, KG * (g + 1))
                for h, cols in enumerate(WH):
                    for k in range(KG):
                        ins = mm(ps[:, 4 + 2 * g + h, 0:HALF], ones[:, :], gsq[:, KG * g + k, cols], start=k == 0,
                                 stop=k == KG - 1)
                ins.then_inc(s_gsum, 1)

            pe.wait_ge(s_mslo, KD)
            with pe.Fori(0, KD // 2) as i:
                for m in range(2):
                    c = i * 4 + (C_OUT + 2 * m)
                    pe.wait_ge(s_wlo, c + 1)
                    chunk(0, m, mixa_hi, mixa_lo, WH, last=False).then_inc(s_pe, 1)
                    pe.wait_ge(s_wlo, c + 2)
                    chunk(1, m, mixs_hi, mixs_lo, WH, first=False).then_inc(s_pe, 1)
            for t in range(NT + 1):
                w, b = rows(t), t % 2
                if t == 0:
                    pe.wait_ge(s_mixo, KD)
                if t >= 2:
                    pe.wait_ge(s_u, t - 1)
                for k in range(KD):
                    ins = nc.tensor.transpose(ps[0:w, 2 * b + k // 4, (k % 4) * P:(k % 4 + 1) * P],
                                              mixo[:, k, tcol(t)], ident[:, :])
                ins.then_inc(s_t1, 1)
            pe.wait_ge(s_u, NT + 1)
            for t in range(NT + 1):
                turn_rows(ffn, t)
            pe.wait_ge(ffn.lo, NT + 1)
            with pe.Fori(0, KF) as j:
                for b in range(2):
                    pe.wait_ge(s_wlo, j * 2 + (C_UP + 1 + b))
                    chunk(b, b, hn2_hi, hn2_lo, FH).then_inc(s_pe, 1)

            def down(slot, k, first=False, last=False):
                pe.wait_ge(s_wlo, k + (C_DOWN + 1))
                pe.wait_ge(s_stlo, k + 1)
                for t in range(NT):
                    for n in range(2):
                        w = slice(n * BANK, (n + 1) * BANK)
                        tk = slice(t * P, (t + 1) * P)
                        ins = three(ps[:, 2 * t + n, :], st_hi[slot][:, tk], st_lo[slot][:, tk], whi[slot][:, w],
                                    wlo[slot][:, w], first, last)
                    if last:
                        ins.then_inc(s_down, 1)
                if not last:
                    ins.then_inc(s_pe, 1)

            down(0, 0, first=True)
            down(1, 1)
            with pe.Fori(1, KF // 2 - 1) as i:
                for b in range(2):
                    down(b, i * 2 + b)
            down(0, KF - 2)
            down(1, KF - 1, last=True)


_INS = ['x', 'meta_tokens', 'norm_mix_pre', 'norm_mix_post', 'norm_ffn_pre', 'norm_ffn_post', 'w_in', 'q_a_norm',
        'w_uq', 'kv_a_norm', 'w_ukv', 'attn_out_norm', 'ssm_conv_w', 'ssm_conv_b', 'ssm_dt_bias', 'ssm_A_log',
        'ssm_D', 'ssm_norm', 'w_out', 'w_up', 'ffn_conv_w', 'ffn_conv_b', 'w_down']


def rope_rows(tokens, dim=64, theta=10000.0):
    import numpy as np

    f = np.float32
    inv = (f(theta) ** (-np.arange(0, dim, 2, dtype=f) / f(dim))).astype(f)
    ang = inv[:, None] * np.arange(tokens, dtype=f)[None, :]
    cos, sin = np.cos(ang).astype(f), np.sin(ang).astype(f)
    return np.ascontiguousarray(np.concatenate([cos] * 4)), np.ascontiguousarray(np.concatenate([-sin, sin] * 2))


def kernel(**inputs):
    import numpy as _np
    import concourse.bacc as _bacc
    from concourse import mybir as _mybir
    from concourse.bass_utils import run_bass_kernel_spmd as _run

    nc = _bacc.Bacc("TRN2", target_bir_lowering=False, num_devices=1)
    arrays, args = {}, []
    for name in _INS:
        a = _np.ascontiguousarray(inputs[name])
        arrays[f"in_{name}_dram"] = a
        args.append(nc.dram_tensor(f"in_{name}_dram", a.shape, _mybir.dt.from_np(a.dtype), kind="ExternalInput").ap())
    seq = inputs["x"].shape[1] + inputs["meta_tokens"].shape[0]
    for name, a in zip(("rope_cos", "rope_sin"), rope_rows(seq)):
        arrays[f"const_{name}"] = a
        args.append(nc.dram_tensor(f"const_{name}", a.shape, _mybir.dt.from_np(a.dtype), kind="ExternalInput").ap())
    out = nc.dram_tensor("out_0_dram", inputs["x"].shape, _mybir.dt.float32, kind="ExternalOutput").ap()
    hymba_layer(nc, *args, out)
    r = _run(nc, [arrays], core_ids=[0])
    return r.results[0]["out_0_dram"]
```

```python
from contextlib import ExitStack, contextmanager

import concourse.bass as bass
from concourse import mybir

F32 = mybir.dt.float32
F32R = mybir.dt.float32r
BF16 = mybir.dt.bfloat16
ALU = mybir.AluOpType
ACT = mybir.ActivationFunctionType
AX = mybir.AxisListType

P = 128
BANK = 512


class Chain:

    def __init__(self, engine, sem):
        self.engine, self.sem, self.base, self.steps = engine, sem, None, 0

    def add(self, ins):
        ins.then_inc(self.sem, 1)
        self.steps += 1
        return ins

    def wait(self):
        self.engine.wait_ge(self.sem, self.steps if self.base is None else self.base + self.steps)

    @contextmanager
    def loop(self, i, trips, per):
        before = self.steps
        self.base, self.steps = i * per, before
        yield
        assert self.steps - before == per, (self.steps - before, per)
        self.base, self.steps = None, before + per * trips


def hymba_layer(nc, x, meta_tokens, norm_mix_pre, norm_mix_post, norm_ffn_pre, norm_ffn_post, w_in,
                q_a_norm, w_uq, kv_a_norm, w_ukv, attn_out_norm, ssm_conv_w, ssm_conv_b, ssm_dt_bias,
                ssm_A_log, ssm_D, ssm_norm, w_out, w_up, ffn_conv_w, ffn_conv_b, w_down,
                rope_cos, rope_sin, out):
    SEQ, D = x.shape[1], x.shape[2]
    META = meta_tokens.shape[0]
    TOK = META + SEQ
    HALF = TOK // 2
    NT = SEQ // P
    KD = D // P
    D_IN = w_in.shape[2]
    R_Q, HEADS = w_uq.shape[1], w_uq.shape[2]
    R_KV = w_ukv.shape[1]
    KQ, KKV = R_Q // P, R_KV // P
    NOPE = 128
    ROPE = w_uq.shape[3] - NOPE
    DV = w_ukv.shape[3] - NOPE
    SCALE = float(NOPE + ROPE) ** -0.5
    SH = ssm_A_log.shape[1]
    D_SSM = ssm_norm.shape[1]
    SP = D_SSM // SH
    TAPS = ssm_conv_w.shape[1]
    D_XBC = ssm_conv_w.shape[2]
    STATE = 128
    GROUPS = (D_XBC - D_SSM) // 2 // STATE
    HG = SH // GROUPS
    GC = HG * SP
    CT = D_XBC // P
    XT = D_SSM // P
    D_FF = w_down.shape[1]
    KF = D_FF // P
    FTAPS = ffn_conv_w.shape[1]
    EPS = 1e-6
    NEG = -1e30
    assert (META, NT, KD, KQ, KKV, CT, KF, ROPE) == (16, 4, 8, 3, 2, 12, 22, 64)

    SLOT = 9 * P
    C_Z = 6
    C_XBC = C_Z + D_SSM // P
    C_ATT = C_XBC + CT
    PAIRS = HEADS // 2
    C_OUT = C_ATT + 2 * PAIRS
    C_UP = C_OUT + 2 * KD
    C_DOWN = C_UP + 2 * KF
    C_END = C_DOWN + KF

    def tcol(t):
        return slice(0, META) if t == 0 else slice(META + P * (t - 1), META + P * t)

    def rows(t):
        return META if t == 0 else P

    NF = SEQ + 4
    F0 = TOK - NF
    FH = (slice(F0, F0 + NF // 2), slice(F0 + NF // 2, TOK))
    WH = (slice(0, HALF), slice(HALF, TOK))

    wi = w_in[0].rearrange("(k p) n -> p k n", p=P)
    wq = w_uq[0].rearrange("(k p) h d -> p k h d", p=P)
    wkv = w_ukv[0].rearrange("(k p) h d -> p k h d", p=P)
    wo = w_out[0].rearrange("(k p) n -> p k n", p=P)
    wu = w_up[0].rearrange("(k p) n -> p k n", p=P)

    with ExitStack() as ctx:
        def sem(name):
            return ctx.enter_context(nc.semaphore(name))

        top = [(nc.sbuf_base + 63) // 64 * 64]

        def fixed(name, shape, dt):
            n = 4 if dt != BF16 else 2
            for s in shape[1:]:
                n *= s
            t = nc.alloc_sbuf_tensor_at(name, shape, dt, offset=top[0])
            top[0] += (n + 63) // 64 * 64
            return t

        wf = [fixed(f"weights_f32_{s}", [P, SLOT], F32) for s in range(2)]
        whi = [fixed(f"weights_hi_{s}", [P, SLOT], F32R) for s in range(2)]
        wlo = [fixed(f"weights_lo_{s}", [P, SLOT], F32R) for s in range(2)]
        h_tm = fixed("h_tm", [P, NT + 1, D], F32)
        ident = fixed("ident", [P, P], F32)
        ident_bf = fixed("ident_bf", [P, P], BF16)
        mask_bf = fixed("mask_bf", [P, P], BF16)
        swap = fixed("swap", [P, P], F32)
        dup = fixed("dup", [ROPE, P], F32)
        dupswap = fixed("dupswap", [ROPE, P], F32)
        ones = fixed("ones", [P, P], F32)
        PARTS3 = 96
        pick = fixed("pick", [PARTS3, SH], BF16)
        vec_rows = fixed("vec_rows", [P, 3, P], F32)
        vec = fixed("vec", [P, 3, 96], F32)
        gain_a = fixed("gain_a", [P, D], F32)
        gain_b = fixed("gain_b", [P, D], F32)
        before = top[0] - 4 * D
        smt = nc.alloc_sbuf_tensor_at("ssm_cols", [P, NT + 1, P], F32, offset=before)
        acs3 = nc.alloc_sbuf_tensor_at("acs_parts", [P, TOK], BF16, offset=before + 4 * (NT + 1) * P)
        dec_b = nc.alloc_sbuf_tensor_at("chunk_decay", [P, NT + 1, SH], F32, offset=before + 4 * (NT + 1) * P + 2 * TOK)
        skip_d = fixed("skip_d", [P, SH], F32)
        dt_small = fixed("dt_small", [SH, 4], F32)
        stat = fixed("stat", [P, 96], F32)
        xn = [fixed(f"normed_{i}", [P, D], F32) for i in range(2)]
        minus_acs = fixed("minus_acs", [P, NT + 1, SH], F32)
        dt_ends = fixed("dt_ends", [SH, NT + 1], F32)
        ends = fixed("chunk_ends", [SH, NT + 1, SH], F32)
        dtw = fixed("dt_weights", [P, KD, SH], F32)
        sm = fixed("ssm_rows", [P, TOK], F32)
        pool = top[0]
        spare = nc.sbuf_usable_end - pool

        def at(name, shape, dt, off):
            n = 4 if dt != BF16 else 2
            for s in shape[1:]:
                n *= s
            assert off + n <= spare, (name, off + n, spare)
            return nc.alloc_sbuf_tensor_at(name, shape, dt, offset=pool + off)

        TB = 4 * TOK
        AB = 4 * (NT + 1) * D
        O_QKV = (XT + CT) * TB
        O_W = O_QKV + 10 * TB
        z_silu = at("z_silu", [P, XT, TOK], F32, 0)
        xbc = at("xbc", [P, CT, TOK], F32, XT * TB)
        qkv_hi = at("qkv_hi", [P, KQ + KKV, TOK], F32R, O_QKV)
        qkv_lo = at("qkv_lo", [P, KQ + KKV, TOK], F32R, O_QKV + 5 * TB)
        hn_hi = at("hn_hi", [P, KD, TOK], F32R, O_W)
        hn_lo = at("hn_lo", [P, KD, TOK], F32R, O_W + 8 * TB)
        qkvk = at("qkvk", [P, C_Z, TOK], F32, O_W + 16 * TB)
        squares = at("squares", [P, KQ + KKV, TOK], F32, O_W + 22 * TB)
        acs_rest = [squares[0:SH, j, :] for j in range(3)]
        XPAD = TAPS - 1
        xpad = [at(f"xpad_{i}", [P, XPAD + TOK + 1], F32, O_W + 27 * TB + i * (TB + 32)) for i in range(2)]
        o = O_W + 29 * TB + 64
        conv = [at(f"conv_{i}", [P, TOK], F32, o + i * TB) for i in range(2)]
        rstd_f = at("rstd_f", [P, 2, TOK], F32, o + 2 * TB)
        attn = at("attn", [P, NT + 1, D], F32, O_W)
        o = O_W + AB
        O_MIXA = o
        PTB = 4 * (NT + 1) * P
        pt_hi = [at(f"pt_hi_{i}", [P, NT + 1, P], F32R, o + i * PTB) for i in range(2)]
        pt_lo = [at(f"pt_lo_{i}", [P, NT + 1, P], F32R, o + (2 + i) * PTB) for i in range(2)]
        o += 4 * PTB
        probs = [at(f"probs_{i}", [P, TOK], F32, o + i * TB) for i in range(2)]
        qn_hi = [at(f"qn_hi_{i}", [P, TOK], F32R, o + (2 + i) * TB) for i in range(2)]
        qn_lo = [at(f"qn_lo_{i}", [P, TOK], F32R, o + (4 + i) * TB) for i in range(2)]
        kn_hi = [at(f"kn_hi_{i}", [P, TOK], F32R, o + (6 + i) * TB) for i in range(2)]
        o += 8 * TB
        kpe_hi = at("kpe_hi", [P, TOK], F32R, o)
        kpe_lo = at("kpe_lo", [P, TOK], F32R, o + TB)
        kn_lo = [at(f"kn_lo_{i}", [P, TOK], F32R, o + (2 + i) * TB) for i in range(2)]
        qpe_hi = at("qpe_hi", [P, TOK], F32R, o + 4 * TB)
        qpe_lo = at("qpe_lo", [P, TOK], F32R, o + 5 * TB)
        o += 6 * TB
        v_parts = at("v_parts", [P, NT + 1, 2, 2, DV], F32R, o)
        o += 8 * (NT + 1) * 2 * DV
        cos_t = at("cos_t", [P, TOK], F32, o)
        sin_t = at("sin_t", [P, TOK], F32, o + TB)
        mixa_hi = at("mixa_hi", [P, KD, TOK], F32R, O_MIXA)
        mixa_lo = at("mixa_lo", [P, KD, TOK], F32R, O_MIXA + 8 * TB)
        gated = at("gated", [P, XT, TOK], F32, O_QKV)
        plan = [O_QKV + 8 * TB]

        def ssm(name, shape, dt=F32):
            n = 4
            for s in shape[1:]:
                n *= s
            if plan[0] < O_MIXA < plan[0] + n:
                plan[0] = O_MIXA + 16 * TB
            t = at(name, shape, dt, plan[0])
            plan[0] += (n + 31) // 32 * 32
            return t

        xbc_c = ssm("xbc_chunk", [P, CT, P])
        decay = ssm("decay", [P, SH, P])
        xdt = ssm("xdt", [P, D_SSM])
        xdte = ssm("xdte", [P, D_SSM])
        b_c = ssm("b_chunk", [P, GROUPS * STATE])
        y_tm = ssm("y_tm", [P, D_SSM])
        state = ssm("state", [P, D_SSM])
        gsq = at("gated_squares", [P, XT, TOK], F32, O_MIXA + 16 * TB)
        mixs_hi = at("mixs_hi", [P, KD, TOK], F32R, 0)
        mixs_lo = at("mixs_lo", [P, KD, TOK], F32R, 8 * TB)
        rstd_g = at("rstd_g", [P, GROUPS, TOK], F32, 16 * TB)
        normed_g = [at(f"normed_g_{i}", [P, TOK], F32, (18 + i) * TB) for i in range(2)]
        post = [at(f"post_{i}", [P, D], F32, (16 + 2 * i) * TB) for i in range(2)]
        squares_out = at("squares_out", [P, D], F32, 20 * TB)
        mixo = at("mixo", [P, KD, TOK], F32, 28 * TB)
        hn2_hi = at("hn2_hi", [P, KD, TOK], F32R, 40 * TB)
        hn2_lo = at("hn2_lo", [P, KD, TOK], F32R, 48 * TB)
        act = at("act", [P, KF, SEQ], F32, 0)
        o = 22 * TB
        u_gate = at("u_gate", [P, NF], F32, o)
        u_value = at("u_value", [P, NF], F32, o + TB)
        c_gate = at("conv_gate", [P, SEQ], F32, o + 2 * TB)
        c_value = at("conv_value", [P, SEQ], F32, o + 3 * TB)
        o = 30 * TB
        st_hi = [at(f"act_hi_{i}", [P, SEQ], F32R, o + i * TB) for i in range(2)]
        st_lo = [at(f"act_lo_{i}", [P, SEQ], F32R, o + (2 + i) * TB) for i in range(2)]
        junk = at("junk", [P, D], F32, 34 * TB)
        y_out = [at(f"y_out_{i}", [P, D], F32, (36 + 2 * i) * TB) for i in range(2)]

        ps = ctx.enter_context(nc.psum_tensor("ps", [P, 8, BANK], F32))

        s_x = [sem(f"x_landed_{t}") for t in range(NT + 1)]
        s_land = [sem(f"weights_landed_{s}") for s in range(2)]
        s_gain_pre, s_gain_att, s_gain_post, s_gain_ffn, s_gain_last = (
            sem(f"gain_{n}_landed") for n in ("pre", "attn", "post", "ffn", "last"))
        s_vec, s_small, s_rope_tab = sem("vectors_landed"), sem("small_landed"), sem("rope_landed")
        s_const = sem("constants_ready")
        s_act, s_dve, s_pool = sem("scalar_steps"), sem("vector_steps"), sem("pool_steps")
        s_whi, s_wlo, s_pe = sem("weights_hi_ready"), sem("weights_lo_ready"), sem("chunk_multiplied")
        s_vt, s_vec_ready = sem("vectors_transposed"), sem("vectors_ready")

        class Norm:

            def __init__(self, name, pair):
                self.pair = pair
                self.rstd, self.xn, self.turned, self.hi, self.lo = (
                    sem(f"{name}_{n}") for n in ("rstd", "scaled", "turned", "hi", "lo"))

        pre, att, ffn = Norm("pre", 0), Norm("attn_norm", 0), Norm("ffn_norm", 2)
        s_evac, s_sq, s_sumsq, s_rstdf = sem("qkvk_copied"), sem("squares_ready"), sem("sums_ready"), sem("rstd_f_ready")
        s_qkvn, s_qkvhi, s_qkvlo = sem("qkv_normed"), sem("qkv_hi_ready"), sem("qkv_lo_ready")
        s_xpad, s_conv, s_xbc = sem("xpad_filled"), sem("conv_done"), sem("xbc_ready")
        s_dtr, s_dtx, s_dtl, s_acs, s_exps = (
            sem(n) for n in ("dt_copied", "dt_biased", "dt_log_ready", "acs_ready", "acs_exps_ready"))
        s_sm, s_negA = sem("ssm_rows_ready"), sem("exp_A_ready")
        s_kpe, s_kper, s_kpehi, s_kpelo = (
            sem(n) for n in ("kpe_turned", "kpe_roped", "kpe_hi_ready", "kpe_lo_ready"))
        s_proj, s_rawcp, s_rope = sem("projections_done"), sem("rope_raw_copied"), sem("qpe_roped")
        s_phi, s_plo = sem("projections_hi"), sem("projections_lo")
        s_S, s_max, s_exp, s_T = sem("scores_ready"), sem("negmax_ready"), sem("probs_ready"), sem("probs_turned")
        s_pthi, s_ptlo, s_pv, s_attn = (
            sem(n) for n in ("probs_t_hi", "probs_t_lo", "pv_ready", "attn_stored"))
        s_smt, s_ends, s_dec, s_smt_ready, s_acs_copied, s_acs3 = (
            sem(n) for n in ("ssm_cols_turned", "ends_ready", "decay_summed", "ssm_cols_ready", "acs_copied",
                             "acs_parts_ready"))
        s_stage, s_xt, s_cb, s_ab, s_off, s_yd, s_st, s_yt = (
            sem(n) for n in ("chunk_staged", "xs_turned", "cb_ready", "acs_spread", "y_from_state",
                             "y_inside_ready",
                             "chunk_state_ready", "y_turned"))
        s_smtc, s_xs, s_xdt, s_xdte, s_xskip, s_yoff, s_ex, s_M = (
            sem(n) for n in ("chunk_cols_ready", "xs_copied", "xdt_ready", "xdte_ready", "xskip_ready",
                             "y_from_state_copied", "decays_ready", "mix_ready"))
        s_sdec = sem("state_decayed")
        s_acs3_zero = sem("acs_parts_zeroed")
        s_y, s_state, s_gate = sem("y_ready"), sem("state_ready"), sem("gated_ready")
        s_gsq, s_gsum, s_rg, s_ng, s_mshi, s_mslo = (
            sem(n) for n in ("gated_squares", "gated_sums", "rstd_g", "normed_g", "mixs_hi_ready", "mixs_lo_ready"))
        s_mixo, s_t1, s_rpost, s_u, s_h = (
            sem(n) for n in ("mix_out_copied", "mix_out_turned", "post_rstd", "post_scaled", "residual_ready"))
        s_ug, s_uv, s_cg, s_cv, s_silu, s_actr = (
            sem(n) for n in ("u_gate_copied", "u_value_copied", "conv_gate_done", "conv_value_done", "silu_ready",
                             "act_ready"))
        s_sthi, s_stlo, s_down, s_rlast, s_ylast, s_yout = (
            sem(n) for n in ("act_hi_ready", "act_lo_ready", "down_ready", "last_rstd", "last_scaled", "y_ready_out"))
        s_out = [sem(f"out_written_{i}") for i in range(2)]

        V_QA, V_KVA, V_SN, V_CW, V_CB = 0, KQ, KQ + KKV, KQ + KKV + XT, KQ + KKV + XT + TAPS * CT
        NV0 = V_CB + CT
        CF = 2 * KF
        ST_PRE, ST_ATT, ST_POST, ST_FFN, ST_LAST, ST_NM, ST_DEN, ST_RDEN, ST_EPS = 0, 10, 20, 30, 40, 50, 60, 70, 95
        R_DT, R_ACS, R_DTE, R_EXP = 0, 32, 64, 96
        UNITS = 2 * (NT + 1)
        eps = stat[:, ST_EPS:ST_EPS + 1]

        PARTS = 4

        def landed(turn):
            return turn * (16 * PARTS) + 16 * PARTS

        def turned(b, w):
            return ps[:, 2 * b:2 * b + 2, :].rearrange("p a (k w) -> p (a k) w", w=P)[:, :, 0:w]

        def pair(b, w=HALF):
            return ps[:, 2 * b:2 * b + 2, 0:w]

        def two(ap):
            return ap.rearrange("p (a b) -> p a b", a=2)

        def one(i):
            return slice(i, i + 1) if isinstance(i, int) else bass.ds(i, 1)

        def by_head(ap):
            return ap.rearrange("p (t h d) -> p t h d", h=2, d=DV)

        def dt_cols(t):
            return t[:, 0:KD * P].rearrange("p (k n) -> p k n", k=KD)[:, :, ROPE:ROPE + SH]

        def bcast(ap, shape):
            return ap.unsqueeze(2).broadcast_to(shape)

        def score_cols(u):
            t = u % (NT + 1)
            return META + P * t

        def score_view(u):
            n, r = score_cols(u), rows(u % (NT + 1))
            b = 2 * (u % 2)
            return ps[0:r, b, 0:n] if n <= BANK else ps[0:r, b:b + 2, 0:n // 2]

        def prob_view(u):
            n, r = score_cols(u), rows(u % (NT + 1))
            v = probs[u % 2][0:r, 0:n]
            return v if n <= BANK else v.rearrange("p (a b) -> p a b", a=2)

        block = ctx.enter_context(nc.Block())

        @block.sync
        def _(sp):
            def load(slot, dst, src, chunk, n=1):
                if chunk is not None:
                    sp.wait_ge(s_wlo, chunk - 1)
                sp.dma_start(dst, src).then_inc(s_land[slot], 16 * PARTS // n)

            def blocks(slot, k=KD, w=P):
                return wf[slot][:, 0:k * w].rearrange("p (k n) -> p k n", k=k)

            sp.dma_start(h_tm[0:META, 0, :], meta_tokens).then_inc(s_x[0], 16)
            for t in range(1, NT + 1):
                sp.dma_start(h_tm[:, t, :], x[0, P * (t - 1):P * t, :]).then_inc(s_x[t], 16)
            for c in range(2):
                load(c, blocks(c), wi[:, :, P * c:P * (c + 1)], None)

            def vector_rows(k, r0, src, n):
                sp.dma_start(vec_rows[r0:r0 + n, k, :], src.rearrange("(n p) -> n p", p=P)).then_inc(s_vec, 16)

            vector_rows(0, V_QA, q_a_norm[0], KQ)
            vector_rows(0, V_KVA, kv_a_norm[0], KKV)
            vector_rows(0, V_SN, ssm_norm[0], XT)
            vector_rows(0, V_CB, ssm_conv_b[0], CT)
            for w in range(TAPS):
                vector_rows(0, V_CW + w * CT, ssm_conv_w[0, w], CT)
            for w in range(2):
                vector_rows(1, w * CF, ffn_conv_w[0, w], CF)
            vector_rows(2, 0, ffn_conv_w[0, 2], CF)
            vector_rows(2, CF, ffn_conv_b[0], CF)
            sp.dma_start(dtw[:, :, :], wi[:, :, D_IN - SH:D_IN]).then_inc(s_small, 16)
            sp.dma_start(dt_small[:, 0:1], ssm_dt_bias.rearrange("a h -> h a")).then_inc(s_small, 16)
            sp.dma_start(dt_small[:, 1:2], ssm_A_log.rearrange("a h -> h a")).then_inc(s_small, 16)
            sp.dma_start(skip_d[:, :], ssm_D[0:1, :].broadcast_to([P, SH])).then_inc(s_small, 16)
            sp.dma_start(cos_t[:, :], rope_cos).then_inc(s_rope_tab, 16)
            sp.dma_start(sin_t[:, :], rope_sin).then_inc(s_rope_tab, 16)

            with sp.Fori(1, C_Z // 2) as i:
                for b in range(2):
                    load(b, blocks(b), wi[:, :, bass.ds(i * (2 * P) + b * P, P)], i * 2 + b)
            with sp.Fori(C_Z // 2, C_ATT // 2) as i:
                for b in range(2):
                    load(b, blocks(b), wi[:, :, bass.ds(i * (2 * P) + (b * P - (P - ROPE)), P)], i * 2 + b)
            with sp.Fori(0, PAIRS) as i:
                c = C_ATT + i * 2
                for hh in range(2):
                    h = i * 2 + hh
                    load(0, wf[0][:, hh * KQ * P:(hh + 1) * KQ * P].rearrange("p (k n) -> p k n", k=KQ),
                         wq[:, :, h, 0:NOPE], c if hh == 0 else None, PARTS)
                    load(0, wf[0][:, 2 * KQ * P:3 * KQ * P].rearrange("p (k n) -> p k n", k=KQ)
                         [:, :, hh * ROPE:(hh + 1) * ROPE], wq[:, :, h, NOPE:NOPE + ROPE], None, PARTS)
                for hh in range(2):
                    h = i * 2 + hh
                    load(1, wf[1][:, hh * KKV * P:(hh + 1) * KKV * P].rearrange("p (k n) -> p k n", k=KKV),
                         wkv[:, :, h, 0:NOPE], c + 1 if hh == 0 else None, PARTS)
                    load(1, wf[1][:, 2 * KKV * P:4 * KKV * P].rearrange("p (k n) -> p k n", k=KKV)
                         [:, :, hh * DV:(hh + 1) * DV], wkv[:, :, h, NOPE:NOPE + DV], None, PARTS)
            with sp.Fori(0, KD // 2) as i:
                for half in range(2):
                    for b in range(2):
                        load(b, blocks(b), wo[:, KD * half:KD * (half + 1), bass.ds(i * (2 * P) + b * P, P)],
                             i * 4 + (C_OUT + 2 * half + b))
            with sp.Fori(0, KF) as j:
                for b in range(2):
                    load(b, blocks(b), wu[:, :, bass.ds(j * P + b * D_FF, P)], C_UP + j * 2 + b)
            with sp.Fori(0, KF // 2) as i:
                for b in range(2):
                    load(b, wf[b][:, 0:D], w_down[0, bass.ds(i * (2 * P) + b * P, P), :], C_DOWN + i * 2 + b)
            for t in range(NT):
                sp.wait_ge(s_yout, t + 1)
                sp.dma_start(out[0, P * t:P * (t + 1), :], y_out[t % 2][:, :]).then_inc(s_out[t % 2], 16)
            for b in range(2):
                sp.wait_ge(s_out[b], 16 * (NT // 2))

        @block.gpsimd
        def _(pool):
            steps = Chain(pool, s_pool)
            for s in range(2):
                steps.add(pool.memset(wf[s][:, KD * P:SLOT], 0.0))
            steps.add(pool.memset(ident[:, :], 0.0))
            for t in (ident_bf, mask_bf, sm, ones):
                steps.add(pool.memset(t[:, :], 1.0 if t is ones else 0.0))
            steps.add(pool.memset(stat[:, ST_EPS:ST_EPS + 1], EPS))
            steps.wait()
            for t in (ident, ident_bf):
                steps.add(pool.affine_select(out=t[:, :], in_=t[:, :], compare_op=ALU.not_equal, fill=1.0, base=0,
                                             pattern=[[-1, P]], channel_multiplier=1))
            steps.add(pool.affine_select(out=mask_bf[:, :], in_=mask_bf[:, :], compare_op=ALU.is_ge, fill=NEG, base=0,
                                         pattern=[[-1, P]], channel_multiplier=1))
            steps.wait()
            H2 = ROPE // 2
            for b in range(P // H2):
                steps.add(pool.tensor_copy(swap[:, b * H2:(b + 1) * H2], ident[:, (b ^ 1) * H2:((b ^ 1) + 1) * H2]))
            for b in range(2):
                steps.add(pool.tensor_copy(dup[:, b * ROPE:(b + 1) * ROPE], ident[0:ROPE, 0:ROPE]))
            steps.add(pool.tensor_tensor(pick[:, :], ident[0:PARTS3, 0:SH], ident[0:PARTS3, 32:32 + SH], ALU.add))
            steps.wait()
            steps.add(pool.tensor_tensor(pick[:, :], pick[:, :], ident[0:PARTS3, 64:64 + SH], ALU.add))
            for b in range(2):
                steps.add(pool.tensor_copy(dupswap[:, b * ROPE:(b + 1) * ROPE], swap[0:ROPE, 0:ROPE]))
            steps.wait()
            pool.memset(xpad[0][:, 0:XPAD], 0.0).then_inc(s_const, 1)
            pool.memset(xpad[1][:, 0:XPAD], 0.0).then_inc(s_const, 1)
            pool.wait_ge(pre.xn, NT + 1)
            pool.dma_start(gain_a[:, :], attn_out_norm[0:1, :].broadcast_to([P, D])).then_inc(s_gain_att, 16)
            pool.wait_ge(att.xn, NT + 1)
            pool.dma_start(gain_a[:, :], norm_mix_post[0:1, :].broadcast_to([P, D])).then_inc(s_gain_post, 16)

            def heads(ap, w=P):
                return ap.rearrange("p (h e) -> p h e", e=SP)

            def chunk(q, w):
                first = isinstance(q, int)
                pool.wait_ge(s_xs, q + 1)
                if not first:
                    pool.wait_ge(s_y, q)
                pool.tensor_tensor(heads(xn[1][0:w, :], w), heads(xn[0][0:w, :], w),
                                   bcast(skip_d[0:w, :], [w, SH, SP]), ALU.mult).then_inc(s_xskip, 1)
                if not first:
                    pool.wait_ge(s_off, q)
                    pool.tensor_tensor(heads(state[:, :]), heads(state[:, :]),
                                       bcast(dec_b[:, q, :], [P, SH, SP]), ALU.mult).then_inc(s_sdec, 1)

            pool.wait_ge(s_small, 16 * 4)
            chunk(0, META)
            with pool.Fori(1, NT + 1) as q:
                chunk(q, P)
            pool.wait_ge(s_gate, NT + 1)
            pool.dma_start(gain_b[:, :], norm_ffn_pre[0:1, :].broadcast_to([P, D])).then_inc(s_gain_ffn, 16)
            for t in range(NT + 1):
                pool.wait_ge(s_u, t + 1)
                n = rows(t)
                pool.tensor_tensor(h_tm[0:n, t, :], h_tm[0:n, t, :], post[t % 2][0:n, :], ALU.add).then_inc(s_h, 1)
            pool.dma_start(gain_a[:, :], norm_ffn_post[0:1, :].broadcast_to([P, D])).then_inc(s_gain_last, 16)
            pool.wait_ge(s_gain_last, 16)

        @block.scalar
        def _(act_e):
            sc = nc.scalar
            steps = Chain(act_e, s_act)

            def split_hi(slot, chunk, turn, width=KD * P):
                act_e.wait_ge(s_land[slot], landed(turn))
                if not (isinstance(chunk, int) and chunk < 2):
                    act_e.wait_ge(s_pe, chunk - 1)
                if isinstance(chunk, int) and chunk == 5:
                    steps.add(sc.activation(whi[slot][:, 0:width], wf[slot][:, 0:width], ACT.Copy))
                    act_e.wait_ge(s_small, 16 * 4)
                    steps.wait()
                    sc.activation(dt_cols(whi[slot]), dtw[:, :, :], ACT.Copy).then_inc(s_whi, 1)
                else:
                    sc.activation(whi[slot][:, 0:width], wf[slot][:, 0:width], ACT.Copy).then_inc(s_whi, 1)

            def rstd(src, n, col, done, scale, junk_out):
                steps.add(sc.activation(junk_out, src, ACT.Square, accum_out=stat[0:n, col:col + 1]))
                steps.wait()
                steps.add(sc.activation(stat[0:n, col:col + 1], stat[0:n, col:col + 1], ACT.Ln, scale=scale,
                                        bias=eps[0:n]))
                steps.wait()
                sc.activation(stat[0:n, col + 5:col + 6], stat[0:n, col:col + 1], ACT.Exp, scale=-0.5).then_inc(done, 1)

            def turned_hi(norm, t, dst):
                act_e.wait_ge(norm.turned, t + 1)
                w, b = rows(t), norm.pair + t % 2
                sc.activation(dst[:, :, tcol(t)], turned(b, w), ACT.Copy).then_inc(norm.hi, 1)

            for dst, src, s in ((gain_a, norm_mix_pre, s_gain_pre),):
                act_e.dma_start(dst[:, :], src[0:1, :].broadcast_to([P, D])).then_inc(s, 16)

            sc.preload_act_table_set("natural_log_exp_and_others")
            act_e.wait_ge(s_const, 2)
            for s in range(NT + 3):
                if s <= NT:
                    act_e.wait_ge(s_x[s], 16)
                    rstd(two(h_tm[0:rows(s), s, :]), rows(s), ST_PRE + s, pre.rstd, 1.0 / D, ps[0:rows(s), 6:8, :])
                if s >= 2:
                    turned_hi(pre, s - 2, hn_hi)
                if s == NT:
                    split_hi(0, 0, 0)
            act_e.wait_ge(s_vt, 1)
            sc.activation(vec[:, 0, 0:NV0], ps[:, 4, 0:NV0], ACT.Copy).then_inc(s_vec_ready, 1)
            sc.activation(vec[:, 1:3, 0:2 * CF], ps[:, 4, 96:3 * 96].rearrange("p (a b) -> p a b", a=2)[:, :, 0:2 * CF],
                          ACT.Copy).then_inc(s_vec_ready, 1)
            split_hi(1, 1, 0)

            for c in range(C_Z):
                act_e.wait_ge(s_pe, c + 1)
                sc.activation(two(qkvk[:, c, :]), pair(c % 2), ACT.Copy).then_inc(s_evac, 1)
                split_hi(c % 2, c + 2, (c + 2) // 2)
                if c < KQ + KKV:
                    act_e.wait_ge(s_evac, c + 1)
                    sc.activation(squares[:, c, :], qkvk[:, c, :], ACT.Square).then_inc(s_sq, 1)
            act_e.wait_ge(s_evac, C_Z)
            sc.activation(xn[0][0:SH, 0:TOK], qkvk[ROPE:ROPE + SH, C_Z - 1, :], ACT.Copy).then_inc(s_dtr, 1)
            for g, (n, b) in enumerate(((R_Q, 2), (R_KV, 3))):
                act_e.wait_ge(s_sumsq, g + 1)
                steps.add(sc.activation(two(rstd_f[:, g, :]), pair(b), ACT.Ln, scale=1.0 / n, bias=eps))
                steps.wait()
                sc.activation(rstd_f[:, g, :], rstd_f[:, g, :], ACT.Exp, scale=-0.5).then_inc(s_rstdf, 1)
            act_e.wait_ge(s_dtx, 2)
            steps.add(sc.activation(xn[0][0:SH, 0:TOK], xn[1][0:SH, 0:TOK], ACT.Abs))
            steps.wait()
            steps.add(sc.activation(xn[0][0:SH, 0:TOK], xn[0][0:SH, 0:TOK], ACT.Exp, scale=-1.0))
            steps.wait()
            sc.activation(xn[0][0:SH, 0:TOK], xn[0][0:SH, 0:TOK], ACT.Ln, bias=1.0).then_inc(s_dtl, 1)
            sc.activation(dt_small[:, 2:3], dt_small[:, 1:2], ACT.Exp).then_inc(s_negA, 1)
            for j in range(KQ + KKV):
                act_e.wait_ge(s_qkvn, j + 1)
                sc.activation(qkv_hi[:, j, :], qkvk[:, j, :], ACT.Copy).then_inc(s_qkvhi, 1)
            act_e.wait_ge(s_acs, NT + 1)
            for t in range(NT + 1):
                c = tcol(t)
                steps.add(sc.activation(xn[1][0:SH, c], xn[0][0:SH, c], ACT.Exp, scale=-1.0,
                                        bias=xn[0][0:SH, c.stop - 1:c.stop]))
            sc.activation(sm[R_EXP:R_EXP + SH, :], xn[0][0:SH, 0:TOK], ACT.Exp).then_inc(s_exps, 1)
            for j in range(3):
                if j:
                    act_e.wait_ge(s_acs3, j)
                else:
                    act_e.wait_ge(s_acs3_zero, 1)
                sc.activation(acs3[32 * j:32 * j + SH, :], acs_rest[j] if j else xn[0][0:SH, 0:TOK], ACT.Copy)\
                    .then_inc(s_acs_copied, 1)

            sc.preload_act_table(ACT.Silu)
            with act_e.Fori(0, XT // 2) as i:
                for b in range(2):
                    c = i * 2 + (C_Z + b)
                    act_e.wait_ge(s_pe, c + 1)
                    sc.activation(two(z_silu[:, i * 2 + b, :]), pair(b), ACT.Silu)
                    split_hi(b, c + 2, i + (C_Z // 2 + 1))
            act_e.wait_ge(s_smt, 1)
            sc.activation(smt[0:META, 0, :], ps[0:META, 4, 0:P], ACT.Copy)
            sc.activation(smt[:, 1:NT + 1, :], ps[:, 5, :].rearrange("p (a b) -> p a b", b=P), ACT.Copy)\
                .then_inc(s_smt_ready, 1)
            act_e.wait_ge(s_dec, 1)
            sc.activation(dec_b[:, :, :], ps[:, 6, 0:(NT + 1) * SH].rearrange("p (a b) -> p a b", b=SH), ACT.Copy)\
                .then_inc(s_smt_ready, 1)
            with act_e.Fori(0, CT // 2) as i:
                for b in range(2):
                    c = i * 2 + (C_XBC + b)
                    act_e.wait_ge(s_pe, c + 1)
                    sc.activation(two(xpad[b][:, XPAD:XPAD + TOK]), pair(b), ACT.Copy).then_inc(s_xpad, 1)
                    split_hi(b, c + 2, i + (C_XBC // 2 + 1), SLOT)
                    act_e.wait_ge(s_conv, i * 2 + (b + 1))
                    sc.activation(xbc[:, i * 2 + b, :], conv[b][:, :], ACT.Silu).then_inc(s_xbc, 1)

            sc.preload_act_table_set("natural_log_exp_and_others")
            act_e.wait_ge(s_kper, 1)
            sc.activation(kpe_hi[:, :], probs[0][:, :], ACT.Copy).then_inc(s_kpehi, 1)

            with act_e.Fori(0, PAIRS) as i:
                def hi(dst, src, n):
                    if n:
                        act_e.wait_ge(s_proj, i * 6 + n)
                    sc.activation(dst, src, ACT.Copy).then_inc(s_phi, 1)

                hi(two(qn_hi[0][:, :]), pair(0), 1)
                hi(two(qn_hi[1][:, :]), pair(1), 2)
                act_e.wait_ge(s_proj, i * 6 + 3)
                sc.activation(two(xn[0][:, 0:TOK]), pair(2), ACT.Copy).then_inc(s_rawcp, 1)
                hi(two(kn_hi[0][:, :]), pair(3), 4)
                act_e.wait_ge(s_rope, i + 1)
                hi(qpe_hi[:, :], probs[0][:, :], 0)
                hi(two(kn_hi[1][:, :]), pair(0), 6)
                act_e.wait_ge(s_pe, i * 2 + (C_ATT + 2))
                hi(v_parts[:, 0:2, :, 0, :], by_head(ps[:, 2, :]), 0)
                hi(v_parts[:, 2:4, :, 0, :], by_head(ps[:, 3, :]), 0)
                hi(v_parts[:, 4:5, :, 0, :], by_head(ps[:, 6, 0:2 * DV]), 0)
                for s in range(UNITS + 3):
                    if s in (4, 6):
                        b = (s - 4) // 2
                        split_hi(b, i * 2 + (C_ATT + 2 + b), i + (C_ATT // 2 + 1), SLOT)
                    if 2 <= s < UNITS + 2:
                        u = s - 2
                        t, r = u % (NT + 1), rows(u % (NT + 1))
                        act_e.wait_ge(s_T, i * UNITS + (u + 1))
                        ins = sc.activation(pt_hi[u % 2][0:META, 0, :], ps[0:META, 4, 0:P], ACT.Copy)
                        if t:
                            ins = sc.activation(pt_hi[u % 2][:, 1:t + 1, :], turned(2, P)[:, 1:t + 1, :], ACT.Copy)
                        ins.then_inc(s_pthi, 1)
                    if s < UNITS:
                        r = rows(s % (NT + 1))
                        act_e.wait_ge(s_max, i * UNITS + (s + 1))
                        sc.activation(prob_view(s), score_view(s), ACT.Exp, scale=SCALE,
                                      bias=stat[0:r, ST_NM + s:ST_NM + s + 1],
                                      accum_out=stat[0:r, ST_DEN + s:ST_DEN + s + 1]).then_inc(s_exp, 1)

            act_e.wait_ge(s_attn, PAIRS * UNITS)
            for s in range(NT + 3):
                if s <= NT:
                    rstd(two(attn[0:rows(s), s, :]), rows(s), ST_ATT + s, att.rstd, 1.0 / D, ps[0:rows(s), 6:8, :])
                if s >= 2:
                    turned_hi(att, s - 2, mixa_hi)

            def stage(q, cols, w):
                sc.activation(xbc_c[:, :, 0:w], xbc[:, :, cols], ACT.Copy).then_inc(s_stage, 1)

            def decays(q, w):
                for h in range(SH):
                    if h % 4 == 0:
                        act_e.wait_ge(s_ab, q * 4 + (h // 4 + 1))
                    ins = sc.activation(decay[0:w, h, 0:w], ps[0:w, 4 + h // 4, (h % 4) * P:(h % 4) * P + w], ACT.Exp,
                                        bias=minus_acs[0:w, q, h:h + 1])
                    if h % 4 == 3:
                        ins.then_inc(s_ex, 1)

            def chunk(q, w, following):
                first = isinstance(q, int) and q == 0
                act_e.wait_ge(s_xt, q + 1)
                if not first:
                    for s in (s_xdte, s_xskip):
                        act_e.wait_ge(s, q)
                sc.activation(two(xn[0][0:w, :]), ps[0:w, 0:2, :], ACT.Copy)
                sc.activation(b_c[0:w, :], ps[0:w, 2, 0:GROUPS * STATE], ACT.Copy).then_inc(s_xs, 1)
                if following is not None:
                    act_e.wait_ge(s_cb if first else s_off, 1 if first else q)
                    stage(q + 1, following, P)
                    decays(q + 1, P)

            def after(q):
                return bass.ds(q * P + META, P) if not isinstance(q, int) else slice(q * P + META, (q + 1) * P + META)

            act_e.wait_ge(s_xbc, CT)
            stage(0, slice(0, META), META)
            act_e.wait_ge(s_smtc, 1)
            decays(0, META)
            chunk(0, META, after(0))
            with act_e.Fori(1, NT) as q:
                chunk(q, P, after(q))
            chunk(NT, P, None)

            act_e.wait_ge(s_gate, NT + 1)
            for k in range(XT):
                sc.activation(gsq[:, k, :], gated[:, k, :], ACT.Square).then_inc(s_gsq, 1)
            for g in range(GROUPS):
                act_e.wait_ge(s_gsum, g + 1)
                steps.add(sc.activation(two(rstd_g[:, g, :]), pair(2 + g), ACT.Ln, scale=1.0 / GC, bias=eps))
                steps.wait()
                sc.activation(rstd_g[:, g, :], rstd_g[:, g, :], ACT.Exp, scale=-0.5).then_inc(s_rg, 1)
                if g == 0:
                    split_hi(0, C_OUT + 2, C_OUT // 2 + 1)
                for k in range(g * (XT // GROUPS), (g + 1) * (XT // GROUPS)):
                    act_e.wait_ge(s_ng, k + 1)
                    sc.activation(mixs_hi[:, k, :], normed_g[k % 2][:, :], ACT.Copy).then_inc(s_mshi, 1)
            split_hi(1, C_OUT + 3, C_OUT // 2 + 1)

            def out_pair(i, first=False):
                c = i * 4 + C_OUT
                if not first:
                    for b in range(2):
                        split_hi(b, c + 2 + b, i * 2 + (C_OUT // 2 + 1))
                for m in range(2):
                    act_e.wait_ge(s_pe, c + 3 + m)
                    sc.activation(two(mixo[:, i * 2 + m, :]), pair(m), ACT.Copy).then_inc(s_mixo, 1)
                    split_hi(m, c + 4 + m, i * 2 + (C_OUT // 2 + 2))

            out_pair(0, first=True)
            with act_e.Fori(1, KD // 2) as i:
                out_pair(i)
            for s in range(NT + 3):
                if s <= NT:
                    n = rows(s)
                    act_e.wait_ge(s_t1, s + 1)
                    rstd(ps[0:n, 2 * (s % 2):2 * (s % 2) + 2, :], n, ST_POST + s, s_rpost, 1.0 / D,
                         two(squares_out[0:n, :]))
                if 1 <= s <= NT + 1:
                    t = s - 1
                    act_e.wait_ge(s_h, t + 1)
                    rstd(h_tm[0:rows(t), t, :], rows(t), ST_FFN + t, ffn.rstd, 1.0 / D, squares_out[0:rows(t), :])
                if s >= 2:
                    turned_hi(ffn, s - 2, hn2_hi)

            sc.preload_act_table(ACT.Silu)
            def stage_hi(slot, k, first=False):
                if not first:
                    act_e.wait_ge(s_pe, k + (C_DOWN - 1))
                sc.activation(st_hi[slot][:, :], act[:, k, :], ACT.Copy).then_inc(s_sthi, 1)

            def up_block(j):
                for b, (u, done) in enumerate(((u_gate, s_ug), (u_value, s_uv))):
                    c = j * 2 + (C_UP + b)
                    act_e.wait_ge(s_pe, c + 1)
                    sc.activation(two(u[:, :]), pair(b, NF // 2), ACT.Copy).then_inc(done, 1)
                    split_hi(b, c + 2, j + (C_UP // 2 + 1))
                act_e.wait_ge(s_cg, j + 1)
                sc.activation(c_gate[:, :], c_gate[:, :], ACT.Silu).then_inc(s_silu, 1)

            with act_e.Fori(0, KF - 1) as j:
                up_block(j)
            for k in range(2):
                act_e.wait_ge(s_actr, k + 1)
                stage_hi(k, k, True)
            up_block(KF - 1)
            act_e.wait_ge(s_actr, KF)

            with act_e.Fori(0, KF // 2 - 1) as i:
                for b in range(2):
                    stage_hi(b, i * 2 + (2 + b))
                    split_hi(b, i * 2 + (C_DOWN + 2 + b), i + (C_DOWN // 2 + 1))
            sc.preload_act_table_set("natural_log_exp_and_others")
            for t in range(NT):
                act_e.wait_ge(s_down, t + 1)
                rstd(ps[:, 2 * t:2 * t + 2, :], P, ST_LAST + t, s_rlast, 1.0 / D, two(junk[:, :]))

        @block.vector
        def _(dve):
            ve = nc.vector
            steps = Chain(dve, s_dve)

            def split_lo(slot, chunk, width=KD * P):
                dve.wait_ge(s_whi, chunk + 1)
                whole = slice(0, width)
                if isinstance(chunk, int) and chunk == 5:
                    steps.add(ve.tensor_tensor(wlo[slot][:, whole], wf[slot][:, whole],
                                               whi[slot][:, whole].bitcast(F32), ALU.subtract))
                    dve.wait_ge(s_small, 16 * 4)
                    steps.wait()
                    ve.tensor_tensor(dt_cols(wlo[slot]), dtw[:, :, :], dt_cols(whi[slot]).bitcast(F32),
                                     ALU.subtract).then_inc(s_wlo, 1)
                else:
                    ve.tensor_tensor(wlo[slot][:, whole], wf[slot][:, whole], whi[slot][:, whole].bitcast(F32),
                                     ALU.subtract).then_inc(s_wlo, 1)

            def scale_rows(norm, t, src, col, gain):
                n = rows(t)
                dve.wait_ge(norm.rstd, t + 1)
                if t >= 2:
                    dve.wait_ge(norm.turned, t - 1)
                ve.scalar_tensor_tensor(xn[t % 2][0:n, :], src, stat[0:n, col + 5 + t:col + 6 + t], gain[0:n, :],
                                        ALU.mult, ALU.mult).then_inc(norm.xn, 1)

            def turned_lo(norm, t, dst, upper):
                dve.wait_ge(norm.hi, t + 1)
                w, b = rows(t), norm.pair + t % 2
                ve.tensor_tensor(dst[:, :, tcol(t)], turned(b, w), upper[:, :, tcol(t)].bitcast(F32),
                                 ALU.subtract).then_inc(norm.lo, 1)

            def norm_rows(norm, src, col, gain, upper, lower):
                for t in range(NT + 2):
                    if t <= NT:
                        scale_rows(norm, t, src[0:rows(t), t, :], col, gain)
                    if t:
                        turned_lo(norm, t - 1, lower, upper)

            dve.wait_ge(s_gain_pre, 16)
            norm_rows(pre, h_tm, ST_PRE, gain_a, hn_hi, hn_lo)
            split_lo(0, 0)
            split_lo(1, 1)
            for c in range(C_Z):
                split_lo(c % 2, c + 2)

            dve.wait_ge(s_dtr, 1)
            ve.tensor_scalar(xn[1][0:SH, 0:TOK], xn[0][0:SH, 0:TOK], dt_small[:, 0:1], None, ALU.add).then_inc(s_dtx, 1)
            dve.wait_ge(s_dtx, 1)
            ve.tensor_scalar(sm[R_DT:R_DT + SH, :], xn[1][0:SH, 0:TOK], 0.0, None, ALU.max).then_inc(s_dtx, 1)
            dve.wait_ge(s_vec_ready, 2)
            for j in range(KQ + KKV):
                g = int(j >= KQ)
                dve.wait_ge(s_rstdf, g + 1)
                ve.scalar_tensor_tensor(qkvk[:, j, :], qkvk[:, j, :], vec[:, 0, V_QA + j:V_QA + j + 1],
                                        rstd_f[:, g, :], ALU.mult, ALU.mult).then_inc(s_qkvn, 1)
            dve.wait_ge(s_dtl, 1)
            steps.add(ve.tensor_tensor(sm[R_DT:R_DT + SH, :], sm[R_DT:R_DT + SH, :], xn[0][0:SH, 0:TOK], ALU.add))
            dve.wait_ge(s_negA, 1)
            steps.wait()
            steps.add(ve.tensor_scalar(xn[1][0:SH, 0:TOK], sm[R_DT:R_DT + SH, :], dt_small[:, 2:3], -1.0, ALU.mult,
                                       ALU.mult))
            steps.wait()
            for t in range(NT + 1):
                c = tcol(t)
                ve.tensor_tensor_scan(xn[0][0:SH, c], ones[0:SH, 0:rows(t)], xn[1][0:SH, c], 0.0, ALU.mult,
                                      ALU.add).then_inc(s_acs, 1)
            ve.memset(acs3[:, :], 0.0).then_inc(s_acs3_zero, 1)
            dve.wait_ge(s_acs, NT + 1)
            steps.add(ve.tensor_copy(sm[R_ACS:R_ACS + SH, :], xn[0][0:SH, 0:TOK]))
            for j in range(KQ + KKV):
                dve.wait_ge(s_qkvhi, j + 1)
                ve.tensor_tensor(qkv_lo[:, j, :], qkvk[:, j, :], qkv_hi[:, j, :].bitcast(F32),
                                 ALU.subtract).then_inc(s_qkvlo, 1)
            dve.wait_ge(s_exps, 1)
            ve.tensor_tensor(sm[R_DTE:R_DTE + SH, :], sm[R_DT:R_DT + SH, :], xn[1][0:SH, 0:TOK],
                             ALU.mult).then_inc(s_sm, 1)
            dve.wait_ge(s_sm, 1)
            steps.add(ve.tensor_copy(dt_ends[:, 0:1], sm[R_EXP:R_EXP + SH, META - 1:META]))
            steps.add(ve.tensor_copy(dt_ends[:, 1:NT + 1], sm[R_EXP:R_EXP + SH, META + P - 1:TOK:P]))
            steps.wait()
            ve.tensor_tensor(ends[:, :, :], bcast(dt_ends[:, :], [SH, NT + 1, SH]),
                             ident[0:SH, 0:SH].unsqueeze(1).broadcast_to([SH, NT + 1, SH]),
                             ALU.mult).then_inc(s_ends, 1)
            for j in range(2):
                dve.wait_ge(s_acs_copied, j + 1)
                ve.tensor_tensor(acs_rest[j + 1], acs_rest[j] if j else xn[0][0:SH, 0:TOK],
                                 acs3[32 * j:32 * j + SH, :], ALU.subtract).then_inc(s_acs3, 1)

            with dve.Fori(0, XT // 2) as i:
                for b in range(2):
                    split_lo(b, i * 2 + (C_Z + 2 + b))

            dve.wait_ge(s_smt_ready, 1)
            ve.tensor_scalar(minus_acs[0:META, 0, :], smt[0:META, 0, R_ACS:R_ACS + SH], -1.0, None, ALU.mult)
            ve.tensor_scalar(minus_acs[:, 1:NT + 1, :], smt[:, 1:NT + 1, R_ACS:R_ACS + SH], -1.0, None, ALU.mult)\
                .then_inc(s_smtc, 1)
            with dve.Fori(0, CT // 2) as i, steps.loop(i, CT // 2, 2 * (TAPS - 1)):
                for b in range(2):
                    t = i * 2 + b
                    dve.wait_ge(s_xpad, t + 1)

                    def tap(w):
                        return vec[:, 0, bass.ds(t + (V_CW + w * CT), 1)]

                    steps.add(ve.tensor_scalar(conv[b][:, :], xpad[b][:, XPAD:XPAD + TOK], tap(XPAD),
                                               vec[:, 0, bass.ds(t + V_CB, 1)], ALU.mult, ALU.add))
                    for w in range(XPAD):
                        steps.wait()
                        ins = ve.scalar_tensor_tensor(conv[b][:, :], xpad[b][:, w:w + TOK], tap(w), conv[b][:, :],
                                                      ALU.mult, ALU.add)
                        if w < XPAD - 1:
                            steps.add(ins)
                        else:
                            ins.then_inc(s_conv, 1)
                    split_lo(b, t + (C_XBC + 2), SLOT)

            dve.wait_ge(s_kpe, 1)
            dve.wait_ge(s_rope_tab, 32)
            steps.add(ve.tensor_tensor(two(probs[0][:, :]), pair(2), two(cos_t[:, :]), ALU.mult))
            steps.add(ve.tensor_tensor(two(probs[1][:, :]), pair(3), two(sin_t[:, :]), ALU.mult))
            steps.wait()
            ve.tensor_tensor(probs[0][:, :], probs[0][:, :], probs[1][:, :], ALU.add).then_inc(s_kper, 1)
            dve.wait_ge(s_kpehi, 1)
            ve.tensor_tensor(kpe_lo[:, :], probs[0][:, :], kpe_hi[:, :].bitcast(F32), ALU.subtract).then_inc(s_kpelo, 1)

            with dve.Fori(0, PAIRS) as i, steps.loop(i, PAIRS, 2 + 3 * UNITS):
                def lo(dst, src, upper, n):
                    dve.wait_ge(s_phi, i * 8 + n)
                    ve.tensor_tensor(dst, src, upper.bitcast(F32), ALU.subtract).then_inc(s_plo, 1)

                lo(two(qn_lo[0][:, :]), pair(0), two(qn_hi[0][:, :]), 1)
                lo(two(qn_lo[1][:, :]), pair(1), two(qn_hi[1][:, :]), 2)
                lo(two(kn_lo[0][:, :]), pair(3), two(kn_hi[0][:, :]), 3)
                dve.wait_ge(s_proj, i * 6 + 5)
                steps.add(ve.tensor_tensor(two(probs[1][:, :]), pair(2), two(sin_t[:, :]), ALU.mult))
                steps.add(ve.tensor_tensor(probs[0][:, :], xn[0][:, 0:TOK], cos_t[:, :], ALU.mult))
                steps.wait()
                ve.tensor_tensor(probs[0][:, :], probs[0][:, :], probs[1][:, :], ALU.add).then_inc(s_rope, 1)
                lo(qpe_lo[:, :], probs[0][:, :], qpe_hi[:, :], 4)
                lo(two(kn_lo[1][:, :]), pair(0), two(kn_hi[1][:, :]), 5)
                for n, (t0, t1, b) in enumerate(((0, 2, 2), (2, 4, 3), (4, 5, 6))):
                    lo(v_parts[:, t0:t1, :, 1, :], by_head(ps[:, b, 0:(t1 - t0) * 2 * DV]), v_parts[:, t0:t1, :, 0, :],
                       6 + n)
                for s in range(UNITS + 3):
                    if s in (5, 7):
                        b = (s - 5) // 2
                        split_lo(b, i * 2 + (C_ATT + 2 + b), SLOT)
                    if s < UNITS:
                        r = rows(s % (NT + 1))
                        v = score_view(s)
                        dve.wait_ge(s_S, i * UNITS + (s + 1))
                        m = stat[0:r, ST_NM + s:ST_NM + s + 1]
                        steps.add(ve.tensor_reduce(m, v, AX.XY if len(v.shape) == 3 else AX.X, ALU.max))
                        steps.wait()
                        ve.tensor_scalar(m, m, -SCALE, None, ALU.mult).then_inc(s_max, 1)
                    if 2 <= s < UNITS + 2:
                        u = s - 2
                        t, r = u % (NT + 1), rows(u % (NT + 1))
                        dve.wait_ge(s_pthi, i * UNITS + (u + 1))
                        ins = ve.tensor_tensor(pt_lo[u % 2][0:META, 0, :], ps[0:META, 4, 0:P],
                                               pt_hi[u % 2][0:META, 0, :].bitcast(F32), ALU.subtract)
                        if t:
                            ins = ve.tensor_tensor(pt_lo[u % 2][:, 1:t + 1, :], turned(2, P)[:, 1:t + 1, :],
                                                   pt_hi[u % 2][:, 1:t + 1, :].bitcast(F32), ALU.subtract)
                        ins.then_inc(s_ptlo, 1)
                    if s >= 3:
                        u = s - 3
                        t, r = u % (NT + 1), rows(u % (NT + 1))
                        rd = stat[0:r, ST_RDEN + u:ST_RDEN + u + 1]
                        dve.wait_ge(s_exp, i * UNITS + (u + 1))
                        steps.add(ve.reciprocal(rd, stat[0:r, ST_DEN + u:ST_DEN + u + 1]))
                        steps.wait()
                        dve.wait_ge(s_pv, i * UNITS + (u + 1))
                        dst = attn[0:r, t, bass.ds(i * (2 * DV) + (u // (NT + 1)) * DV, DV)]
                        steps.add(ve.tensor_scalar(dst, ps[0:r, 6, DV:2 * DV], rd, None, ALU.mult))
                        steps.wait()
                        ve.scalar_tensor_tensor(dst, ps[0:r, 6, 0:DV], rd, dst, ALU.mult, ALU.add).then_inc(s_attn, 1)

            dve.wait_ge(s_gain_att, 16)
            norm_rows(att, attn, ST_ATT, gain_a, mixa_hi, mixa_lo)

            def heads(ap):
                return ap.rearrange("p (h e) -> p h e", e=SP)

            def both(ap):
                return ap.rearrange("p a (h e) -> p (a h) e", e=SP)

            def chunk(q, cols, w):
                first = isinstance(q, int)
                dve.wait_ge(s_xs, q + 1)
                ve.tensor_tensor(heads(xdt[0:w, :]), heads(xn[0][0:w, :]),
                                 bcast(smt[0:w, q, R_DT:R_DT + SH], [w, SH, SP]), ALU.mult).then_inc(s_xdt, 1)
                ve.tensor_tensor(heads(xdte[0:w, :]), heads(xn[0][0:w, :]),
                                 bcast(smt[0:w, q, R_DTE:R_DTE + SH], [w, SH, SP]), ALU.mult).then_inc(s_xdte, 1)
                if not first:
                    dve.wait_ge(s_off, q)
                    ve.tensor_tensor(heads(y_tm[:, :]), both(ps[:, 0:2, :]),
                                     bcast(smt[:, q, R_EXP:R_EXP + SH], [P, SH, SP]), ALU.mult).then_inc(s_yoff, 1)
                dve.wait_ge(s_cb, q + 1)
                for j in range(4):
                    dve.wait_ge(s_ex, q * 4 + (j + 1))
                    d = decay[0:w, 4 * j:4 * j + 4, 0:w]
                    g = 4 * j // HG
                    ins = ve.tensor_tensor(d, d, ps[0:w, 3, g * P:g * P + w].unsqueeze(1).broadcast_to([w, 4, w]),
                                           ALU.mult)
                ins.then_inc(s_M, 1)
                dve.wait_ge(s_xskip, q + 1)
                if first:
                    dve.wait_ge(s_st, q + 1)
                    ve.tensor_copy(two(state[:, :]), ps[:, 6:8, :]).then_inc(s_state, 1)
                    dve.wait_ge(s_yd, q + 1)
                    ve.tensor_tensor(two(y_tm[0:w, :]), ps[0:w, 0:2, :], two(xn[1][0:w, :]), ALU.add).then_inc(s_y, 1)
                else:
                    dve.wait_ge(s_yoff, q)
                    steps.add(ve.tensor_tensor(y_tm[:, :], y_tm[:, :], xn[1][:, :], ALU.add))
                    dve.wait_ge(s_st, q + 1)
                    dve.wait_ge(s_sdec, q)
                    ve.tensor_tensor(two(state[:, :]), ps[:, 6:8, :], two(state[:, :]), ALU.add).then_inc(s_state, 1)
                    dve.wait_ge(s_yd, q + 1)
                    steps.wait()
                    ve.tensor_tensor(two(y_tm[:, :]), ps[:, 0:2, :], two(y_tm[:, :]), ALU.add).then_inc(s_y, 1)
                dve.wait_ge(s_yt, q + 1)
                ve.tensor_tensor(gated[:, :, cols], turned(1, w), z_silu[:, :, cols], ALU.mult).then_inc(s_gate, 1)

            chunk(0, slice(0, META), META)
            with dve.Fori(1, NT + 1) as q, steps.loop(q - 1, NT, 1):
                chunk(q, bass.ds(q * P - (P - META), P), P)

            split_lo(0, C_OUT + 2)
            for k in range(XT + 1):
                if k < XT:
                    dve.wait_ge(s_rg, k // (XT // GROUPS) + 1)
                    if k >= 2:
                        dve.wait_ge(s_mslo, k - 1)
                    ve.scalar_tensor_tensor(normed_g[k % 2][:, :], gated[:, k, :], vec[:, 0, V_SN + k:V_SN + k + 1],
                                            rstd_g[:, k // (XT // GROUPS), :], ALU.mult, ALU.mult).then_inc(s_ng, 1)
                if k:
                    dve.wait_ge(s_mshi, k)
                    ve.tensor_tensor(mixs_lo[:, k - 1, :], normed_g[(k - 1) % 2][:, :],
                                     mixs_hi[:, k - 1, :].bitcast(F32), ALU.subtract).then_inc(s_mslo, 1)

            split_lo(1, C_OUT + 3)
            for b in range(2):
                split_lo(b, C_OUT + 4 + b)
            with dve.Fori(1, KD // 2) as i:
                for m in range(2):
                    for b in range(2):
                        split_lo(b, i * 4 + (C_OUT + 2 * m + 2 + b))
            dve.wait_ge(s_gain_post, 16)
            dve.wait_ge(s_gain_ffn, 16)
            for s in range(NT + 3):
                if s <= NT:
                    n = rows(s)
                    dve.wait_ge(s_rpost, s + 1)
                    if s >= 2:
                        dve.wait_ge(s_h, s - 1)
                    ve.scalar_tensor_tensor(two(post[s % 2][0:n, :]), ps[0:n, 2 * (s % 2):2 * (s % 2) + 2, :],
                                            stat[0:n, ST_POST + 5 + s:ST_POST + 6 + s], two(gain_a[0:n, :]),
                                            ALU.mult, ALU.mult).then_inc(s_u, 1)
                if 1 <= s <= NT + 1:
                    scale_rows(ffn, s - 1, h_tm[0:rows(s - 1), s - 1, :], ST_FFN, gain_b)
                if s >= 2:
                    turned_lo(ffn, s - 2, hn2_lo, hn2_hi)

            def up_block(j):
                for b, (u, cv, ready, done) in enumerate(((u_gate, c_gate, s_ug, s_cg), (u_value, c_value, s_uv, s_cv))):
                    dve.wait_ge(ready, j + 1)
                    steps.add(ve.tensor_scalar(cv[:, :], u[:, NF - SEQ:NF],
                                               vec[:, 2, one(j + b * KF)],
                                               vec[:, 2, one(j + (CF + b * KF))], ALU.mult, ALU.add))
                    for w in range(FTAPS - 1):
                        o = NF - SEQ - (FTAPS - 1) + w
                        steps.wait()
                        ins = ve.scalar_tensor_tensor(cv[:, :], u[:, o:o + SEQ],
                                                      vec[:, 1, one(j + (w * CF + b * KF))], cv[:, :],
                                                      ALU.mult, ALU.add)
                        if w < FTAPS - 2:
                            steps.add(ins)
                        else:
                            ins.then_inc(done, 1)
                    split_lo(b, j * 2 + (C_UP + 2 + b))
                dve.wait_ge(s_silu, j + 1)
                dve.wait_ge(s_cv, j + 1)
                ve.tensor_tensor(act[:, j, :], c_gate[:, :], c_value[:, :], ALU.mult).then_inc(s_actr, 1)
                dve.wait_ge(s_actr, j + 1)

            def stage_lo(slot, k):
                dve.wait_ge(s_sthi, k + 1)
                ve.tensor_tensor(st_lo[slot][:, :], act[:, k, :], st_hi[slot][:, :].bitcast(F32),
                                 ALU.subtract).then_inc(s_stlo, 1)

            with dve.Fori(0, KF - 1) as j, steps.loop(j, KF - 1, 2 * (FTAPS - 1)):
                up_block(j)
            for k in range(2):
                stage_lo(k, k)
            up_block(KF - 1)
            with dve.Fori(0, KF // 2 - 1) as i:
                for b in range(2):
                    stage_lo(b, i * 2 + (2 + b))
                    split_lo(b, i * 2 + (C_DOWN + 2 + b))
            dve.wait_ge(s_gain_last, 16)
            for t in range(NT):
                dve.wait_ge(s_rlast, t + 1)
                if t >= 2:
                    dve.wait_ge(s_out[t % 2], 16)
                ve.scalar_tensor_tensor(two(y_out[t % 2][:, :]), ps[:, 2 * t:2 * t + 2, :],
                                        stat[:, ST_LAST + 5 + t:ST_LAST + 6 + t], two(gain_a[:, :]),
                                        ALU.mult, ALU.mult).then_inc(s_ylast, 1)
                dve.wait_ge(s_ylast, t + 1)
                ve.tensor_tensor(y_out[t % 2][:, :], y_out[t % 2][:, :], h_tm[:, t + 1, :], ALU.add)\
                    .then_inc(s_yout, 1)

        @block.tensor
        def _(pe):
            mm = nc.tensor.matmul

            def three(out_ap, w_hi, w_lo, x_hi, x_lo, first, last):
                mm(out_ap, w_hi, x_hi, start=first, stop=False)
                mm(out_ap, w_hi, x_lo, start=False, stop=False)
                return mm(out_ap, w_lo, x_hi, start=False, stop=last)

            def chunk(slot, b, x_hi, x_lo, halves, first=True, last=True, tokens=None):
                for h, cols in enumerate(halves):
                    if tokens is not None:
                        pe.wait_ge(tokens, (3, NT + 1)[h])
                    w = cols.stop - cols.start
                    for k in range(KD):
                        ins = three(ps[:, 2 * b + h, 0:w], whi[slot][:, k * P:(k + 1) * P],
                                    wlo[slot][:, k * P:(k + 1) * P], x_hi[:, k, cols], x_lo[:, k, cols],
                                    first and k == 0, last and k == KD - 1)
                return ins

            def turn_rows(norm, t):
                w, b = rows(t), t % 2
                pe.wait_ge(norm.xn, t + 1)
                if t >= 2:
                    pe.wait_ge(norm.lo, t - 1)
                for k in range(KD):
                    ins = nc.tensor.transpose(turned(norm.pair + b, w)[:, k, :], xn[b][0:w, k * P:(k + 1) * P], ident[0:w, 0:w])
                ins.then_inc(norm.turned, 1)

            pe.wait_ge(s_const, 2)
            for t in range(NT + 1):
                turn_rows(pre, t)
            pe.wait_ge(s_vec, 16 * 12)
            for k, n in enumerate((NV0, 2 * CF, 2 * CF)):
                ins = nc.tensor.transpose(ps[:, 4, k * 96:k * 96 + n], vec_rows[0:n, k, :], ident[0:n, 0:n])
            ins.then_inc(s_vt, 1)
            for c in range(C_Z):
                pe.wait_ge(s_wlo, c + 1)
                chunk(c % 2, c % 2, hn_hi, hn_lo, WH, tokens=pre.lo).then_inc(s_pe, 1)
            for g, (j0, j1) in enumerate(((0, KQ), (KQ, KQ + KKV))):
                pe.wait_ge(s_sq, j1)
                for h, cols in enumerate(WH):
                    for j in range(j0, j1):
                        ins = mm(ps[:, 4 + 2 * g + h, 0:HALF], ones[:, :], squares[:, j, cols], start=j == j0,
                                 stop=j == j1 - 1)
                ins.then_inc(s_sumsq, 1)
            def in_chunks(c0, c1):
                with pe.Fori(c0 // 2, c1 // 2) as i:
                    for b in range(2):
                        pe.wait_ge(s_wlo, i * 2 + (b + 1))
                        chunk(b, b, hn_hi, hn_lo, WH).then_inc(s_pe, 1)

            in_chunks(C_Z, C_XBC)
            pe.wait_ge(s_sm, 1)
            nc.tensor.transpose(ps[0:META, 4, 0:P], sm[:, tcol(0)], ident[:, :])
            for t in range(1, NT + 1):
                ins = nc.tensor.transpose(ps[:, 5, (t - 1) * P:t * P], sm[:, tcol(t)], ident[:, :])
            ins.then_inc(s_smt, 1)
            pe.wait_ge(s_ends, 1)
            mm(ps[:, 6, 0:(NT + 1) * SH], ones[0:SH, :], ends[:, :, :].rearrange("p a b -> p (a b)"), start=True,
               stop=True).then_inc(s_dec, 1)
            in_chunks(C_XBC, C_XBC + CT // 2)
            pe.wait_ge(s_rstdf, 2)
            pe.wait_ge(s_evac, C_Z)
            pe.wait_ge(s_smt_ready, 2)
            for b, m in enumerate((dup, dupswap)):
                for h, cols in enumerate(WH):
                    ins = mm(ps[:, 4 + 2 * b + h, 0:HALF], m[:, :], qkvk[0:ROPE, C_Z - 1, cols], start=True, stop=True)
            ins.then_inc(s_kpe, 1)
            in_chunks(C_XBC + CT // 2, C_ATT)

            pe.wait_ge(s_qkvlo, KQ + KKV)
            with pe.Fori(0, PAIRS) as i:
                def project(b, slot, col, K, j0, step=P):
                    for h, cols in enumerate(WH):
                        for k in range(K):
                            w = slice(col + k * step, col + k * step + P)
                            ins = three(ps[:, 2 * b + h, 0:HALF], whi[slot][:, w], wlo[slot][:, w],
                                        qkv_hi[:, j0 + k, cols], qkv_lo[:, j0 + k, cols], k == 0, k == K - 1)
                    return ins

                def values(t, dst):
                    cols = slice(0, P) if t == 0 else tcol(t)
                    for k in range(KKV):
                        w = slice(2 * KKV * P + k * 2 * DV, 2 * KKV * P + (k + 1) * 2 * DV)
                        ins = three(dst, qkv_hi[:, KQ + k, cols], qkv_lo[:, KQ + k, cols], whi[1][:, w], wlo[1][:, w],
                                    k == 0, k == KKV - 1)
                    return ins

                pe.wait_ge(s_wlo, i * 2 + (C_ATT + 1))
                project(0, 0, 0, KQ, 0).then_inc(s_proj, 1)
                pe.wait_ge(s_xpad, CT)
                project(1, 0, KQ * P, KQ, 0).then_inc(s_proj, 1)
                pe.wait_ge(s_kper, 1)
                project(2, 0, 2 * KQ * P, KQ, 0).then_inc(s_proj, 1)
                pe.wait_ge(s_wlo, i * 2 + (C_ATT + 2))
                pe.wait_ge(s_plo, i * 8 + 1)
                project(3, 1, 0, KKV, KQ).then_inc(s_proj, 1)
                pe.wait_ge(s_rawcp, i + 1)
                mm(ps[:, 4, 0:HALF], swap[:, :], xn[0][:, WH[0]], start=True, stop=True).then_inc(s_pe, 1)
                mm(ps[:, 5, 0:HALF], swap[:, :], xn[0][:, WH[1]], start=True, stop=True).then_inc(s_proj, 1)
                project(0, 1, KKV * P, KKV, KQ).then_inc(s_proj, 1)
                pe.wait_ge(s_plo, i * 8 + 2)
                values(0, ps[:, 2, 0:2 * DV])
                values(1, ps[:, 2, 2 * DV:4 * DV])
                values(2, ps[:, 3, 0:2 * DV])
                values(3, ps[:, 3, 2 * DV:4 * DV])
                pe.wait_ge(s_plo, i * 8 + 3)
                values(4, ps[:, 6, 0:2 * DV]).then_inc(s_pe, 1)

                def scores(u):
                    hh, t = divmod(u, NT + 1)
                    n, b = score_cols(u), 2 * (u % 2)
                    qc = slice(0, P) if t == 0 else tcol(t)
                    pr = slice(hh * ROPE, (hh + 1) * ROPE)
                    parts = [(ps[:, b, 0:n], 0, n)] if n <= BANK else \
                        [(ps[:, b + h, 0:HALF], h * HALF, (h + 1) * HALF) for h in range(2)]
                    for dst, c0, c1 in parts:
                        ks = slice(c0, c1)
                        three(dst, qn_hi[hh][:, qc], qn_lo[hh][:, qc], kn_hi[hh][:, ks], kn_lo[hh][:, ks], True, False)
                        masked = c1 == n
                        ins = three(dst, qpe_hi[pr, qc], qpe_lo[pr, qc], kpe_hi[pr, ks], kpe_lo[pr, ks], False,
                                    not masked)
                    d = META if t == 0 else P
                    last = parts[-1]
                    w = last[2] - last[1]
                    return mm(ps[:, b + len(parts) - 1, w - d:w], ident_bf[:, :], mask_bf[:, 0:d], start=False, stop=True)

                for s in range(UNITS + 3):
                    if s < UNITS:
                        if s == 0:
                            pe.wait_ge(s_kpelo, 1)
                            pe.wait_ge(s_plo, i * 8 + 5)
                        elif s == 1:
                            pe.wait_ge(s_plo, i * 8 + 7)
                        else:
                            pe.wait_ge(s_exp, i * UNITS + (s - 1))
                        scores(s).then_inc(s_S, 1)
                    if 2 <= s < UNITS + 2:
                        u = s - 2
                        t = u % (NT + 1)
                        pe.wait_ge(s_exp, i * UNITS + (u + 1))
                        if s == 2:
                            pe.wait_ge(s_plo, i * 8 + 8)
                        else:
                            pe.wait_ge(s_ptlo, i * UNITS + u)
                        p = probs[u % 2]
                        ins = nc.tensor.transpose(ps[0:META, 4, 0:P], p[:, 0:META], ident[:, :])
                        for j in range(t):
                            ins = nc.tensor.transpose(turned(2, P)[:, 1 + j, :],
                                                      p[:, META + j * P:META + (j + 1) * P], ident[:, :])
                        ins.then_inc(s_T, 1)
                    if s >= 3:
                        u = s - 3
                        hh, t = divmod(u, NT + 1)
                        pe.wait_ge(s_ptlo, i * UNITS + (u + 1))
                        if u >= 1:
                            pe.wait_ge(s_attn, i * UNITS + u)
                        for j in range(t + 1):
                            kr = slice(0, META if j == 0 else P)
                            v = v_parts[kr, j, hh, :, :].rearrange("p a d -> p (a d)")
                            mm(ps[:, 6, 0:2 * DV], pt_hi[u % 2][kr, j, :], v, start=j == 0, stop=False)
                            ins = mm(ps[:, 6, 0:2 * DV], pt_lo[u % 2][kr, j, :], v, start=False, stop=j == t)
                        ins.then_inc(s_pv, 1)

            for t in range(NT + 1):
                turn_rows(att, t)

            pe.wait_ge(att.lo, NT + 1)
            pe.wait_ge(s_smt_ready, 2)
            pe.wait_ge(s_acs_copied, 3)

            def turn_chunk(q, w):
                pe.wait_ge(s_stage, q + 1)
                for k in range(XT):
                    nc.tensor.transpose(ps[0:w, k // 4, (k % 4) * P:(k % 4 + 1) * P], xbc_c[:, k, 0:w], ident[:, :])
                if not (isinstance(q, int) and q == 0):
                    pe.wait_ge(s_gate, q)
                for g in range(GROUPS):
                    ins = nc.tensor.transpose(ps[0:w, 2, g * P:(g + 1) * P], xbc_c[:, XT + g, 0:w], ident[:, :])
                ins.then_inc(s_xt, 1)
                for g in range(GROUPS):
                    ins = mm(ps[0:w, 3, g * P:g * P + w], xbc_c[:, XT + g, 0:w], xbc_c[:, XT + GROUPS + g, 0:w],
                             start=True, stop=True)
                ins.then_inc(s_cb, 1)

            def spread(q, cols, w):
                for j in range(4):
                    if j == 2 and not (isinstance(q, int) and q == 0):
                        pe.wait_ge(s_state, q)
                    block4 = ps[0:w, 4 + j, :].rearrange("p (a b) -> p a b", b=P)[:, :, 0:w]
                    mm(block4, mask_bf[0:w, 0:w], ident_bf[0:w, 0:w].unsqueeze(1).broadcast_to([w, 4, w]), start=True,
                       stop=False)
                    for h in range(4 * j, 4 * j + 4):
                        ins = mm(ps[0:w, 4 + j, (h % 4) * P:(h % 4) * P + w],
                                 pick[:, h:h + 1].broadcast_to([PARTS3, w]), acs3[0:PARTS3, cols], start=False,
                                 stop=h % 4 == 3)
                    ins.then_inc(s_ab, 1)

            def ssm_chunk(q, w, following=None):
                first = isinstance(q, int) and q == 0
                pe.wait_ge(s_xs, q + 1)
                if not first:
                    pe.wait_ge(s_state, q)
                    for g in range(GROUPS):
                        ins = mm(ps[:, g, :], xbc_c[:, XT + GROUPS + g, :], state[:, g * GC:(g + 1) * GC],
                                 start=True, stop=True)
                    ins.then_inc(s_off, 1)
                pe.wait_ge(s_ex, q * 4 + 4)
                pe.wait_ge(s_xdte, q + 1)
                for g in range(GROUPS):
                    ins = mm(ps[:, 6 + g, :], b_c[0:w, g * STATE:(g + 1) * STATE], xdte[0:w, g * GC:(g + 1) * GC],
                             start=True, stop=True)
                ins.then_inc(s_st, 1)
                pe.wait_ge(s_M, q + 1)
                if not first:
                    pe.wait_ge(s_yoff, q)
                for h in range(SH):
                    ins = mm(ps[0:w, h // HG, (h % HG) * SP:(h % HG + 1) * SP], decay[0:w, h, 0:w],
                             xdt[0:w, h * SP:(h + 1) * SP], start=True, stop=True)
                ins.then_inc(s_yd, 1)
                if following is not None:
                    spread(q + 1, following, P)
                pe.wait_ge(s_y, q + 1)
                for k in range(XT):
                    ins = nc.tensor.transpose(turned(1, w)[:, k, :], y_tm[0:w, k * P:(k + 1) * P], ident[0:w, 0:w])
                ins.then_inc(s_yt, 1)
                if following is not None:
                    turn_chunk(q + 1, P)

            spread(0, slice(0, META), META)
            turn_chunk(0, META)
            ssm_chunk(0, META, tcol(1))
            with pe.Fori(1, NT) as q:
                ssm_chunk(q, P, bass.ds(q * P + META, P))
            ssm_chunk(NT, P)
            KG = XT // GROUPS

            def out_half(i, half):
                for b in range(2):
                    pe.wait_ge(s_wlo, i * 4 + (C_OUT + 2 * half + b + 1))
                    x = (mixs_hi, mixs_lo) if half else (mixa_hi, mixa_lo)
                    chunk(b, b, x[0], x[1], WH, first=half == 0, last=half == 1).then_inc(s_pe, 1)
                    if isinstance(i, int) and half == 0 and b == 0:
                        for g in range(GROUPS):
                            pe.wait_ge(s_gsq, KG * (g + 1))
                            for h, cols in enumerate(WH):
                                for k in range(KG):
                                    ins = mm(ps[:, 4 + 2 * g + h, 0:HALF], ones[:, :], gsq[:, KG * g + k, cols],
                                             start=k == 0, stop=k == KG - 1)
                            ins.then_inc(s_gsum, 1)

            pe.wait_ge(s_gate, NT + 1)
            out_half(0, 0)
            pe.wait_ge(s_mslo, KD)
            out_half(0, 1)
            with pe.Fori(1, KD // 2) as i:
                for half in range(2):
                    out_half(i, half)
            for s in range(NT + 3):
                if s <= NT:
                    w, b = rows(s), s % 2
                    if s == 0:
                        pe.wait_ge(s_mixo, KD)
                    if s >= 2:
                        pe.wait_ge(s_u, s - 1)
                    for k in range(KD):
                        ins = nc.tensor.transpose(ps[0:w, 2 * b + k // 4, (k % 4) * P:(k % 4 + 1) * P],
                                                  mixo[:, k, tcol(s)], ident[:, :])
                    ins.then_inc(s_t1, 1)
                if s >= 2:
                    turn_rows(ffn, s - 2)
            pe.wait_ge(s_u, NT + 1)
            with pe.Fori(0, KF) as j:
                for b in range(2):
                    pe.wait_ge(s_wlo, j * 2 + (C_UP + 1 + b))
                    chunk(b, b, hn2_hi, hn2_lo, FH, tokens=ffn.lo).then_inc(s_pe, 1)

            def down_tile(slot, t, first=False, last=False):
                for n in range(2):
                    w = slice(n * BANK, (n + 1) * BANK)
                    tk = slice(t * P, (t + 1) * P)
                    ins = three(ps[:, 2 * t + n, :], st_hi[slot][:, tk], st_lo[slot][:, tk], whi[slot][:, w],
                                wlo[slot][:, w], first, last)
                return ins

            def down(slot, k, first=False):
                pe.wait_ge(s_wlo, k + (C_DOWN + 1))
                pe.wait_ge(s_stlo, k + 1)
                for t in (2, 3, 0, 1):
                    if first and t < 2:
                        pe.wait_ge((s_ug, s_uv)[t], KF)
                    ins = down_tile(slot, t, first)
                ins.then_inc(s_pe, 1)

            down(0, 0, first=True)
            down(1, 1)
            with pe.Fori(1, KF // 2 - 1) as i:
                for b in range(2):
                    down(b, i * 2 + b)
            pe.wait_ge(s_wlo, C_END - 1)
            pe.wait_ge(s_stlo, KF - 1)
            for t in range(3):
                down_tile(0, t)
            pe.wait_ge(s_wlo, C_END)
            pe.wait_ge(s_stlo, KF)
            for t in range(NT):
                if t == 2:
                    down_tile(0, 3)
                down_tile(1, t, last=True).then_inc(s_down, 1)


_INS = ['x', 'meta_tokens', 'norm_mix_pre', 'norm_mix_post', 'norm_ffn_pre', 'norm_ffn_post', 'w_in', 'q_a_norm',
        'w_uq', 'kv_a_norm', 'w_ukv', 'attn_out_norm', 'ssm_conv_w', 'ssm_conv_b', 'ssm_dt_bias', 'ssm_A_log',
        'ssm_D', 'ssm_norm', 'w_out', 'w_up', 'ffn_conv_w', 'ffn_conv_b', 'w_down']


def rope_rows(tokens, dim=64, theta=10000.0):
    import numpy as np

    f = np.float32
    inv = (f(theta) ** (-np.arange(0, dim, 2, dtype=f) / f(dim))).astype(f)
    ang = inv[:, None] * np.arange(tokens, dtype=f)[None, :]
    cos, sin = np.cos(ang).astype(f), np.sin(ang).astype(f)
    return np.ascontiguousarray(np.concatenate([cos] * 4)), np.ascontiguousarray(np.concatenate([-sin, sin] * 2))


def kernel(**inputs):
    import numpy as _np
    import concourse.bacc as _bacc
    from concourse import mybir as _mybir
    from concourse.bass_utils import run_bass_kernel_spmd as _run

    nc = _bacc.Bacc("TRN2", target_bir_lowering=False, num_devices=1)
    arrays, args = {}, []
    for name in _INS:
        a = _np.ascontiguousarray(inputs[name])
        arrays[f"in_{name}_dram"] = a
        args.append(nc.dram_tensor(f"in_{name}_dram", a.shape, _mybir.dt.from_np(a.dtype), kind="ExternalInput").ap())
    seq = inputs["x"].shape[1] + inputs["meta_tokens"].shape[0]
    for name, a in zip(("rope_cos", "rope_sin"), rope_rows(seq)):
        arrays[f"const_{name}"] = a
        args.append(nc.dram_tensor(f"const_{name}", a.shape, _mybir.dt.from_np(a.dtype), kind="ExternalInput").ap())
    out = nc.dram_tensor("out_0_dram", inputs["x"].shape, _mybir.dt.float32, kind="ExternalOutput").ap()
    hymba_layer(nc, *args, out)
    r = _run(nc, [arrays], core_ids=[0])
    return r.results[0]["out_0_dram"]
```

```python
from contextlib import ExitStack, contextmanager

import concourse.bass as bass
from concourse import mybir

F32 = mybir.dt.float32
F32R = mybir.dt.float32r
BF16 = mybir.dt.bfloat16
ALU = mybir.AluOpType
ACT = mybir.ActivationFunctionType
AX = mybir.AxisListType

P = 128
BANK = 512


class Chain:

    def __init__(self, engine, sem):
        self.engine, self.sem, self.base, self.steps = engine, sem, None, 0

    def add(self, ins):
        ins.then_inc(self.sem, 1)
        self.steps += 1
        return ins

    def wait(self):
        self.engine.wait_ge(self.sem, self.steps if self.base is None else self.base + self.steps)

    @contextmanager
    def loop(self, i, trips, per):
        before = self.steps
        self.base, self.steps = i * per, before
        yield
        assert self.steps - before == per, (self.steps - before, per)
        self.base, self.steps = None, before + per * trips


def hymba_layer(nc, x, meta_tokens, norm_mix_pre, norm_mix_post, norm_ffn_pre, norm_ffn_post, w_in,
                q_a_norm, w_uq, kv_a_norm, w_ukv, attn_out_norm, ssm_conv_w, ssm_conv_b, ssm_dt_bias,
                ssm_A_log, ssm_D, ssm_norm, w_out, w_up, ffn_conv_w, ffn_conv_b, w_down,
                rope_cos, rope_sin, out):
    SEQ, D = x.shape[1], x.shape[2]
    META = meta_tokens.shape[0]
    TOK = META + SEQ
    HALF = TOK // 2
    NT = SEQ // P
    KD = D // P
    D_IN = w_in.shape[2]
    R_Q, HEADS = w_uq.shape[1], w_uq.shape[2]
    R_KV = w_ukv.shape[1]
    KQ, KKV = R_Q // P, R_KV // P
    NOPE = 128
    ROPE = w_uq.shape[3] - NOPE
    DV = w_ukv.shape[3] - NOPE
    SCALE = float(NOPE + ROPE) ** -0.5
    SH = ssm_A_log.shape[1]
    D_SSM = ssm_norm.shape[1]
    SP = D_SSM // SH
    TAPS = ssm_conv_w.shape[1]
    D_XBC = ssm_conv_w.shape[2]
    STATE = 128
    GROUPS = (D_XBC - D_SSM) // 2 // STATE
    HG = SH // GROUPS
    GC = HG * SP
    CT = D_XBC // P
    XT = D_SSM // P
    D_FF = w_down.shape[1]
    KF = D_FF // P
    FTAPS = ffn_conv_w.shape[1]
    EPS = 1e-6
    NEG = -1e30
    assert (META, NT, KD, KQ, KKV, CT, KF, ROPE) == (16, 4, 8, 3, 2, 12, 22, 64)

    SLOT = 9 * P
    C_Z = 6
    C_XBC = C_Z + D_SSM // P
    C_ATT = C_XBC + CT
    PAIRS = HEADS // 2
    C_OUT = C_ATT + 2 * PAIRS
    C_UP = C_OUT + 2 * KD
    C_DOWN = C_UP + 2 * KF
    C_END = C_DOWN + KF

    def tcol(t):
        return slice(0, META) if t == 0 else slice(META + P * (t - 1), META + P * t)

    def rows(t):
        return META if t == 0 else P

    NF = SEQ + 4
    F0 = TOK - NF
    FH = (slice(F0, F0 + NF // 2), slice(F0 + NF // 2, TOK))
    WH = (slice(0, HALF), slice(HALF, TOK))

    wi = w_in[0].rearrange("(k p) n -> p k n", p=P)
    wq = w_uq[0].rearrange("(k p) h d -> p k h d", p=P)
    wkv = w_ukv[0].rearrange("(k p) h d -> p k h d", p=P)
    wo = w_out[0].rearrange("(k p) n -> p k n", p=P)
    wu = w_up[0].rearrange("(k p) n -> p k n", p=P)

    with ExitStack() as ctx:
        def sem(name):
            return ctx.enter_context(nc.semaphore(name))

        top = [(nc.sbuf_base + 63) // 64 * 64]

        def fixed(name, shape, dt):
            n = 4 if dt != BF16 else 2
            for s in shape[1:]:
                n *= s
            t = nc.alloc_sbuf_tensor_at(name, shape, dt, offset=top[0])
            top[0] += (n + 63) // 64 * 64
            return t

        wf = [fixed(f"weights_f32_{s}", [P, SLOT], F32) for s in range(2)]
        whi = [fixed(f"weights_hi_{s}", [P, SLOT], F32R) for s in range(2)]
        wlo = [fixed(f"weights_lo_{s}", [P, SLOT], F32R) for s in range(2)]
        h_tm = fixed("h_tm", [P, NT + 1, D], F32)
        ident = fixed("ident", [P, P], F32)
        ident_bf = fixed("ident_bf", [P, P], BF16)
        mask_bf = fixed("mask_bf", [P, P], BF16)
        swap = fixed("swap", [P, P], F32)
        dup = fixed("dup", [ROPE, P], F32)
        dupswap = fixed("dupswap", [ROPE, P], F32)
        ones = fixed("ones", [P, P], F32)
        PARTS3 = 96
        pick = fixed("pick", [PARTS3, SH], BF16)
        vec_rows = fixed("vec_rows", [P, 3, P], F32)
        vec = fixed("vec", [P, 3, 96], F32)
        gain_a = fixed("gain_a", [P, D], F32)
        gain_b = fixed("gain_b", [P, D], F32)
        before = top[0] - 4 * D
        smt = nc.alloc_sbuf_tensor_at("ssm_cols", [P, NT + 1, P], F32, offset=before)
        acs3 = nc.alloc_sbuf_tensor_at("acs_parts", [P, TOK], BF16, offset=before + 4 * (NT + 1) * P)
        dec_b = nc.alloc_sbuf_tensor_at("chunk_decay", [P, NT + 1, SH], F32, offset=before + 4 * (NT + 1) * P + 2 * TOK)
        skip_d = fixed("skip_d", [P, SH], F32)
        dt_small = fixed("dt_small", [SH, 4], F32)
        stat = fixed("stat", [P, 96], F32)
        xn = [fixed(f"normed_{i}", [P, D], F32) for i in range(2)]
        minus_acs = fixed("minus_acs", [P, NT + 1, SH], F32)
        dt_ends = fixed("dt_ends", [SH, NT + 1], F32)
        ends = fixed("chunk_ends", [SH, NT + 1, SH], F32)
        dtw = fixed("dt_weights", [P, KD, SH], F32)
        sm = fixed("ssm_rows", [P, TOK], F32)
        pool = top[0]
        spare = nc.sbuf_usable_end - pool

        def at(name, shape, dt, off):
            n = 4 if dt != BF16 else 2
            for s in shape[1:]:
                n *= s
            assert off + n <= spare, (name, off + n, spare)
            return nc.alloc_sbuf_tensor_at(name, shape, dt, offset=pool + off)

        TB = 4 * TOK
        AB = 4 * (NT + 1) * D
        O_QKV = (XT + CT) * TB
        O_W = O_QKV + 10 * TB
        z_silu = at("z_silu", [P, XT, TOK], F32, 0)
        xbc = at("xbc", [P, CT, TOK], F32, XT * TB)
        qkv_hi = at("qkv_hi", [P, KQ + KKV, TOK], F32R, O_QKV)
        qkv_lo = at("qkv_lo", [P, KQ + KKV, TOK], F32R, O_QKV + 5 * TB)
        hn_hi = at("hn_hi", [P, KD, TOK], F32R, O_W)
        hn_lo = at("hn_lo", [P, KD, TOK], F32R, O_W + 8 * TB)
        qkvk = at("qkvk", [P, C_Z, TOK], F32, O_W + 16 * TB)
        squares = at("squares", [P, KQ + KKV, TOK], F32, O_W + 22 * TB)
        acs_rest = [squares[0:SH, j, :] for j in range(3)]
        kpe_parts = [qkvk[:, j, :] for j in range(2)]
        XPAD = TAPS - 1
        xpad = [at(f"xpad_{i}", [P, XPAD + TOK + 1], F32, O_W + 27 * TB + i * (TB + 32)) for i in range(2)]
        o = O_W + 29 * TB + 64
        conv = [at(f"conv_{i}", [P, TOK], F32, o + i * TB) for i in range(2)]
        rstd_f = at("rstd_f", [P, 2, TOK], F32, o + 2 * TB)
        attn = at("attn", [P, NT + 1, D], F32, O_W)
        o = O_W + AB
        O_MIXA = o
        PTB = 4 * (NT + 1) * P
        pt_hi = [at(f"pt_hi_{i}", [P, NT + 1, P], F32R, o + i * PTB) for i in range(2)]
        pt_lo = [at(f"pt_lo_{i}", [P, NT + 1, P], F32R, o + (2 + i) * PTB) for i in range(2)]
        o += 4 * PTB
        probs = [at(f"probs_{i}", [P, TOK], F32, o + i * TB) for i in range(2)]
        qn_hi = [at(f"qn_hi_{i}", [P, TOK], F32R, o + (2 + i) * TB) for i in range(2)]
        qn_lo = [at(f"qn_lo_{i}", [P, TOK], F32R, o + (4 + i) * TB) for i in range(2)]
        kn_hi = [at(f"kn_hi_{i}", [P, TOK], F32R, o + (6 + i) * TB) for i in range(2)]
        o += 8 * TB
        kpe_hi = at("kpe_hi", [P, TOK], F32R, o)
        kpe_lo = at("kpe_lo", [P, TOK], F32R, o + TB)
        kn_lo = [at(f"kn_lo_{i}", [P, TOK], F32R, o + (2 + i) * TB) for i in range(2)]
        qpe_hi = at("qpe_hi", [P, TOK], F32R, o + 4 * TB)
        qpe_lo = at("qpe_lo", [P, TOK], F32R, o + 5 * TB)
        o += 6 * TB
        v_parts = at("v_parts", [P, NT + 1, 2, 2, DV], F32R, o)
        o += 8 * (NT + 1) * 2 * DV
        cos_t = at("cos_t", [P, TOK], F32, o)
        sin_t = at("sin_t", [P, TOK], F32, o + TB)
        mixa_hi = at("mixa_hi", [P, KD, TOK], F32R, O_MIXA)
        mixa_lo = at("mixa_lo", [P, KD, TOK], F32R, O_MIXA + 8 * TB)
        gated = z_silu
        plan = [O_QKV]

        def ssm(name, shape, dt=F32):
            n = 4
            for s in shape[1:]:
                n *= s
            assert plan[0] + n <= O_MIXA
            t = at(name, shape, dt, plan[0])
            plan[0] += (n + 31) // 32 * 32
            return t

        xbc_c = ssm("xbc_chunk", [P, CT, P])
        decay = ssm("decay", [P, SH, P])
        xdt = ssm("xdt", [P, D_SSM])
        xdte = ssm("xdte", [P, D_SSM])
        b_c = ssm("b_chunk", [P, GROUPS * STATE])
        y_tm = ssm("y_tm", [P, D_SSM])
        state = ssm("state", [P, D_SSM])
        gsq = at("gated_squares", [P, XT, TOK], F32, O_MIXA + 16 * TB)
        mixs_hi = at("mixs_hi", [P, KD, TOK], F32R, 0)
        mixs_lo = at("mixs_lo", [P, KD, TOK], F32R, 8 * TB)
        rstd_g = at("rstd_g", [P, GROUPS, TOK], F32, 16 * TB)
        normed_g = [at(f"normed_g_{i}", [P, TOK], F32, (18 + i) * TB) for i in range(2)]
        post = [at(f"post_{i}", [P, D], F32, (16 + 2 * i) * TB) for i in range(2)]
        squares_out = at("squares_out", [P, D], F32, 20 * TB)
        mixo = at("mixo", [P, KD, TOK], F32, 28 * TB)
        hn2_hi = at("hn2_hi", [P, KD, TOK], F32R, 40 * TB)
        hn2_lo = at("hn2_lo", [P, KD, TOK], F32R, 48 * TB)
        act = at("act", [P, KF, SEQ], F32, 0)
        o = 22 * TB
        u_gate = at("u_gate", [P, NF], F32, o)
        u_value = at("u_value", [P, NF], F32, o + TB)
        c_gate = at("conv_gate", [P, SEQ], F32, o + 2 * TB)
        c_value = at("conv_value", [P, SEQ], F32, o + 3 * TB)
        o = 30 * TB
        st_hi = [at(f"act_hi_{i}", [P, SEQ], F32R, o + i * TB) for i in range(2)]
        st_lo = [at(f"act_lo_{i}", [P, SEQ], F32R, o + (2 + i) * TB) for i in range(2)]
        junk = at("junk", [P, D], F32, 34 * TB)
        y_out = [at(f"y_out_{i}", [P, D], F32, (36 + 2 * i) * TB) for i in range(NT)]

        ps = ctx.enter_context(nc.psum_tensor("ps", [P, 8, BANK], F32))

        s_x = [sem(f"x_landed_{t}") for t in range(NT + 1)]
        s_land = [sem(f"weights_landed_{s}") for s in range(2)]
        s_gain_pre, s_gain_att, s_gain_post, s_gain_ffn, s_gain_last = (
            sem(f"gain_{n}_landed") for n in ("pre", "attn", "post", "ffn", "last"))
        s_vec, s_small, s_rope_tab = sem("vectors_landed"), sem("small_landed"), sem("rope_landed")
        s_const = sem("constants_ready")
        s_act, s_dve, s_pool = sem("scalar_steps"), sem("vector_steps"), sem("pool_steps")
        s_whi, s_wlo, s_pe = sem("weights_hi_ready"), sem("weights_lo_ready"), sem("chunk_multiplied")
        s_vt, s_vec_ready = sem("vectors_transposed"), sem("vectors_ready")

        class Norm:

            def __init__(self, name, pair):
                self.pair = pair
                self.rstd, self.xn, self.turned, self.hi, self.lo = (
                    sem(f"{name}_{n}") for n in ("rstd", "scaled", "turned", "hi", "lo"))

        pre, att, ffn = Norm("pre", 2), Norm("attn_norm", 0), Norm("ffn_norm", 2)
        s_evac, s_sq, s_sumsq, s_rstdf = sem("qkvk_copied"), sem("squares_ready"), sem("sums_ready"), sem("rstd_f_ready")
        s_qkvn, s_qkvhi, s_qkvlo = sem("qkv_normed"), sem("qkv_hi_ready"), sem("qkv_lo_ready")
        s_xpad, s_conv, s_xbc = sem("xpad_filled"), sem("conv_done"), sem("xbc_ready")
        s_dtr, s_dtx, s_dtl, s_acs, s_exps = (
            sem(n) for n in ("dt_copied", "dt_biased", "dt_log_ready", "acs_ready", "acs_exps_ready"))
        s_sm, s_negA = sem("ssm_rows_ready"), sem("exp_A_ready")
        s_kpe, s_kper, s_kpehi, s_kpelo = (
            sem(n) for n in ("kpe_turned", "kpe_roped", "kpe_hi_ready", "kpe_lo_ready"))
        s_cos, s_val = sem("qpe_times_cos"), sem("value_pairs_ready")
        s_proj, s_rawcp, s_rope = sem("projections_done"), sem("rope_raw_copied"), sem("qpe_roped")
        s_phi, s_plo = sem("projections_hi"), sem("projections_lo")
        s_S, s_max, s_exp, s_T = sem("scores_ready"), sem("negmax_ready"), sem("probs_ready"), sem("probs_turned")
        s_pthi, s_ptlo, s_pv, s_attn = (
            sem(n) for n in ("probs_t_hi", "probs_t_lo", "pv_ready", "attn_stored"))
        s_smt, s_ends, s_dec, s_smt_ready, s_acs_copied, s_acs3 = (
            sem(n) for n in ("ssm_cols_turned", "ends_ready", "decay_summed", "ssm_cols_ready", "acs_copied",
                             "acs_parts_ready"))
        s_stage, s_xt, s_ab, s_off, s_yd, s_st, s_yt = (
            sem(n) for n in ("chunk_staged", "chunk_turned", "acs_spread", "y_from_state",
                             "y_inside_ready",
                             "chunk_state_ready", "y_turned"))
        s_smtc, s_xs, s_xdt, s_xdte, s_xskip, s_yoff, s_ex, s_M = (
            sem(n) for n in ("chunk_cols_ready", "xs_copied", "xdt_ready", "xdte_ready", "xskip_ready",
                             "y_from_state_copied", "decays_ready", "mix_ready"))
        s_seg = sem("meta_segments_ready")
        s_sdec, s_yadd = sem("state_decayed"), sem("skip_added")
        s_acs3_zero = sem("acs_parts_zeroed")
        s_y, s_state, s_gate = sem("y_ready"), sem("state_ready"), sem("gated_ready")
        s_gsq, s_gsum, s_rg, s_ng, s_mshi, s_mslo = (
            sem(n) for n in ("gated_squares", "gated_sums", "rstd_g", "normed_g", "mixs_hi_ready", "mixs_lo_ready"))
        s_mixo, s_t1, s_rpost, s_u, s_h = (
            sem(n) for n in ("mix_out_copied", "mix_out_turned", "post_rstd", "post_scaled", "residual_ready"))
        s_ug, s_uv, s_cg, s_cv, s_silu, s_actr = (
            sem(n) for n in ("u_gate_copied", "u_value_copied", "conv_gate_done", "conv_value_done", "silu_ready",
                             "act_ready"))
        s_sthi, s_stlo, s_down, s_rlast, s_ylast, s_yout = (
            sem(n) for n in ("act_hi_ready", "act_lo_ready", "down_ready", "last_rstd", "last_scaled", "y_ready_out"))
        s_out = sem("out_written")

        V_QA, V_KVA, V_SN, V_CW, V_CB = 0, KQ, KQ + KKV, KQ + KKV + XT, KQ + KKV + XT + TAPS * CT
        NV0 = V_CB + CT
        CF = 2 * KF
        ST_PRE, ST_ATT, ST_POST, ST_FFN, ST_LAST, ST_NM, ST_DEN, ST_RDEN, ST_EPS = 0, 10, 20, 30, 40, 50, 60, 70, 95
        R_DT, R_ACS, R_DTE, R_EXP = 0, 32, 64, 96
        HI_AT = (3, 4, 5, 6)
        UNITS = 2 * (NT + 1)
        eps = stat[:, ST_EPS:ST_EPS + 1]

        OUT_COLS = [[slice(0, D)]] * (NT - 1) + [[slice(0, D // 2), slice(D // 2, D)]]
        SPREAD = (6, 7, 4, 5)
        LAG = 2
        PARTS = 4

        def landed(turn):
            return turn * (16 * PARTS) + 16 * PARTS

        def turned(b, w):
            return ps[:, 2 * b:2 * b + 2, :].rearrange("p a (k w) -> p (a k) w", w=P)[:, :, 0:w]

        def quarter(b, w):
            return ps[:, b, :].rearrange("p (k w) -> p k w", w=P)[:, :, 0:w]

        def pair(b, w=HALF):
            return ps[:, 2 * b:2 * b + 2, 0:w]

        def two(ap):
            return ap.rearrange("p (a b) -> p a b", a=2)

        def spreads(q, j):
            return q * 4 + (j - 2)

        def one(i):
            return slice(i, i + 1) if isinstance(i, int) else bass.ds(i, 1)

        def by_head(ap):
            return ap.rearrange("p (t h d) -> p t h d", h=2, d=DV)

        def dt_cols(t):
            return t[:, 0:KD * P].rearrange("p (k n) -> p k n", k=KD)[:, :, ROPE:ROPE + SH]

        def bcast(ap, shape):
            return ap.unsqueeze(2).broadcast_to(shape)

        def score_cols(u):
            t = u % (NT + 1)
            return META + P * t

        def score_view(u):
            n, r = score_cols(u), rows(u % (NT + 1))
            b = 2 * (u % 2)
            return ps[0:r, b, 0:n] if n <= BANK else ps[0:r, b:b + 2, 0:n // 2]

        def prob_view(u):
            n, r = score_cols(u), rows(u % (NT + 1))
            v = probs[u % 2][0:r, 0:n]
            return v if n <= BANK else v.rearrange("p (a b) -> p a b", a=2)

        block = ctx.enter_context(nc.Block())

        @block.sync
        def _(sp):
            def load(slot, dst, src, chunk, n=1):
                if chunk is not None:
                    sp.wait_ge(s_wlo, chunk - 1)
                sp.dma_start(dst, src).then_inc(s_land[slot], 16 * PARTS // n)

            def blocks(slot, k=KD, w=P):
                return wf[slot][:, 0:k * w].rearrange("p (k n) -> p k n", k=k)

            sp.dma_start(h_tm[0:META, 0, :], meta_tokens).then_inc(s_x[0], 16)
            for t in range(1, NT + 1):
                sp.dma_start(h_tm[:, t, :], x[0, P * (t - 1):P * t, :]).then_inc(s_x[t], 16)
            for c in range(2):
                load(c, blocks(c), wi[:, :, P * c:P * (c + 1)], None)

            def vector_rows(k, r0, src, n):
                sp.dma_start(vec_rows[r0:r0 + n, k, :], src.rearrange("(n p) -> n p", p=P)).then_inc(s_vec, 16)

            vector_rows(0, V_QA, q_a_norm[0], KQ)
            vector_rows(0, V_KVA, kv_a_norm[0], KKV)
            vector_rows(0, V_SN, ssm_norm[0], XT)
            vector_rows(0, V_CB, ssm_conv_b[0], CT)
            for w in range(TAPS):
                vector_rows(0, V_CW + w * CT, ssm_conv_w[0, w], CT)
            for w in range(2):
                vector_rows(1, w * CF, ffn_conv_w[0, w], CF)
            vector_rows(2, 0, ffn_conv_w[0, 2], CF)
            vector_rows(2, CF, ffn_conv_b[0], CF)
            sp.dma_start(dtw[:, :, :], wi[:, :, D_IN - SH:D_IN]).then_inc(s_small, 16)
            sp.dma_start(dt_small[:, 0:1], ssm_dt_bias.rearrange("a h -> h a")).then_inc(s_small, 16)
            sp.dma_start(dt_small[:, 1:2], ssm_A_log.rearrange("a h -> h a")).then_inc(s_small, 16)
            sp.dma_start(skip_d[:, :], ssm_D[0:1, :].broadcast_to([P, SH])).then_inc(s_small, 16)
            sp.dma_start(cos_t[:, :], rope_cos).then_inc(s_rope_tab, 16)
            sp.dma_start(sin_t[:, :], rope_sin).then_inc(s_rope_tab, 16)

            with sp.Fori(1, C_Z // 2) as i:
                for b in range(2):
                    load(b, blocks(b), wi[:, :, bass.ds(i * (2 * P) + b * P, P)], i * 2 + b)
            with sp.Fori(C_Z // 2, C_ATT // 2) as i:
                for b in range(2):
                    load(b, blocks(b), wi[:, :, bass.ds(i * (2 * P) + (b * P - (P - ROPE)), P)], i * 2 + b)
            with sp.Fori(0, PAIRS) as i:
                c = C_ATT + i * 2
                for hh in range(2):
                    h = i * 2 + hh
                    load(0, wf[0][:, hh * KQ * P:(hh + 1) * KQ * P].rearrange("p (k n) -> p k n", k=KQ),
                         wq[:, :, h, 0:NOPE], c if hh == 0 else None, PARTS)
                    load(0, wf[0][:, 2 * KQ * P:3 * KQ * P].rearrange("p (k n) -> p k n", k=KQ)
                         [:, :, hh * ROPE:(hh + 1) * ROPE], wq[:, :, h, NOPE:NOPE + ROPE], None, PARTS)
                for hh in range(2):
                    h = i * 2 + hh
                    load(1, wf[1][:, hh * KKV * P:(hh + 1) * KKV * P].rearrange("p (k n) -> p k n", k=KKV),
                         wkv[:, :, h, 0:NOPE], c + 1 if hh == 0 else None, PARTS)
                    load(1, wf[1][:, 2 * KKV * P:4 * KKV * P].rearrange("p (k n) -> p k n", k=KKV)
                         [:, :, hh * DV:(hh + 1) * DV], wkv[:, :, h, NOPE:NOPE + DV], None, PARTS)
            with sp.Fori(0, KD // 2) as i:
                for half in range(2):
                    for b in range(2):
                        load(b, blocks(b), wo[:, KD * half:KD * (half + 1), bass.ds(i * (2 * P) + b * P, P)],
                             i * 4 + (C_OUT + 2 * half + b))
            with sp.Fori(0, KF) as j:
                for b in range(2):
                    load(b, blocks(b), wu[:, :, bass.ds(j * P + b * D_FF, P)], C_UP + j * 2 + b)
            with sp.Fori(0, KF // 2) as i:
                for b in range(2):
                    load(b, wf[b][:, 0:D], w_down[0, bass.ds(i * (2 * P) + b * P, P), :], C_DOWN + i * 2 + b)
            for t in range(NT):
                for n, cols in enumerate(OUT_COLS[t]):
                    sp.wait_ge(s_yout, t + n + 1)
                    sp.dma_start(out[0, P * t:P * (t + 1), cols], y_out[t][:, cols]).then_inc(s_out, 16)
            sp.wait_ge(s_out, 16 * (NT + 1))

        @block.gpsimd
        def _(pool):
            steps = Chain(pool, s_pool)
            for s in range(2):
                steps.add(pool.memset(wf[s][:, KD * P:SLOT], 0.0))
            steps.add(pool.memset(ident[:, :], 0.0))
            for t in (ident_bf, mask_bf, sm, ones):
                steps.add(pool.memset(t[:, :], 1.0 if t is ones else 0.0))
            steps.add(pool.memset(stat[:, ST_EPS:ST_EPS + 1], EPS))
            steps.wait()
            for t in (ident, ident_bf):
                steps.add(pool.affine_select(out=t[:, :], in_=t[:, :], compare_op=ALU.not_equal, fill=1.0, base=0,
                                             pattern=[[-1, P]], channel_multiplier=1))
            steps.add(pool.affine_select(out=mask_bf[:, :], in_=mask_bf[:, :], compare_op=ALU.is_ge, fill=NEG, base=0,
                                         pattern=[[-1, P]], channel_multiplier=1))
            steps.wait()
            H2 = ROPE // 2
            for b in range(P // H2):
                steps.add(pool.tensor_copy(swap[:, b * H2:(b + 1) * H2], ident[:, (b ^ 1) * H2:((b ^ 1) + 1) * H2]))
            for b in range(2):
                steps.add(pool.tensor_copy(dup[:, b * ROPE:(b + 1) * ROPE], ident[0:ROPE, 0:ROPE]))
            steps.add(pool.tensor_tensor(pick[:, :], ident[0:PARTS3, 0:SH], ident[0:PARTS3, 32:32 + SH], ALU.add))
            steps.wait()
            steps.add(pool.tensor_tensor(pick[:, :], pick[:, :], ident[0:PARTS3, 64:64 + SH], ALU.add))
            for b in range(2):
                steps.add(pool.tensor_copy(dupswap[:, b * ROPE:(b + 1) * ROPE], swap[0:ROPE, 0:ROPE]))
            steps.wait()
            pool.memset(xpad[0][:, 0:XPAD], 0.0).then_inc(s_const, 1)
            pool.memset(xpad[1][:, 0:XPAD], 0.0).then_inc(s_const, 1)
            pool.wait_ge(pre.xn, NT + 1)
            pool.dma_start(gain_a[:, :], attn_out_norm[0:1, :].broadcast_to([P, D])).then_inc(s_gain_att, 16)
            pool.wait_ge(s_rope_tab, 32)
            pool.wait_ge(s_kpelo, 1)
            with pool.Fori(0, PAIRS) as i:
                pool.wait_ge(s_rawcp, i + 1)
                pool.tensor_tensor(probs[0][:, :], xn[0][:, 0:TOK], cos_t[:, :], ALU.mult).then_inc(s_cos, 1)
                for b in range(2):
                    pool.wait_ge(s_whi, i * 2 + (C_ATT + 3 + b))
                    pool.tensor_tensor(wlo[b][:, :], wf[b][:, :], whi[b][:, :].bitcast(F32), ALU.subtract)\
                        .then_inc(s_wlo, 1)
            pool.wait_ge(att.xn, NT + 1)
            pool.dma_start(gain_a[:, :], norm_mix_post[0:1, :].broadcast_to([P, D])).then_inc(s_gain_post, 16)

            def heads(ap, w=P):
                return ap.rearrange("p (h e) -> p h e", e=SP)

            def chunk(q, w):
                first = isinstance(q, int)
                pool.wait_ge(s_xs, q + 1)
                if not first:
                    pool.wait_ge(s_y, q)
                pool.tensor_tensor(heads(xdte[0:w, :], w), heads(xn[0][0:w, :], w),
                                   bcast(smt[0:w, q, R_DTE:R_DTE + SH], [w, SH, SP]), ALU.mult).then_inc(s_xdte, 1)
                if not first:
                    pool.wait_ge(s_off, q)
                    pool.tensor_tensor(heads(state[:, :]), heads(state[:, :]),
                                       bcast(dec_b[:, q, :], [P, SH, SP]), ALU.mult).then_inc(s_sdec, 1)
                pool.tensor_tensor(heads(xn[1][0:w, :], w), heads(xn[0][0:w, :], w),
                                   bcast(skip_d[0:w, :], [w, SH, SP]), ALU.mult).then_inc(s_xskip, 1)
                if not first:
                    pool.wait_ge(s_yoff, q)
                    pool.wait_ge(s_xskip, q + 1)
                    pool.tensor_tensor(y_tm[:, :], y_tm[:, :], xn[1][:, :], ALU.add).then_inc(s_yadd, 1)

            pool.wait_ge(s_small, 16 * 4)
            chunk(0, META)
            with pool.Fori(1, NT + 1) as q:
                chunk(q, P)
            pool.wait_ge(s_gate, 2 * (NT + 1))
            pool.dma_start(gain_b[:, :], norm_ffn_pre[0:1, :].broadcast_to([P, D])).then_inc(s_gain_ffn, 16)
            for t in range(NT + 1):
                pool.wait_ge(s_u, t + 1)
                n = rows(t)
                pool.tensor_tensor(h_tm[0:n, t, :], h_tm[0:n, t, :], post[t % 2][0:n, :], ALU.add).then_inc(s_h, 1)
            pool.dma_start(gain_a[:, :], norm_ffn_post[0:1, :].broadcast_to([P, D])).then_inc(s_gain_last, 16)
            pool.wait_ge(s_gain_last, 16)

        @block.scalar
        def _(act_e):
            sc = nc.scalar
            steps = Chain(act_e, s_act)

            def split_hi(slot, chunk, turn, width=KD * P):
                act_e.wait_ge(s_land[slot], landed(turn))
                if not (isinstance(chunk, int) and chunk < 2):
                    act_e.wait_ge(s_pe, chunk - 1)
                if isinstance(chunk, int) and chunk == 5:
                    steps.add(sc.activation(whi[slot][:, 0:width], wf[slot][:, 0:width], ACT.Copy))
                    act_e.wait_ge(s_small, 16 * 4)
                    steps.wait()
                    sc.activation(dt_cols(whi[slot]), dtw[:, :, :], ACT.Copy).then_inc(s_whi, 1)
                else:
                    sc.activation(whi[slot][:, 0:width], wf[slot][:, 0:width], ACT.Copy).then_inc(s_whi, 1)

            def rstd(src, n, col, done, scale, junk_out):
                steps.add(sc.activation(junk_out, src, ACT.Square, accum_out=stat[0:n, col:col + 1]))
                steps.wait()
                steps.add(sc.activation(stat[0:n, col:col + 1], stat[0:n, col:col + 1], ACT.Ln, scale=scale,
                                        bias=eps[0:n]))
                steps.wait()
                sc.activation(stat[0:n, col + 5:col + 6], stat[0:n, col:col + 1], ACT.Exp, scale=-0.5).then_inc(done, 1)

            def turned_hi(norm, t, dst):
                act_e.wait_ge(norm.turned, t + 1)
                w, b = rows(t), norm.pair + t % 2
                sc.activation(dst[:, :, tcol(t)], turned(b, w), ACT.Copy).then_inc(norm.hi, 1)

            for dst, src, s in ((gain_a, norm_mix_pre, s_gain_pre),):
                act_e.dma_start(dst[:, :], src[0:1, :].broadcast_to([P, D])).then_inc(s, 16)

            sc.preload_act_table_set("natural_log_exp_and_others")
            act_e.wait_ge(s_const, 2)
            for s in range(NT + 3):
                if s <= NT:
                    act_e.wait_ge(s_x[s], 16)
                    rstd(h_tm[0:rows(s), s, :], rows(s), ST_PRE + s, pre.rstd, 1.0 / D,
                         squares[0:rows(s), 0:2, :].rearrange("p a b -> p (a b)")[:, 0:D])
                if s >= 2:
                    turned_hi(pre, s - 2, hn_hi)
                if s in (NT, NT + 1):
                    split_hi(s - NT, s - NT, 0)

            for c in range(C_Z):
                act_e.wait_ge(s_pe, c + 1)
                sc.activation(two(qkvk[:, c, :]), pair(c % 2), ACT.Copy).then_inc(s_evac, 1)
                split_hi(c % 2, c + 2, (c + 2) // 2)
                if c == 1:
                    act_e.wait_ge(s_vt, 1)
                    sc.activation(vec[:, 0, 0:NV0], ps[:, 4, 0:NV0], ACT.Copy).then_inc(s_vec_ready, 1)
                    sc.activation(vec[:, 1:3, 0:2 * CF],
                                  ps[:, 4, 96:3 * 96].rearrange("p (a b) -> p a b", a=2)[:, :, 0:2 * CF],
                                  ACT.Copy).then_inc(s_vec_ready, 1)
                if c < KQ + KKV:
                    act_e.wait_ge(s_evac, c + 1)
                    sc.activation(squares[:, c, :], qkvk[:, c, :], ACT.Square).then_inc(s_sq, 1)
            act_e.wait_ge(s_evac, C_Z)
            sc.activation(xn[0][0:SH, 0:TOK], qkvk[ROPE:ROPE + SH, C_Z - 1, :], ACT.Copy).then_inc(s_dtr, 1)
            for g, (n, b) in enumerate(((R_Q, 2), (R_KV, 3))):
                act_e.wait_ge(s_sumsq, g + 1)
                steps.add(sc.activation(two(rstd_f[:, g, :]), pair(b), ACT.Ln, scale=1.0 / n, bias=eps))
                steps.wait()
                sc.activation(rstd_f[:, g, :], rstd_f[:, g, :], ACT.Exp, scale=-0.5).then_inc(s_rstdf, 1)
            act_e.wait_ge(s_dtx, 2)
            steps.add(sc.activation(xn[0][0:SH, 0:TOK], xn[1][0:SH, 0:TOK], ACT.Abs))
            steps.wait()
            steps.add(sc.activation(xn[0][0:SH, 0:TOK], xn[0][0:SH, 0:TOK], ACT.Exp, scale=-1.0))
            steps.wait()
            sc.activation(xn[0][0:SH, 0:TOK], xn[0][0:SH, 0:TOK], ACT.Ln, bias=1.0).then_inc(s_dtl, 1)
            sc.activation(dt_small[:, 2:3], dt_small[:, 1:2], ACT.Exp).then_inc(s_negA, 1)
            for j in range(KQ + KKV):
                act_e.wait_ge(s_qkvn, j + 1)
                sc.activation(qkv_hi[:, j, :], qkvk[:, j, :], ACT.Copy).then_inc(s_qkvhi, 1)
            def z_raw(b):
                act_e.wait_ge(s_pe, C_Z + b + 1)
                steps.add(sc.activation(two(z_silu[:, b, :]), pair(b), ACT.Copy))
                split_hi(b, C_Z + b + 2, C_Z // 2 + 1)

            z_raw(0)
            act_e.wait_ge(s_acs, NT + 1)
            for t in range(NT + 1):
                c = tcol(t)
                steps.add(sc.activation(xn[1][0:SH, c], xn[0][0:SH, c], ACT.Exp, scale=-1.0,
                                        bias=xn[0][0:SH, c.stop - 1:c.stop]))
            sc.activation(sm[R_EXP:R_EXP + SH, :], xn[0][0:SH, 0:TOK], ACT.Exp).then_inc(s_exps, 1)
            for j in range(3):
                if j:
                    act_e.wait_ge(s_acs3, j)
                else:
                    act_e.wait_ge(s_acs3_zero, 1)
                sc.activation(acs3[32 * j:32 * j + SH, :], acs_rest[j] if j else xn[0][0:SH, 0:TOK], ACT.Copy)\
                    .then_inc(s_acs_copied, 1)
                if j == 0:
                    z_raw(1)

            sc.preload_act_table(ACT.Silu)
            steps.wait()
            sc.activation(z_silu[:, 0:2, :], z_silu[:, 0:2, :], ACT.Silu)
            with act_e.Fori(1, XT // 2) as i:
                for b in range(2):
                    c = i * 2 + (C_Z + b)
                    act_e.wait_ge(s_pe, c + 1)
                    sc.activation(two(z_silu[:, i * 2 + b, :]), pair(b), ACT.Silu)
                    split_hi(b, c + 2, i + (C_Z // 2 + 1))
            act_e.wait_ge(s_smt, 1)
            sc.activation(smt[0:META, 0, :], ps[0:META, 4, 0:P], ACT.Copy)
            sc.activation(smt[:, 1:NT + 1, :], ps[:, 5, :].rearrange("p (a b) -> p a b", b=P), ACT.Copy)\
                .then_inc(s_smt_ready, 1)
            act_e.wait_ge(s_dec, 1)
            sc.activation(dec_b[:, :, :], ps[:, 6, 0:(NT + 1) * SH].rearrange("p (a b) -> p a b", b=SH), ACT.Copy)\
                .then_inc(s_smt_ready, 1)
            def xbc_chunks(i0, i1):
                with act_e.Fori(i0, i1) as i:
                    for b in range(2):
                        c = i * 2 + (C_XBC + b)
                        act_e.wait_ge(s_pe, c + 1)
                        sc.activation(two(xpad[b][:, XPAD:XPAD + TOK]), pair(b), ACT.Copy).then_inc(s_xpad, 1)
                        split_hi(b, c + 2, i + (C_XBC // 2 + 1), SLOT)
                        act_e.wait_ge(s_conv, i * 2 + (b + 1))
                        sc.activation(xbc[:, i * 2 + b, :], conv[b][:, :], ACT.Silu).then_inc(s_xbc, 1)

            xbc_chunks(0, CT // 4)
            xbc_chunks(CT // 4, CT // 4 + 1)
            act_e.wait_ge(s_kper, 1)
            sc.activation(kpe_hi[:, :], kpe_parts[0], ACT.Copy).then_inc(s_kpehi, 1)
            xbc_chunks(CT // 4 + 1, CT // 2)
            sc.preload_act_table_set("natural_log_exp_and_others")

            with act_e.Fori(0, PAIRS) as i:
                def hi(dst, src, n):
                    if n:
                        act_e.wait_ge(s_proj, i * 6 + n)
                    sc.activation(dst, src, ACT.Copy).then_inc(s_phi, 1)

                hi(two(qn_hi[0][:, :]), pair(0), 1)
                hi(two(qn_hi[1][:, :]), pair(1), 2)
                act_e.wait_ge(s_proj, i * 6 + 3)
                sc.activation(two(xn[0][:, 0:TOK]), pair(2), ACT.Copy).then_inc(s_rawcp, 1)
                hi(two(kn_hi[0][:, :]), pair(3), 4)
                hi(two(kn_hi[1][:, :]), pair(0), 6)
                act_e.wait_ge(s_rope, i + 1)
                hi(qpe_hi[:, :], probs[0][:, :], 0)
                act_e.wait_ge(s_val, i * 2 + 1)
                hi(v_parts[:, 0:2, :, 0, :], by_head(ps[:, 4, :]), 0)
                act_e.wait_ge(s_val, i * 2 + 2)
                hi(v_parts[:, 2:4, :, 0, :], by_head(ps[:, 5, :]), 0)
                act_e.wait_ge(s_pe, i * 2 + (C_ATT + 2))
                hi(v_parts[:, 4:5, :, 0, :], by_head(ps[:, 6, 0:2 * DV]), 0)
                for s in range(UNITS + 3):
                    if s in HI_AT:
                        b, part = divmod(HI_AT.index(s), 2)
                        if part == 0:
                            act_e.wait_ge(s_land[b], landed(i + (C_ATT // 2 + 1)))
                            act_e.wait_ge(s_pe, i * 2 + (C_ATT + 1 + b))
                        w = slice(part * SLOT // 2, (part + 1) * SLOT // 2)
                        ins = sc.activation(whi[b][:, w], wf[b][:, w], ACT.Copy)
                        if part:
                            ins.then_inc(s_whi, 1)
                    if 2 <= s < UNITS + 2:
                        u = s - 2
                        t, r = u % (NT + 1), rows(u % (NT + 1))
                        act_e.wait_ge(s_T, i * UNITS + (u + 1))
                        sc.activation(pt_hi[u % 2][:, 0:t + 1, :], turned(2, P)[:, 0:t + 1, :], ACT.Copy)\
                            .then_inc(s_pthi, 1)
                    if s < UNITS:
                        r = rows(s % (NT + 1))
                        act_e.wait_ge(s_max, i * UNITS + (s + 1))
                        sc.activation(prob_view(s), score_view(s), ACT.Exp, scale=SCALE,
                                      bias=stat[0:r, ST_NM + s:ST_NM + s + 1],
                                      accum_out=stat[0:r, ST_DEN + s:ST_DEN + s + 1]).then_inc(s_exp, 1)

            act_e.wait_ge(s_attn, PAIRS * UNITS)
            for s in range(NT + 3):
                if s <= NT:
                    rstd(two(attn[0:rows(s), s, :]), rows(s), ST_ATT + s, att.rstd, 1.0 / D, ps[0:rows(s), 6:8, :])
                if s >= 2:
                    turned_hi(att, s - 2, mixa_hi)

            def stage(q, cols, w):
                sc.activation(xbc_c[:, :, 0:w], xbc[:, :, cols], ACT.Copy).then_inc(s_stage, 1)

            def chunk(q, w, following, before=None):
                first = isinstance(q, int) and q == 0
                if first:
                    act_e.wait_ge(s_seg, 1)
                    sc.activation(decay[0:w, :, 0:w], decay[0:w, :, 0:w], ACT.Exp).then_inc(s_ex, 1)
                act_e.wait_ge(s_xt, q + 1)
                if not first:
                    for s in (s_xdt, s_xdte, s_xskip):
                        act_e.wait_ge(s, q)
                sc.activation(two(xn[0][0:w, :]), ps[0:w, 0:2, :], ACT.Copy)
                sc.activation(b_c[0:w, :], ps[0:w, 2, 0:GROUPS * STATE], ACT.Copy).then_inc(s_xs, 1)
                if not first:
                    for h in range(SH):
                        if h % 4 == 0:
                            act_e.wait_ge(s_ab, spreads(q, h // 4))
                        ins = sc.activation(decay[0:w, h, 0:w], ps[0:w, SPREAD[h // 4], (h % 4) * P:(h % 4) * P + w],
                                            ACT.Exp, bias=minus_acs[0:w, q, h:h + 1])
                        if h % 4 == 3:
                            ins.then_inc(s_ex, 1)
                if following is not None:
                    if not first:
                        act_e.wait_ge(s_off, q)
                    stage(q + 1, following, P)
                if before is not None:
                    squares_of(q, before)

            def squares_of(q, cols):
                act_e.wait_ge(s_gate, q * 2)
                sc.activation(gsq[:, :, cols], gated[:, :, cols], ACT.Square).then_inc(s_gsq, 1)

            act_e.wait_ge(s_xbc, CT)
            stage(0, tcol(0), META)
            chunk(0, META, tcol(1))
            chunk(1, P, tcol(2), tcol(0))
            with act_e.Fori(2, NT) as q:
                chunk(q, P, bass.ds(q * P + META, P), bass.ds(q * P - (2 * P - META), P))
            chunk(NT, P, None, tcol(NT - 1))
            squares_of(NT + 1, tcol(NT))

            for g in range(GROUPS):
                act_e.wait_ge(s_gsum, g + 1)
                steps.add(sc.activation(two(rstd_g[:, g, :]), pair(2 + g), ACT.Ln, scale=1.0 / GC, bias=eps))
                steps.wait()
                sc.activation(rstd_g[:, g, :], rstd_g[:, g, :], ACT.Exp, scale=-0.5).then_inc(s_rg, 1)
                for k in range(g * (XT // GROUPS), (g + 1) * (XT // GROUPS)):
                    act_e.wait_ge(s_ng, k + 1)
                    sc.activation(mixs_hi[:, k, :], normed_g[k % 2][:, :], ACT.Copy).then_inc(s_mshi, 1)
                    if k == XT - 2:
                        split_hi(0, C_OUT + 2, C_OUT // 2 + 1)
            split_hi(1, C_OUT + 3, C_OUT // 2 + 1)

            def out_pair(i, first=False):
                c = i * 4 + C_OUT
                if not first:
                    for b in range(2):
                        split_hi(b, c + 2 + b, i * 2 + (C_OUT // 2 + 1))
                for m in range(2):
                    act_e.wait_ge(s_pe, c + 3 + m)
                    sc.activation(two(mixo[:, i * 2 + m, :]), pair(m), ACT.Copy).then_inc(s_mixo, 1)
                    split_hi(m, c + 4 + m, i * 2 + (C_OUT // 2 + 2))

            out_pair(0, first=True)
            with act_e.Fori(1, KD // 2) as i:
                out_pair(i)
            for s in range(NT + LAG + 2):
                if s <= NT:
                    n = rows(s)
                    act_e.wait_ge(s_t1, s + 1)
                    rstd(ps[0:n, 2 * (s % 2):2 * (s % 2) + 2, :], n, ST_POST + s, s_rpost, 1.0 / D,
                         two(squares_out[0:n, :]))
                if LAG <= s <= NT + LAG:
                    t = s - LAG
                    act_e.wait_ge(s_h, t + 1)
                    rstd(h_tm[0:rows(t), t, :], rows(t), ST_FFN + t, ffn.rstd, 1.0 / D, squares_out[0:rows(t), :])
                if s > LAG:
                    turned_hi(ffn, s - LAG - 1, hn2_hi)

            sc.preload_act_table(ACT.Silu)
            def stage_hi(slot, k, first=False):
                if not first:
                    act_e.wait_ge(s_pe, k + (C_DOWN - 1))
                sc.activation(st_hi[slot][:, :], act[:, k, :], ACT.Copy).then_inc(s_sthi, 1)

            def up_block(j):
                for b, (u, done) in enumerate(((u_gate, s_ug), (u_value, s_uv))):
                    c = j * 2 + (C_UP + b)
                    act_e.wait_ge(s_pe, c + 1)
                    sc.activation(two(u[:, :]), pair(b, NF // 2), ACT.Copy).then_inc(done, 1)
                    split_hi(b, c + 2, j + (C_UP // 2 + 1))
                act_e.wait_ge(s_cg, j + 1)
                sc.activation(c_gate[:, :], c_gate[:, :], ACT.Silu).then_inc(s_silu, 1)

            with act_e.Fori(0, KF - 1) as j:
                up_block(j)
            for k in range(2):
                act_e.wait_ge(s_actr, k + 1)
                stage_hi(k, k, True)
            up_block(KF - 1)
            act_e.wait_ge(s_actr, KF)

            with act_e.Fori(0, KF // 2 - 1) as i:
                for b in range(2):
                    stage_hi(b, i * 2 + (2 + b))
                    split_hi(b, i * 2 + (C_DOWN + 2 + b), i + (C_DOWN // 2 + 1))
            sc.preload_act_table_set("natural_log_exp_and_others")
            for t in range(NT):
                act_e.wait_ge(s_down, t + 1)
                rstd(ps[:, 2 * t:2 * t + 2, :], P, ST_LAST + t, s_rlast, 1.0 / D, two(junk[:, :]))

        @block.vector
        def _(dve):
            ve = nc.vector
            steps = Chain(dve, s_dve)

            def split_lo(slot, chunk, width=KD * P):
                dve.wait_ge(s_whi, chunk + 1)
                whole = slice(0, width)
                if isinstance(chunk, int) and chunk == 5:
                    steps.add(ve.tensor_tensor(wlo[slot][:, whole], wf[slot][:, whole],
                                               whi[slot][:, whole].bitcast(F32), ALU.subtract))
                    dve.wait_ge(s_small, 16 * 4)
                    steps.wait()
                    ve.tensor_tensor(dt_cols(wlo[slot]), dtw[:, :, :], dt_cols(whi[slot]).bitcast(F32),
                                     ALU.subtract).then_inc(s_wlo, 1)
                else:
                    ve.tensor_tensor(wlo[slot][:, whole], wf[slot][:, whole], whi[slot][:, whole].bitcast(F32),
                                     ALU.subtract).then_inc(s_wlo, 1)

            def scale_rows(norm, t, src, col, gain):
                n = rows(t)
                dve.wait_ge(norm.rstd, t + 1)
                if t >= 2:
                    dve.wait_ge(norm.turned, t - 1)
                ve.scalar_tensor_tensor(xn[t % 2][0:n, :], src, stat[0:n, col + 5 + t:col + 6 + t], gain[0:n, :],
                                        ALU.mult, ALU.mult).then_inc(norm.xn, 1)

            def turned_lo(norm, t, dst, upper):
                dve.wait_ge(norm.hi, t + 1)
                w, b = rows(t), norm.pair + t % 2
                ve.tensor_tensor(dst[:, :, tcol(t)], turned(b, w), upper[:, :, tcol(t)].bitcast(F32),
                                 ALU.subtract).then_inc(norm.lo, 1)

            def norm_rows(norm, src, col, gain, upper, lower, between=lambda t: None):
                for t in range(NT + 2):
                    if t <= NT:
                        scale_rows(norm, t, src[0:rows(t), t, :], col, gain)
                    if t:
                        turned_lo(norm, t - 1, lower, upper)
                        between(t - 1)

            def first_chunks(t):
                if t in (2, 3):
                    split_lo(t - 2, t - 2)

            dve.wait_ge(s_gain_pre, 16)
            norm_rows(pre, h_tm, ST_PRE, gain_a, hn_hi, hn_lo, first_chunks)
            for c in range(C_Z):
                split_lo(c % 2, c + 2)

            dve.wait_ge(s_dtr, 1)
            ve.tensor_scalar(xn[1][0:SH, 0:TOK], xn[0][0:SH, 0:TOK], dt_small[:, 0:1], None, ALU.add).then_inc(s_dtx, 1)
            dve.wait_ge(s_dtx, 1)
            ve.tensor_scalar(sm[R_DT:R_DT + SH, :], xn[1][0:SH, 0:TOK], 0.0, None, ALU.max).then_inc(s_dtx, 1)
            dve.wait_ge(s_vec_ready, 2)
            for j in range(KQ + KKV):
                g = int(j >= KQ)
                dve.wait_ge(s_rstdf, g + 1)
                ve.scalar_tensor_tensor(qkvk[:, j, :], qkvk[:, j, :], vec[:, 0, V_QA + j:V_QA + j + 1],
                                        rstd_f[:, g, :], ALU.mult, ALU.mult).then_inc(s_qkvn, 1)
            dve.wait_ge(s_dtl, 1)
            steps.add(ve.tensor_tensor(sm[R_DT:R_DT + SH, :], sm[R_DT:R_DT + SH, :], xn[0][0:SH, 0:TOK], ALU.add))
            dve.wait_ge(s_negA, 1)
            steps.wait()
            steps.add(ve.tensor_scalar(xn[1][0:SH, 0:TOK], sm[R_DT:R_DT + SH, :], dt_small[:, 2:3], -1.0, ALU.mult,
                                       ALU.mult))
            steps.wait()
            for t in range(NT + 1):
                c = tcol(t)
                ve.tensor_tensor_scan(xn[0][0:SH, c], ones[0:SH, 0:rows(t)], xn[1][0:SH, c], 0.0, ALU.mult,
                                      ALU.add).then_inc(s_acs, 1)
            ve.memset(acs3[:, :], 0.0).then_inc(s_acs3_zero, 1)
            dve.wait_ge(s_acs, NT + 1)
            steps.add(ve.tensor_copy(sm[R_ACS:R_ACS + SH, :], xn[0][0:SH, 0:TOK]))
            split_lo(0, C_Z + 2)
            for j in range(KQ + KKV):
                dve.wait_ge(s_qkvhi, j + 1)
                ve.tensor_tensor(qkv_lo[:, j, :], qkvk[:, j, :], qkv_hi[:, j, :].bitcast(F32),
                                 ALU.subtract).then_inc(s_qkvlo, 1)
            dve.wait_ge(s_exps, 1)
            ve.tensor_tensor(sm[R_DTE:R_DTE + SH, :], sm[R_DT:R_DT + SH, :], xn[1][0:SH, 0:TOK],
                             ALU.mult).then_inc(s_sm, 1)
            dve.wait_ge(s_sm, 1)
            steps.add(ve.tensor_copy(dt_ends[:, 0:1], sm[R_EXP:R_EXP + SH, META - 1:META]))
            steps.add(ve.tensor_copy(dt_ends[:, 1:NT + 1], sm[R_EXP:R_EXP + SH, META + P - 1:TOK:P]))
            steps.wait()
            ve.tensor_tensor(ends[:, :, :], bcast(dt_ends[:, :], [SH, NT + 1, SH]),
                             ident[0:SH, 0:SH].unsqueeze(1).broadcast_to([SH, NT + 1, SH]),
                             ALU.mult).then_inc(s_ends, 1)
            for j in range(2):
                dve.wait_ge(s_acs_copied, j + 1)
                ve.tensor_tensor(acs_rest[j + 1], acs_rest[j] if j else xn[0][0:SH, 0:TOK],
                                 acs3[32 * j:32 * j + SH, :], ALU.subtract).then_inc(s_acs3, 1)
                if j == 0:
                    split_lo(1, C_Z + 3)

            with dve.Fori(1, XT // 2) as i:
                for b in range(2):
                    split_lo(b, i * 2 + (C_Z + 2 + b))

            dve.wait_ge(s_smt_ready, 1)
            ve.tensor_scalar(minus_acs[0:META, 0, :], smt[0:META, 0, R_ACS:R_ACS + SH], -1.0, None, ALU.mult)
            ve.tensor_scalar(minus_acs[:, 1:NT + 1, :], smt[:, 1:NT + 1, R_ACS:R_ACS + SH], -1.0, None, ALU.mult)\
                .then_inc(s_smtc, 1)
            def xbc_chunks(i0, i1):
                with dve.Fori(i0, i1) as i, steps.loop(i - i0, i1 - i0, 2 * (TAPS - 1)):
                    for b in range(2):
                        t = i * 2 + b
                        dve.wait_ge(s_xpad, t + 1)

                        def tap(w):
                            return vec[:, 0, bass.ds(t + (V_CW + w * CT), 1)]

                        steps.add(ve.tensor_scalar(conv[b][:, :], xpad[b][:, XPAD:XPAD + TOK], tap(XPAD),
                                                   vec[:, 0, bass.ds(t + V_CB, 1)], ALU.mult, ALU.add))
                        for w in range(XPAD):
                            steps.wait()
                            ins = ve.scalar_tensor_tensor(conv[b][:, :], xpad[b][:, w:w + TOK], tap(w),
                                                          conv[b][:, :], ALU.mult, ALU.add)
                            if w < XPAD - 1:
                                steps.add(ins)
                            else:
                                ins.then_inc(s_conv, 1)
                        split_lo(b, t + (C_XBC + 2), SLOT)

            xbc_chunks(0, CT // 4)
            dve.wait_ge(s_kpe, 1)
            dve.wait_ge(s_rope_tab, 32)
            steps.add(ve.tensor_tensor(two(kpe_parts[0]), pair(2), two(cos_t[:, :]), ALU.mult))
            steps.add(ve.tensor_tensor(two(kpe_parts[1]), pair(3), two(sin_t[:, :]), ALU.mult))
            steps.wait()
            ve.tensor_tensor(kpe_parts[0], kpe_parts[0], kpe_parts[1], ALU.add).then_inc(s_kper, 1)
            xbc_chunks(CT // 4, CT // 4 + 1)
            dve.wait_ge(s_kpehi, 1)
            ve.tensor_tensor(kpe_lo[:, :], kpe_parts[0], kpe_hi[:, :].bitcast(F32), ALU.subtract).then_inc(s_kpelo, 1)
            xbc_chunks(CT // 4 + 1, CT // 2)

            with dve.Fori(0, PAIRS) as i, steps.loop(i, PAIRS, 1 + 3 * UNITS):
                def lo(dst, src, upper, n):
                    dve.wait_ge(s_phi, i * 8 + n)
                    ve.tensor_tensor(dst, src, upper.bitcast(F32), ALU.subtract).then_inc(s_plo, 1)

                lo(two(qn_lo[0][:, :]), pair(0), two(qn_hi[0][:, :]), 1)
                lo(two(qn_lo[1][:, :]), pair(1), two(qn_hi[1][:, :]), 2)
                lo(two(kn_lo[0][:, :]), pair(3), two(kn_hi[0][:, :]), 3)
                dve.wait_ge(s_proj, i * 6 + 5)
                steps.add(ve.tensor_tensor(two(probs[1][:, :]), pair(2), two(sin_t[:, :]), ALU.mult))
                dve.wait_ge(s_cos, i + 1)
                steps.wait()
                ve.tensor_tensor(probs[0][:, :], probs[0][:, :], probs[1][:, :], ALU.add).then_inc(s_rope, 1)
                lo(two(kn_lo[1][:, :]), pair(0), two(kn_hi[1][:, :]), 4)
                lo(qpe_lo[:, :], probs[0][:, :], qpe_hi[:, :], 5)
                for n, (t0, t1, b) in enumerate(((0, 2, 4), (2, 4, 5), (4, 5, 6))):
                    lo(v_parts[:, t0:t1, :, 1, :], by_head(ps[:, b, 0:(t1 - t0) * 2 * DV]), v_parts[:, t0:t1, :, 0, :],
                       6 + n)
                for s in range(UNITS + 3):
                    if s < UNITS:
                        r = rows(s % (NT + 1))
                        v = score_view(s)
                        dve.wait_ge(s_S, i * UNITS + (s + 1))
                        m = stat[0:r, ST_NM + s:ST_NM + s + 1]
                        steps.add(ve.tensor_reduce(m, v, AX.XY if len(v.shape) == 3 else AX.X, ALU.max))
                        steps.wait()
                        ve.tensor_scalar(m, m, -SCALE, None, ALU.mult).then_inc(s_max, 1)
                    if 2 <= s < UNITS + 2:
                        u = s - 2
                        t, r = u % (NT + 1), rows(u % (NT + 1))
                        dve.wait_ge(s_pthi, i * UNITS + (u + 1))
                        ve.tensor_tensor(pt_lo[u % 2][:, 0:t + 1, :], turned(2, P)[:, 0:t + 1, :],
                                         pt_hi[u % 2][:, 0:t + 1, :].bitcast(F32), ALU.subtract).then_inc(s_ptlo, 1)
                    if s >= 3:
                        u = s - 3
                        t, r = u % (NT + 1), rows(u % (NT + 1))
                        rd = stat[0:r, ST_RDEN + u:ST_RDEN + u + 1]
                        dve.wait_ge(s_exp, i * UNITS + (u + 1))
                        steps.add(ve.reciprocal(rd, stat[0:r, ST_DEN + u:ST_DEN + u + 1]))
                        steps.wait()
                        dve.wait_ge(s_pv, i * UNITS + (u + 1))
                        dst = attn[0:r, t, bass.ds(i * (2 * DV) + (u // (NT + 1)) * DV, DV)]
                        steps.add(ve.tensor_scalar(dst, ps[0:r, 6 + u % 2, DV:2 * DV], rd, None, ALU.mult))
                        steps.wait()
                        ve.scalar_tensor_tensor(dst, ps[0:r, 6 + u % 2, 0:DV], rd, dst, ALU.mult, ALU.add).then_inc(s_attn, 1)

            dve.wait_ge(s_gain_att, 16)
            norm_rows(att, attn, ST_ATT, gain_a, mixa_hi, mixa_lo)

            def heads(ap):
                return ap.rearrange("p (h e) -> p h e", e=SP)

            def both(ap):
                return ap.rearrange("p a (h e) -> p (a h) e", e=SP)

            def chunk(q, cols, w):
                first = isinstance(q, int)
                if first:
                    dve.wait_ge(s_ab, 1)
                    dve.wait_ge(s_smtc, 1)
                    ve.tensor_tensor(decay[0:w, :, 0:w], ps[0:w, SPREAD[0], 0:SH * w].rearrange("p (h l) -> p h l", l=w),
                                     bcast(minus_acs[0:w, 0, :], [w, SH, w]), ALU.add).then_inc(s_seg, 1)
                dve.wait_ge(s_xs, q + 1)
                for j in range(4):
                    dve.wait_ge(s_ex, 1 if first else spreads(q, j))
                    d = decay[0:w, 4 * j:4 * j + 4, 0:w]
                    g = 4 * j // HG
                    cb = ps[0:w, 2, (GROUPS + g) * P:(GROUPS + g) * P + w]
                    ins = ve.tensor_tensor(d, d, cb.unsqueeze(1).broadcast_to([w, 4, w]), ALU.mult)
                ins.then_inc(s_M, 1)
                ve.tensor_tensor(heads(xdt[0:w, :]), heads(xn[0][0:w, :]),
                                 bcast(smt[0:w, q, R_DT:R_DT + SH], [w, SH, SP]), ALU.mult).then_inc(s_xdt, 1)
                if first:
                    dve.wait_ge(s_st, q + 1)
                    ve.tensor_copy(two(state[:, :]), ps[:, 6:8, :]).then_inc(s_state, 1)
                    dve.wait_ge(s_yd, q + 1)
                    dve.wait_ge(s_xskip, q + 1)
                    ve.tensor_tensor(two(y_tm[0:w, :]), ps[0:w, 4:6, :], two(xn[1][0:w, :]), ALU.add).then_inc(s_y, 1)
                else:
                    dve.wait_ge(s_off, q)
                    ve.tensor_tensor(heads(y_tm[:, :]), both(ps[:, 0:2, :]),
                                     bcast(smt[:, q, R_EXP:R_EXP + SH], [P, SH, SP]), ALU.mult).then_inc(s_yoff, 1)
                    dve.wait_ge(s_st, q + 1)
                    dve.wait_ge(s_sdec, q)
                    ve.tensor_tensor(two(state[:, :]), ps[:, 6:8, :], two(state[:, :]), ALU.add).then_inc(s_state, 1)
                    dve.wait_ge(s_yd, q + 1)
                    dve.wait_ge(s_yadd, q)
                    ve.tensor_tensor(two(y_tm[:, :]), ps[:, 4:6, :], two(y_tm[:, :]), ALU.add).then_inc(s_y, 1)
                for half in range(2):
                    dve.wait_ge(s_yt, q * 2 + (half + 1))
                    blocks = slice(half * (XT // 2), (half + 1) * (XT // 2))
                    ve.tensor_tensor(gated[:, blocks, cols], quarter(3, w), z_silu[:, blocks, cols],
                                     ALU.mult).then_inc(s_gate, 1)

            chunk(0, slice(0, META), META)
            with dve.Fori(1, NT + 1) as q:
                chunk(q, bass.ds(q * P - (P - META), P), P)

            for k in range(XT + 1):
                if k < XT:
                    dve.wait_ge(s_rg, k // (XT // GROUPS) + 1)
                    if k >= 2:
                        dve.wait_ge(s_mslo, k - 1)
                    ve.scalar_tensor_tensor(normed_g[k % 2][:, :], gated[:, k, :], vec[:, 0, V_SN + k:V_SN + k + 1],
                                            rstd_g[:, k // (XT // GROUPS), :], ALU.mult, ALU.mult).then_inc(s_ng, 1)
                if k:
                    dve.wait_ge(s_mshi, k)
                    ve.tensor_tensor(mixs_lo[:, k - 1, :], normed_g[(k - 1) % 2][:, :],
                                     mixs_hi[:, k - 1, :].bitcast(F32), ALU.subtract).then_inc(s_mslo, 1)
                if k == XT - 1:
                    split_lo(0, C_OUT + 2)

            split_lo(1, C_OUT + 3)
            for b in range(2):
                split_lo(b, C_OUT + 4 + b)
            with dve.Fori(1, KD // 2) as i:
                for m in range(2):
                    for b in range(2):
                        split_lo(b, i * 4 + (C_OUT + 2 * m + 2 + b))
            dve.wait_ge(s_gain_post, 16)
            dve.wait_ge(s_gain_ffn, 16)
            for s in range(NT + LAG + 2):
                if s <= NT:
                    n = rows(s)
                    dve.wait_ge(s_rpost, s + 1)
                    if s >= 2:
                        dve.wait_ge(s_h, s - 1)
                    ve.scalar_tensor_tensor(two(post[s % 2][0:n, :]), ps[0:n, 2 * (s % 2):2 * (s % 2) + 2, :],
                                            stat[0:n, ST_POST + 5 + s:ST_POST + 6 + s], two(gain_a[0:n, :]),
                                            ALU.mult, ALU.mult).then_inc(s_u, 1)
                if LAG <= s <= NT + LAG:
                    scale_rows(ffn, s - LAG, h_tm[0:rows(s - LAG), s - LAG, :], ST_FFN, gain_b)
                if s > LAG:
                    turned_lo(ffn, s - LAG - 1, hn2_lo, hn2_hi)

            def up_block(j):
                for b, (u, cv, ready, done) in enumerate(((u_gate, c_gate, s_ug, s_cg), (u_value, c_value, s_uv, s_cv))):
                    dve.wait_ge(ready, j + 1)
                    steps.add(ve.tensor_scalar(cv[:, :], u[:, NF - SEQ:NF],
                                               vec[:, 2, one(j + b * KF)],
                                               vec[:, 2, one(j + (CF + b * KF))], ALU.mult, ALU.add))
                    for w in range(FTAPS - 1):
                        o = NF - SEQ - (FTAPS - 1) + w
                        steps.wait()
                        ins = ve.scalar_tensor_tensor(cv[:, :], u[:, o:o + SEQ],
                                                      vec[:, 1, one(j + (w * CF + b * KF))], cv[:, :],
                                                      ALU.mult, ALU.add)
                        if w < FTAPS - 2:
                            steps.add(ins)
                        else:
                            ins.then_inc(done, 1)
                    split_lo(b, j * 2 + (C_UP + 2 + b))
                dve.wait_ge(s_silu, j + 1)
                dve.wait_ge(s_cv, j + 1)
                ve.tensor_tensor(act[:, j, :], c_gate[:, :], c_value[:, :], ALU.mult).then_inc(s_actr, 1)
                dve.wait_ge(s_actr, j + 1)

            def stage_lo(slot, k):
                dve.wait_ge(s_sthi, k + 1)
                ve.tensor_tensor(st_lo[slot][:, :], act[:, k, :], st_hi[slot][:, :].bitcast(F32),
                                 ALU.subtract).then_inc(s_stlo, 1)

            with dve.Fori(0, KF - 1) as j, steps.loop(j, KF - 1, 2 * (FTAPS - 1)):
                up_block(j)
            for k in range(2):
                stage_lo(k, k)
            up_block(KF - 1)
            with dve.Fori(0, KF // 2 - 1) as i:
                for b in range(2):
                    stage_lo(b, i * 2 + (2 + b))
                    split_lo(b, i * 2 + (C_DOWN + 2 + b))
            dve.wait_ge(s_gain_last, 16)
            for t in range(NT):
                dve.wait_ge(s_rlast, t + 1)
                for n, cols in enumerate(OUT_COLS[t]):
                    y, w = y_out[t][:, cols], cols.stop - cols.start
                    b = 2 * t + cols.start // BANK
                    src = ps[:, b:b + w // BANK, :]
                    ve.scalar_tensor_tensor(y.rearrange("p (a b) -> p a b", b=BANK), src,
                                            stat[:, ST_LAST + 5 + t:ST_LAST + 6 + t],
                                            gain_a[:, cols].rearrange("p (a b) -> p a b", b=BANK),
                                            ALU.mult, ALU.mult).then_inc(s_ylast, 1)
                    dve.wait_ge(s_ylast, t + n + 1)
                    ve.tensor_tensor(y, y, h_tm[:, t + 1, cols], ALU.add).then_inc(s_yout, 1)

        @block.tensor
        def _(pe):
            mm = nc.tensor.matmul

            def three(out_ap, w_hi, w_lo, x_hi, x_lo, first, last):
                mm(out_ap, w_hi, x_hi, start=first, stop=False)
                mm(out_ap, w_hi, x_lo, start=False, stop=False)
                return mm(out_ap, w_lo, x_hi, start=False, stop=last)

            def chunk(slot, b, x_hi, x_lo, halves, first=True, last=True, only=(0, 1)):
                for h in only:
                    cols = halves[h]
                    w = cols.stop - cols.start
                    for k in range(KD):
                        ins = three(ps[:, 2 * b + h, 0:w], whi[slot][:, k * P:(k + 1) * P],
                                    wlo[slot][:, k * P:(k + 1) * P], x_hi[:, k, cols], x_lo[:, k, cols],
                                    first and k == 0, last and k == KD - 1)
                return ins

            def turn_rows(norm, t):
                w, b = rows(t), t % 2
                pe.wait_ge(norm.xn, t + 1)
                if t >= 2:
                    pe.wait_ge(norm.lo, t - 1)
                for k in range(KD):
                    ins = nc.tensor.transpose(turned(norm.pair + b, w)[:, k, :], xn[b][0:w, k * P:(k + 1) * P], ident[0:w, 0:w])
                ins.then_inc(norm.turned, 1)

            pe.wait_ge(s_const, 2)
            def first_halves(norm, c, b, x_hi, x_lo, halves):
                pe.wait_ge(norm.lo, 3)
                pe.wait_ge(s_wlo, c + b + 1)
                chunk(b, b, x_hi, x_lo, halves, only=(0,))

            for t in range(NT + 1):
                turn_rows(pre, t)
                if t == NT - 1:
                    first_halves(pre, 0, 0, hn_hi, hn_lo, WH)
            first_halves(pre, 0, 1, hn_hi, hn_lo, WH)
            pe.wait_ge(pre.lo, NT + 1)
            for c in range(2):
                chunk(c, c, hn_hi, hn_lo, WH, only=(1,)).then_inc(s_pe, 1)
            pe.wait_ge(s_vec, 16 * 12)
            for k, n in enumerate((NV0, 2 * CF, 2 * CF)):
                ins = nc.tensor.transpose(ps[:, 4, k * 96:k * 96 + n], vec_rows[0:n, k, :], ident[0:n, 0:n])
            ins.then_inc(s_vt, 1)
            for c in range(2, C_Z):
                pe.wait_ge(s_wlo, c + 1)
                chunk(c % 2, c % 2, hn_hi, hn_lo, WH).then_inc(s_pe, 1)
            for g, (j0, j1) in enumerate(((0, KQ), (KQ, KQ + KKV))):
                pe.wait_ge(s_sq, j1)
                for h, cols in enumerate(WH):
                    for j in range(j0, j1):
                        ins = mm(ps[:, 4 + 2 * g + h, 0:HALF], ones[:, :], squares[:, j, cols], start=j == j0,
                                 stop=j == j1 - 1)
                ins.then_inc(s_sumsq, 1)
            def in_chunks(c0, c1):
                with pe.Fori(c0 // 2, c1 // 2) as i:
                    for b in range(2):
                        pe.wait_ge(s_wlo, i * 2 + (b + 1))
                        chunk(b, b, hn_hi, hn_lo, WH).then_inc(s_pe, 1)

            in_chunks(C_Z, C_XBC)
            pe.wait_ge(s_sm, 1)
            nc.tensor.transpose(ps[0:META, 4, 0:P], sm[:, tcol(0)], ident[:, :])
            for t in range(1, NT + 1):
                ins = nc.tensor.transpose(ps[:, 5, (t - 1) * P:t * P], sm[:, tcol(t)], ident[:, :])
            ins.then_inc(s_smt, 1)
            pe.wait_ge(s_ends, 1)
            mm(ps[:, 6, 0:(NT + 1) * SH], ones[0:SH, :], ends[:, :, :].rearrange("p a b -> p (a b)"), start=True,
               stop=True).then_inc(s_dec, 1)
            in_chunks(C_XBC, C_XBC + CT // 2)
            pe.wait_ge(s_rstdf, 2)
            pe.wait_ge(s_evac, C_Z)
            pe.wait_ge(s_smt_ready, 2)
            for b, m in enumerate((dup, dupswap)):
                for h, cols in enumerate(WH):
                    ins = mm(ps[:, 4 + 2 * b + h, 0:HALF], m[:, :], qkvk[0:ROPE, C_Z - 1, cols], start=True, stop=True)
            ins.then_inc(s_kpe, 1)
            in_chunks(C_XBC + CT // 2, C_ATT)

            pe.wait_ge(s_qkvlo, KQ + KKV)
            with pe.Fori(0, PAIRS) as i:
                def project(b, slot, col, K, j0, step=P):
                    for h, cols in enumerate(WH):
                        for k in range(K):
                            w = slice(col + k * step, col + k * step + P)
                            ins = three(ps[:, 2 * b + h, 0:HALF], whi[slot][:, w], wlo[slot][:, w],
                                        qkv_hi[:, j0 + k, cols], qkv_lo[:, j0 + k, cols], k == 0, k == K - 1)
                    return ins

                def values(t, dst):
                    cols = slice(0, P) if t == 0 else tcol(t)
                    for k in range(KKV):
                        w = slice(2 * KKV * P + k * 2 * DV, 2 * KKV * P + (k + 1) * 2 * DV)
                        ins = three(dst, qkv_hi[:, KQ + k, cols], qkv_lo[:, KQ + k, cols], whi[1][:, w], wlo[1][:, w],
                                    k == 0, k == KKV - 1)
                    return ins

                pe.wait_ge(s_wlo, i * 2 + (C_ATT + 1))
                project(0, 0, 0, KQ, 0).then_inc(s_proj, 1)
                pe.wait_ge(s_xpad, CT)
                project(1, 0, KQ * P, KQ, 0).then_inc(s_proj, 1)
                pe.wait_ge(s_kper, 1)
                project(2, 0, 2 * KQ * P, KQ, 0).then_inc(s_proj, 1)
                pe.wait_ge(s_wlo, i * 2 + (C_ATT + 2))
                pe.wait_ge(s_plo, i * 8 + 1)
                project(3, 1, 0, KKV, KQ).then_inc(s_proj, 1)
                pe.wait_ge(s_rawcp, i + 1)
                mm(ps[:, 4, 0:HALF], swap[:, :], xn[0][:, WH[0]], start=True, stop=True).then_inc(s_pe, 1)
                mm(ps[:, 5, 0:HALF], swap[:, :], xn[0][:, WH[1]], start=True, stop=True).then_inc(s_proj, 1)
                project(0, 1, KKV * P, KKV, KQ).then_inc(s_proj, 1)
                pe.wait_ge(s_rope, i + 1)
                values(0, ps[:, 4, 0:2 * DV])
                values(1, ps[:, 4, 2 * DV:4 * DV]).then_inc(s_val, 1)
                values(2, ps[:, 5, 0:2 * DV])
                values(3, ps[:, 5, 2 * DV:4 * DV]).then_inc(s_val, 1)
                pe.wait_ge(s_plo, i * 8 + 3)
                values(4, ps[:, 6, 0:2 * DV]).then_inc(s_pe, 1)

                def scores(u):
                    hh, t = divmod(u, NT + 1)
                    n, b = score_cols(u), 2 * (u % 2)
                    qc = slice(0, P) if t == 0 else tcol(t)
                    pr = slice(hh * ROPE, (hh + 1) * ROPE)
                    parts = [(ps[:, b, 0:n], 0, n)] if n <= BANK else \
                        [(ps[:, b + h, 0:HALF], h * HALF, (h + 1) * HALF) for h in range(2)]
                    for dst, c0, c1 in parts:
                        ks = slice(c0, c1)
                        three(dst, qn_hi[hh][:, qc], qn_lo[hh][:, qc], kn_hi[hh][:, ks], kn_lo[hh][:, ks], True, False)
                        masked = c1 == n
                        ins = three(dst, qpe_hi[pr, qc], qpe_lo[pr, qc], kpe_hi[pr, ks], kpe_lo[pr, ks], False,
                                    not masked)
                    d = META if t == 0 else P
                    last = parts[-1]
                    w = last[2] - last[1]
                    return mm(ps[:, b + len(parts) - 1, w - d:w], ident_bf[:, :], mask_bf[:, 0:d], start=False, stop=True)

                for s in range(UNITS + 3):
                    if s < UNITS:
                        if s == 0:
                            pe.wait_ge(s_kpelo, 1)
                            pe.wait_ge(s_plo, i * 8 + 5)
                        elif s >= 2:
                            pe.wait_ge(s_exp, i * UNITS + (s - 1))
                        scores(s).then_inc(s_S, 1)
                    if 2 <= s < UNITS + 2:
                        u = s - 2
                        t = u % (NT + 1)
                        pe.wait_ge(s_exp, i * UNITS + (u + 1))
                        if s == 2:
                            pe.wait_ge(s_plo, i * 8 + 8)
                        else:
                            pe.wait_ge(s_ptlo, i * UNITS + u)
                        p = probs[u % 2]
                        ins = nc.tensor.transpose(ps[0:META, 4, 0:P], p[:, 0:META], ident[:, :])
                        for j in range(t):
                            ins = nc.tensor.transpose(turned(2, P)[:, 1 + j, :],
                                                      p[:, META + j * P:META + (j + 1) * P], ident[:, :])
                        ins.then_inc(s_T, 1)
                    if s >= 3:
                        u = s - 3
                        hh, t = divmod(u, NT + 1)
                        pe.wait_ge(s_ptlo, i * UNITS + (u + 1))
                        if u >= 2:
                            pe.wait_ge(s_attn, i * UNITS + (u - 1))
                        o = ps[:, 6 + u % 2, 0:2 * DV]
                        for j in range(t + 1):
                            kr = slice(0, META if j == 0 else P)
                            v = v_parts[kr, j, hh, :, :].rearrange("p a d -> p (a d)")
                            mm(o, pt_hi[u % 2][kr, j, :], v, start=j == 0, stop=False)
                            ins = mm(o, pt_lo[u % 2][kr, j, :], v, start=False, stop=j == t)
                        ins.then_inc(s_pv, 1)

            for t in range(NT + 1):
                turn_rows(att, t)

            pe.wait_ge(att.lo, NT + 1)
            pe.wait_ge(s_smt_ready, 2)
            pe.wait_ge(s_acs_copied, 3)

            def turn_chunk(q, w):
                pe.wait_ge(s_stage, q + 1)
                for k in range(XT):
                    nc.tensor.transpose(ps[0:w, k // 4, (k % 4) * P:(k % 4 + 1) * P], xbc_c[:, k, 0:w], ident[:, :])
                for g in range(GROUPS):
                    nc.tensor.transpose(ps[0:w, 2, g * P:(g + 1) * P], xbc_c[:, XT + g, 0:w], ident[:, :])
                for g in range(GROUPS):
                    ins = mm(ps[0:w, 2, (GROUPS + g) * P:(GROUPS + g) * P + w], xbc_c[:, XT + g, 0:w],
                             xbc_c[:, XT + GROUPS + g, 0:w], start=True, stop=True)
                ins.then_inc(s_xt, 1)

            def spread(js, cols, w):
                for j in js:
                    block4 = quarter(SPREAD[j], w)[0:w]
                    mm(block4, mask_bf[0:w, 0:w], ident_bf[0:w, 0:w].unsqueeze(1).broadcast_to([w, 4, w]), start=True,
                       stop=False)
                    for h in range(4 * j, 4 * j + 4):
                        ins = mm(ps[0:w, SPREAD[j], (h % 4) * P:(h % 4) * P + w],
                                 pick[:, h:h + 1].broadcast_to([PARTS3, w]), acs3[0:PARTS3, cols], start=False,
                                 stop=h % 4 == 3)
                    ins.then_inc(s_ab, 1)

            def ssm_chunk(q, w, following=None):
                first = isinstance(q, int) and q == 0
                pe.wait_ge(s_xs, q + 1)
                if not first:
                    for g in range(GROUPS):
                        ins = mm(ps[:, g, :], xbc_c[:, XT + GROUPS + g, :], state[:, g * GC:(g + 1) * GC],
                                 start=True, stop=True)
                    ins.then_inc(s_off, 1)
                pe.wait_ge(s_ex, 1 if first else spreads(q, 3))
                pe.wait_ge(s_xdte, q + 1)
                for g in range(GROUPS):
                    ins = mm(ps[:, 6 + g, :], b_c[0:w, g * STATE:(g + 1) * STATE], xdte[0:w, g * GC:(g + 1) * GC],
                             start=True, stop=True)
                ins.then_inc(s_st, 1)
                pe.wait_ge(s_M, q + 1)
                pe.wait_ge(s_xdt, q + 1)
                for h in range(SH):
                    ins = mm(ps[0:w, 4 + h // HG, (h % HG) * SP:(h % HG + 1) * SP], decay[0:w, h, 0:w],
                             xdt[0:w, h * SP:(h + 1) * SP], start=True, stop=True)
                ins.then_inc(s_yd, 1)
                if following is not None:
                    if not first:
                        pe.wait_ge(s_yoff, q)
                    turn_chunk(q + 1, P)
                    pe.wait_ge(s_state, q + 1)
                    spread((0, 1), following, P)
                pe.wait_ge(s_y, q + 1)
                for half in range(2):
                    if half:
                        if following is not None:
                            spread((2, 3), following, P)
                        pe.wait_ge(s_gate, q * 2 + 1)
                    elif not first:
                        pe.wait_ge(s_gate, q * 2)
                    for k in range(XT // 2):
                        c = half * (XT // 2) + k
                        ins = nc.tensor.transpose(quarter(3, w)[:, k, :], y_tm[0:w, c * P:(c + 1) * P],
                                                  ident[0:w, 0:w])
                    ins.then_inc(s_yt, 1)

            def spread_meta(w):
                dst = ps[0:w, SPREAD[0], 0:SH * w].rearrange("p (h l) -> p h l", l=w)
                mm(dst, mask_bf[0:w, 0:w], ident_bf[0:w, 0:w].unsqueeze(1).broadcast_to([w, SH, w]), start=True,
                   stop=False)
                for h in range(SH):
                    ins = mm(dst[:, h, :], pick[:, h:h + 1].broadcast_to([PARTS3, w]), acs3[0:PARTS3, tcol(0)],
                             start=False, stop=h == SH - 1)
                ins.then_inc(s_ab, 1)

            spread_meta(META)
            turn_chunk(0, META)
            ssm_chunk(0, META, tcol(1))
            with pe.Fori(1, NT) as q:
                ssm_chunk(q, P, bass.ds(q * P + META, P))
            ssm_chunk(NT, P)
            KG = XT // GROUPS

            def out_half(i, half):
                x = (mixs_hi, mixs_lo) if half else (mixa_hi, mixa_lo)
                for b in range(2):
                    pe.wait_ge(s_wlo, i * 4 + (C_OUT + 2 * half + b + 1))
                    chunk(b, b, x[0], x[1], WH, first=half == 0, last=half == 1).then_inc(s_pe, 1)

            pe.wait_ge(s_gate, 2 * (NT + 1))
            for g in range(GROUPS):
                pe.wait_ge(s_gsq, NT + 1)
                for h, cols in enumerate(WH):
                    for k in range(KG):
                        ins = mm(ps[:, 4 + 2 * g + h, 0:HALF], ones[:, :], gsq[:, KG * g + k, cols], start=k == 0,
                                 stop=k == KG - 1)
                ins.then_inc(s_gsum, 1)
            out_half(0, 0)
            pe.wait_ge(s_mslo, KD)
            out_half(0, 1)
            with pe.Fori(1, KD // 2) as i:
                for half in range(2):
                    out_half(i, half)
            for s in range(NT + LAG + 2):
                if s <= NT:
                    w, b = rows(s), s % 2
                    if s == 0:
                        pe.wait_ge(s_mixo, KD)
                    if s >= 2:
                        pe.wait_ge(s_u, s - 1)
                    for k in range(KD):
                        ins = nc.tensor.transpose(ps[0:w, 2 * b + k // 4, (k % 4) * P:(k % 4 + 1) * P],
                                                  mixo[:, k, tcol(s)], ident[:, :])
                    ins.then_inc(s_t1, 1)
                if s > LAG:
                    turn_rows(ffn, s - LAG - 1)
                if s >= NT + LAG:
                    pe.wait_ge(s_u, NT + 1)
                    first_halves(ffn, C_UP, s - NT - LAG, hn2_hi, hn2_lo, FH)
            pe.wait_ge(ffn.lo, NT + 1)
            for b in range(2):
                chunk(b, b, hn2_hi, hn2_lo, FH, only=(1,)).then_inc(s_pe, 1)
            with pe.Fori(1, KF) as j:
                for b in range(2):
                    pe.wait_ge(s_wlo, j * 2 + (C_UP + 1 + b))
                    chunk(b, b, hn2_hi, hn2_lo, FH).then_inc(s_pe, 1)

            def down_tile(slot, t, first=False, last=False):
                for n in range(2):
                    w = slice(n * BANK, (n + 1) * BANK)
                    tk = slice(t * P, (t + 1) * P)
                    ins = three(ps[:, 2 * t + n, :], st_hi[slot][:, tk], st_lo[slot][:, tk], whi[slot][:, w],
                                wlo[slot][:, w], first, last)
                return ins

            def down(slot, k, first=False):
                pe.wait_ge(s_wlo, k + (C_DOWN + 1))
                pe.wait_ge(s_stlo, k + 1)
                for t in (2, 3, 0, 1):
                    if first and t < 2:
                        pe.wait_ge((s_ug, s_uv)[t], KF)
                    ins = down_tile(slot, t, first)
                ins.then_inc(s_pe, 1)

            down(0, 0, first=True)
            down(1, 1)
            with pe.Fori(1, KF // 2 - 1) as i:
                for b in range(2):
                    down(b, i * 2 + b)
            pe.wait_ge(s_wlo, C_END - 1)
            pe.wait_ge(s_stlo, KF - 1)
            for t in range(3):
                down_tile(0, t)
            pe.wait_ge(s_wlo, C_END)
            pe.wait_ge(s_stlo, KF)
            for t in range(NT):
                if t == 2:
                    down_tile(0, 3)
                down_tile(1, t, last=True).then_inc(s_down, 1)


_INS = ['x', 'meta_tokens', 'norm_mix_pre', 'norm_mix_post', 'norm_ffn_pre', 'norm_ffn_post', 'w_in', 'q_a_norm',
        'w_uq', 'kv_a_norm', 'w_ukv', 'attn_out_norm', 'ssm_conv_w', 'ssm_conv_b', 'ssm_dt_bias', 'ssm_A_log',
        'ssm_D', 'ssm_norm', 'w_out', 'w_up', 'ffn_conv_w', 'ffn_conv_b', 'w_down']


def rope_rows(tokens, dim=64, theta=10000.0):
    import numpy as np

    f = np.float32
    inv = (f(theta) ** (-np.arange(0, dim, 2, dtype=f) / f(dim))).astype(f)
    ang = inv[:, None] * np.arange(tokens, dtype=f)[None, :]
    cos, sin = np.cos(ang).astype(f), np.sin(ang).astype(f)
    return np.ascontiguousarray(np.concatenate([cos] * 4)), np.ascontiguousarray(np.concatenate([-sin, sin] * 2))


def kernel(**inputs):
    import numpy as _np
    import concourse.bacc as _bacc
    from concourse import mybir as _mybir
    from concourse.bass_utils import run_bass_kernel_spmd as _run

    nc = _bacc.Bacc("TRN2", target_bir_lowering=False, num_devices=1)
    arrays, args = {}, []
    for name in _INS:
        a = _np.ascontiguousarray(inputs[name])
        arrays[f"in_{name}_dram"] = a
        args.append(nc.dram_tensor(f"in_{name}_dram", a.shape, _mybir.dt.from_np(a.dtype), kind="ExternalInput").ap())
    seq = inputs["x"].shape[1] + inputs["meta_tokens"].shape[0]
    for name, a in zip(("rope_cos", "rope_sin"), rope_rows(seq)):
        arrays[f"const_{name}"] = a
        args.append(nc.dram_tensor(f"const_{name}", a.shape, _mybir.dt.from_np(a.dtype), kind="ExternalInput").ap())
    out = nc.dram_tensor("out_0_dram", inputs["x"].shape, _mybir.dt.float32, kind="ExternalOutput").ap()
    hymba_layer(nc, *args, out)
    r = _run(nc, [arrays], core_ids=[0])
    return r.results[0]["out_0_dram"]
```
